# Optimizing a Trainium2 kernel written in Bass

```python
import jax, jax.numpy as jnp
from jax import lax
import numpy as np

D_MODEL = 1024
BATCH = 1
SEQ = 256
DEPTH = 2

GRID_W = 64
CTX_LEN = 256
N_MIXERS = 2
N_A_LAYERS = (DEPTH + N_MIXERS - 1) // N_MIXERS
N_B_LAYERS = DEPTH // N_MIXERS
DN_ALPHA = (2.0 * DEPTH) ** 0.25
DN_BETA = (8.0 * DEPTH) ** -0.25
LN_EPS = 1e-5
CHUNK = 128
ROWS_PER_CHUNK = CHUNK // GRID_W
A_WIDTH = D_MODEL
A_HEADS = 8
A_GROUP = A_WIDTH // A_HEADS
GLA_HEADS = 4
GLA_DK = D_MODEL // 2 // GLA_HEADS
GLA_DV = D_MODEL // GLA_HEADS
GLA_QK = GLA_HEADS * GLA_DK
GLA_V = GLA_HEADS * GLA_DV
GLA_GATE_RANK = 16
GLA_TAU = 16.0
GLA_CHUNK = 64
GLA_IN = 2 * GLA_QK + 2 * GLA_V + 2 * GLA_GATE_RANK
PEER_HEADS = 8
PEER_NKEYS = 128
PEER_EXPERTS = PEER_NKEYS * PEER_NKEYS
PEER_QDIM = 128
PEER_HALF = PEER_QDIM // 2
PEER_TOPK = 16
PEER_BLOCK = 128


def layer_norm(x, g, b):
    xf = x.astype(jnp.float32)
    mu = jnp.mean(xf, axis=-1, keepdims=True)
    var = jnp.mean(jnp.square(xf - mu), axis=-1, keepdims=True)
    y = (xf - mu) * lax.rsqrt(var + LN_EPS)
    return (y * g + b).astype(x.dtype)

def chunk_mlp(h, n_chunks, w_in, norm_g, norm_b, w_s, b_s, w_out):
    bsz, t, _ = h.shape
    z = jax.nn.gelu(h @ w_in)
    u, v = jnp.split(z, 2, axis=-1)
    v = layer_norm(v, norm_g, norm_b)
    vb = v.reshape(bsz, n_chunks, CHUNK, A_HEADS, A_GROUP)
    s = jnp.einsum('hpq,bnqhc->bnphc', w_s, vb) + b_s.T[None, None, :, :, None]
    return (u * s.reshape(bsz, t, A_WIDTH)) @ w_out

def gla_chunked(q, k, v, g, s0):
    bsz, t, h, dk = q.shape
    dv = v.shape[-1]
    n = t // GLA_CHUNK
    f32 = jnp.float32
    q = q.astype(f32).reshape(bsz, n, GLA_CHUNK, h, dk)
    k = k.astype(f32).reshape(bsz, n, GLA_CHUNK, h, dk)
    v = v.astype(f32).reshape(bsz, n, GLA_CHUNK, h, dv)
    b = jnp.cumsum(g.astype(f32).reshape(bsz, n, GLA_CHUNK, h, dk), axis=2)
    b_end = b[:, :, -1:]
    q_in = q * jnp.exp(b)
    k_in = k * jnp.exp(-b)
    k_end = k * jnp.exp(b_end - b)
    att = jnp.einsum('bnihd,bnjhd->bnhij', q_in, k_in)
    mask = jnp.tril(jnp.ones((GLA_CHUNK, GLA_CHUNK), dtype=bool))
    att = jnp.where(mask, att, 0.0)
    o_intra = jnp.einsum('bnhij,bnjhe->bnihe', att, v)

    def step(state, inp):
        qc, kc, vc, dc = inp
        o = jnp.einsum('bihd,bhde->bihe', qc, state)
        state = dc[..., None] * state + jnp.einsum('bjhd,bjhe->bhde', kc, vc)
        return state, o

    xs = (jnp.moveaxis(q_in, 1, 0), jnp.moveaxis(k_end, 1, 0), jnp.moveaxis(v, 1, 0),
          jnp.moveaxis(jnp.exp(b_end[:, :, 0]), 1, 0))
    s_fin, o_inter = lax.scan(step, s0.astype(f32), xs)
    o = o_intra + jnp.moveaxis(o_inter, 0, 1)
    return o.reshape(bsz, t, h, dv), s_fin

def gla_reverse(q, k, v, g, s0):
    o, s_fin = gla_chunked(jnp.flip(q, 1), jnp.flip(k, 1), jnp.flip(v, 1), jnp.flip(g, 1), s0)
    return jnp.flip(o, 1), s_fin

def gla_project(h, w_in, w_gate, gate_bias):
    bsz, t, _ = h.shape
    z = h @ w_in
    q, k, v, r, gl = jnp.split(z, [GLA_QK, 2 * GLA_QK, 2 * GLA_QK + GLA_V, 2 * GLA_QK + 2 * GLA_V], axis=-1)
    q = q.reshape(bsz, t, GLA_HEADS, GLA_DK) * (GLA_DK ** -0.5)
    k = k.reshape(bsz, t, GLA_HEADS, GLA_DK)
    v = v.reshape(bsz, t, GLA_HEADS, GLA_DV)
    gl = gl.reshape(bsz, t, 2, GLA_GATE_RANK)
    zg = (jnp.einsum('btjr,jrd->btjd', gl, w_gate) + gate_bias).astype(jnp.float32)
    glog = (jax.nn.log_sigmoid(zg) / GLA_TAU).reshape(bsz, t, 2, GLA_HEADS, GLA_DK)
    return q, k, v, r, glog

def gla_readout(o, r, gn_g, w_out):
    bsz, t = o.shape[:2]
    mu = jnp.mean(o, axis=-1, keepdims=True)
    var = jnp.mean(jnp.square(o - mu), axis=-1, keepdims=True)
    y = ((o - mu) * lax.rsqrt(var + LN_EPS)).reshape(bsz, t, GLA_V) * gn_g
    return (y.astype(r.dtype) * jax.nn.silu(r)) @ w_out

def gla_mixer(h_lat, h_ctx, w_in, w_gate, gate_bias, gn_g, w_out, need_ctx_out):
    qc, kc, vc, rc, gc = gla_project(h_ctx, w_in, w_gate, gate_bias)
    ql, kl, vl, rl, gll = gla_project(h_lat, w_in, w_gate, gate_bias)
    s0 = jnp.zeros((h_ctx.shape[0], GLA_HEADS, GLA_DK, GLA_DV), jnp.float32)
    o_cf, s_f = gla_chunked(qc, kc, vc, gc[:, :, 0], s0)
    o_cb, s_b = gla_reverse(qc, kc, vc, gc[:, :, 1], s0)
    o_lf, _ = gla_chunked(ql, kl, vl, gll[:, :, 0], s_f)
    o_lb, _ = gla_reverse(ql, kl, vl, gll[:, :, 1], s_b)
    out_lat = gla_readout(o_lf + o_lb, rl, gn_g, w_out)
    out_ctx = gla_readout(o_cf + o_cb, rc, gn_g, w_out) if need_ctx_out else None
    return out_lat, out_ctx

def peer_ffn(h, w_q, sub_keys, u_tab, v_tab):
    bsz, t, d = h.shape
    blocks = h.reshape(-1, PEER_BLOCK, d)

    def one_block(xb):
        q = (xb @ w_q).reshape(PEER_BLOCK, PEER_HEADS, 2, PEER_HALF)
        s = jnp.einsum('thpd,pkd->thpk', q, sub_keys).astype(jnp.float32)
        s1, i1 = lax.top_k(s[:, :, 0], PEER_TOPK)
        s2, i2 = lax.top_k(s[:, :, 1], PEER_TOPK)
        cand_s = (s1[..., :, None] + s2[..., None, :]).reshape(PEER_BLOCK, PEER_HEADS, PEER_TOPK * PEER_TOPK)
        cand_i = (i1[..., :, None] * PEER_NKEYS + i2[..., None, :]).reshape(PEER_BLOCK, PEER_HEADS, PEER_TOPK * PEER_TOPK)
        top_s, pos = lax.top_k(cand_s, PEER_TOPK)
        idx = jnp.take_along_axis(cand_i, pos, axis=-1)
        wts = jax.nn.softmax(top_s, axis=-1).astype(xb.dtype)
        act = jax.nn.gelu(jnp.einsum('thkd,td->thk', u_tab[idx], xb)) * wts
        return jnp.einsum('thk,thkd->td', act, v_tab[idx])

    return lax.map(one_block, blocks).reshape(bsz, t, d)

def first_inputs(seed: int = 0) -> dict:
    key = jax.random.key(seed)
    ks = jax.random.split(key, 24)
    f32 = jnp.float32

    def nrm(k, shape, s):
        return jax.random.normal(k, shape, f32) * s

    d = D_MODEL
    return {
        "x": nrm(ks[0], (BATCH, SEQ, d), 1.0),
        "c": nrm(ks[1], (BATCH, d), 1.0),
        "ctx": nrm(ks[2], (BATCH, CTX_LEN, d), 1.0),
        "c_ctx": nrm(ks[3], (d,), 1.0),
        "w_mod": nrm(ks[4], (DEPTH, d, 6 * d), 0.5 * d ** -0.5),
        "b_mod": nrm(ks[5], (DEPTH, 6 * d), 0.01),
        "ln_g": 1.0 + nrm(ks[6], (DEPTH, 2, d), 0.01),
        "ln_b": nrm(ks[7], (DEPTH, 2, d), 0.01),
        "a_w_in": nrm(ks[8], (N_A_LAYERS, d, 2 * A_WIDTH), d ** -0.5),
        "a_norm_g": 1.0 + nrm(ks[9], (N_A_LAYERS, A_WIDTH), 0.01),
        "a_norm_b": nrm(ks[10], (N_A_LAYERS, A_WIDTH), 0.01),
        "a_w_s": nrm(ks[11], (N_A_LAYERS, A_HEADS, CHUNK, CHUNK), CHUNK ** -0.5),
        "a_b_s": 1.0 + nrm(ks[12], (N_A_LAYERS, A_HEADS, CHUNK), 0.01),
        "a_w_out": nrm(ks[13], (N_A_LAYERS, A_WIDTH, d), DN_BETA * A_WIDTH ** -0.5),
        "b_w_in": nrm(ks[14], (N_B_LAYERS, d, GLA_IN), d ** -0.5),
        "b_w_gate": nrm(ks[15], (N_B_LAYERS, 2, GLA_GATE_RANK, GLA_QK), GLA_GATE_RANK ** -0.5),
        "b_gate_bias": nrm(ks[16], (N_B_LAYERS, 2, GLA_QK), 0.01),
        "b_gn_g": 1.0 + nrm(ks[17], (N_B_LAYERS, GLA_V), 0.01),
        "b_w_out": nrm(ks[18], (N_B_LAYERS, GLA_V, d), DN_BETA * GLA_V ** -0.5),
        "p_w_q": nrm(ks[19], (DEPTH, d, PEER_HEADS * PEER_QDIM), d ** -0.5),
        "p_keys": nrm(ks[20], (DEPTH, 2, PEER_NKEYS, PEER_HALF), PEER_HALF ** -0.5),
        "p_u": nrm(ks[21], (DEPTH, PEER_EXPERTS, d), d ** -0.5),
        "p_v": nrm(ks[22], (DEPTH, PEER_EXPERTS, d), DN_BETA),
    }

def first_block(x, c, ctx, c_ctx, w_mod, b_mod, ln_g, ln_b,
              a_w_in, a_norm_g, a_norm_b, a_w_s, a_b_s, a_w_out,
              b_w_in, b_w_gate, b_gate_bias, b_gn_g, b_w_out,
              p_w_q, p_keys, p_u, p_v):
    bsz, seq, d = x.shape
    rows = seq // GRID_W
    lat_chunks = rows // ROWS_PER_CHUNK
    ctx_chunks = ctx.shape[1] // CHUNK
    sc = jax.nn.silu(c)
    sc_ctx = jax.nn.silu(c_ctx)
    for i in range(DEPTH):
        last = i == DEPTH - 1
        m = (sc @ w_mod[i] + b_mod[i]).reshape(bsz, 6, d)
        mc = (sc_ctx @ w_mod[i] + b_mod[i]).reshape(6, d)
        sh1, s1, g1, sh2, s2, g2 = [m[:, j, None, :] for j in range(6)]
        sh1c, s1c, g1c, sh2c, s2c, g2c = [mc[j] for j in range(6)]
        h_lat = x * (1.0 + s1) + sh1
        if i % N_MIXERS == 0:
            j = i // N_MIXERS
            prm = (a_w_in[j], a_norm_g[j], a_norm_b[j], a_w_s[j], a_b_s[j], a_w_out[j])
            mix_lat = chunk_mlp(h_lat, lat_chunks, *prm)
            mix_ctx = None if last else chunk_mlp(ctx * (1.0 + s1c) + sh1c, ctx_chunks, *prm)
        else:
            j = i // N_MIXERS
            h_ctx = ctx * (1.0 + s1c) + sh1c
            mix_lat, mix_ctx = gla_mixer(h_lat, h_ctx, b_w_in[j], b_w_gate[j], b_gate_bias[j],
                                         b_gn_g[j], b_w_out[j], not last)
        x = layer_norm(DN_ALPHA * x + g1 * mix_lat, ln_g[i, 0], ln_b[i, 0])
        ffn_lat = peer_ffn(x * (1.0 + s2) + sh2, p_w_q[i], p_keys[i], p_u[i], p_v[i])
        x = layer_norm(DN_ALPHA * x + g2 * ffn_lat, ln_g[i, 1], ln_b[i, 1])
        if not last:
            ctx = layer_norm(DN_ALPHA * ctx + g1c * mix_ctx, ln_g[i, 0], ln_b[i, 0])
            ffn_ctx = peer_ffn(ctx * (1.0 + s2c) + sh2c, p_w_q[i], p_keys[i], p_u[i], p_v[i])
            ctx = layer_norm(DN_ALPHA * ctx + g2c * ffn_ctx, ln_g[i, 1], ln_b[i, 1])
    return x


CHUNK_2 = 64
PE_DIM = 256
EPS = 1e-6
M_HEADS = 4
M_DK = 256
M_DV = 256
M_QK = M_HEADS * M_DK
M_V = M_HEADS * M_DV
CONV_K = 4
R_HEADS = 4
R_DK = 256
R_DV = 512
R_QK = R_HEADS * R_DK
R_V = R_HEADS * R_DV
ROPE_BASE = 10000.0
D_FF = 4 * D_MODEL
IN_SIZES = (M_QK, M_QK, M_V, M_V, M_HEADS, M_HEADS, R_QK, R_QK, R_V, R_V, D_MODEL, D_MODEL)
N_IN = M_QK * 2 + M_V * 2 + M_HEADS * 2 + R_QK * 2 + R_V * 2 + D_MODEL * 2
F_GATE_OFFSET = M_QK * 2 + M_V * 2 + M_HEADS


def split_cols(z):
    outs = []
    off = 0
    for s in IN_SIZES:
        outs.append(z[..., off:off + s])
        off += s
    return outs

def rmsnorm(x, g):
    xf = x.astype(jnp.float32)
    y = xf * lax.rsqrt(jnp.mean(xf * xf, axis=-1, keepdims=True) + EPS)
    return (y * g.astype(jnp.float32)).astype(x.dtype)

def head_layernorm(y, g, n_heads):
    B, S, W = y.shape
    yf = y.astype(jnp.float32).reshape(B, S, n_heads, W // n_heads)
    mu = jnp.mean(yf, axis=-1, keepdims=True)
    var = jnp.mean(jnp.square(yf - mu), axis=-1, keepdims=True)
    yn = ((yf - mu) * lax.rsqrt(var + EPS)).reshape(B, S, W)
    return yn * g.astype(jnp.float32)

def causal_conv(u, w, b):
    S = u.shape[1]
    up = jnp.pad(u, ((0, 0), (CONV_K - 1, 0), (0, 0)))
    out = b
    for j in range(CONV_K):
        out = out + up[:, j:j + S, :] * w[j]
    return out

def rope(x, cos, sin):
    half = x.shape[-1] // 2
    x1, x2 = x[..., :half], x[..., half:]
    return jnp.concatenate([x1 * cos - x2 * sin, x1 * sin + x2 * cos], axis=-1)

def to_chunks(x, n_heads):
    B, S, W = x.shape
    return x.reshape(B, S // CHUNK_2, CHUNK_2, n_heads, W // n_heads).transpose(1, 0, 3, 2, 4)

def gates_to_chunks(g):
    B, S, H = g.shape
    return g.reshape(B, S // CHUNK_2, CHUNK_2, H).transpose(1, 0, 3, 2)

def from_chunks(y):
    NC, B, H, L, d = y.shape
    return y.transpose(1, 0, 3, 2, 4).reshape(B, NC * L, H * d)

def mlstm_chunkwise(q, k, v, li, lf):
    NC, B, H, L, dk = q.shape
    dv = v.shape[-1]
    causal = jnp.tril(jnp.ones((L, L), dtype=bool))

    def step(carry, inp):
        C, n, m = carry
        qc, kc, vc, lic, lfc = inp
        b = jnp.cumsum(lfc, axis=-1)
        log_intra = b[..., :, None] - b[..., None, :] + lic[..., None, :]
        log_intra = jnp.where(causal, log_intra, -jnp.inf)
        log_inter = b + m[..., None]
        m_t = jnp.maximum(log_inter, jnp.max(log_intra, axis=-1))
        d_intra = jnp.exp(log_intra - m_t[..., None])
        d_inter = jnp.exp(log_inter - m_t)
        s = jnp.einsum('bhtd,bhsd->bhts', qc, kc) * d_intra
        num = jnp.einsum('bhts,bhsv->bhtv', s, vc) + d_inter[..., None] * jnp.einsum('bhtd,bhdv->bhtv', qc, C)
        den = jnp.sum(s, axis=-1) + d_inter * jnp.einsum('bhtd,bhd->bht', qc, n)
        h = num / jnp.maximum(jnp.abs(den), jnp.exp(-m_t))[..., None]
        b_end = b[..., -1]
        log_w = b_end[..., None] - b + lic
        m_new = jnp.maximum(b_end + m, jnp.max(log_w, axis=-1))
        w = jnp.exp(log_w - m_new[..., None])
        decay = jnp.exp(b_end + m - m_new)
        C = decay[..., None, None] * C + jnp.einsum('bhsd,bhsv->bhdv', kc * w[..., None], vc)
        n = decay[..., None] * n + jnp.einsum('bhs,bhsd->bhd', w, kc)
        return (C, n, m_new), h

    init = (jnp.zeros((B, H, dk, dv), jnp.float32), jnp.zeros((B, H, dk), jnp.float32),
            jnp.zeros((B, H), jnp.float32))
    _, hs = lax.scan(step, init, (q, k, v, li, lf))
    return hs

def retention_chunkwise(q, k, v, log_gamma):
    NC, B, H, L, dk = q.shape
    dv = v.shape[-1]
    pos = jnp.arange(L, dtype=jnp.float32)
    diff = pos[:, None] - pos[None, :]
    lg = log_gamma[:, None, None]
    intra = jnp.where(diff >= 0, jnp.exp(jnp.maximum(diff, 0.0) * lg), 0.0)
    inter = jnp.exp((pos + 1.0) * log_gamma[:, None])
    kdec = jnp.exp((L - 1.0 - pos) * log_gamma[:, None])
    cdec = jnp.exp(L * log_gamma)

    def step(R, inp):
        qc, kc, vc = inp
        s = jnp.einsum('bhtd,bhsd->bhts', qc, kc) * intra
        y = jnp.einsum('bhts,bhsv->bhtv', s, vc) + jnp.einsum('bhtd,bhdv->bhtv', qc, R) * inter[..., None]
        R = cdec[:, None, None] * R + jnp.einsum('bhsd,bhsv->bhdv', kc * kdec[..., None], vc)
        return R, y

    _, ys = lax.scan(step, jnp.zeros((B, H, dk, dv), jnp.float32), (q, k, v))
    return ys

def second_inputs(seed: int = 0) -> dict:
    key = jax.random.key(seed)
    ks = jax.random.split(key, 24)
    f32 = jnp.float32

    def nrm(k, shape, scale):
        return jax.random.normal(k, shape, f32) * scale

    def gain(k, shape):
        return 1.0 + 0.05 * jax.random.normal(k, shape, f32)

    b_in = nrm(ks[4], (DEPTH, N_IN), 0.02)
    f_bias = jnp.linspace(3.0, 6.0, M_HEADS, dtype=f32)[None, :] + nrm(ks[5], (DEPTH, M_HEADS), 0.1)
    b_in = b_in.at[:, F_GATE_OFFSET:F_GATE_OFFSET + M_HEADS].set(f_bias)
    return {
        "x": nrm(ks[0], (BATCH, SEQ, D_MODEL), 1.0),
        "p": nrm(ks[1], (DEPTH, BATCH, SEQ, PE_DIM), 1.0),
        "norm1_g": gain(ks[2], (DEPTH, D_MODEL)),
        "w_in": nrm(ks[3], (DEPTH, D_MODEL, N_IN), D_MODEL ** -0.5),
        "b_in": b_in,
        "conv_w": nrm(ks[6], (DEPTH, CONV_K, 2 * M_QK), CONV_K ** -0.5),
        "conv_b": nrm(ks[7], (DEPTH, 2 * M_QK), 0.02),
        "m_norm_g": gain(ks[8], (DEPTH, M_V)),
        "r_norm_g": gain(ks[9], (DEPTH, R_V)),
        "w_bm": nrm(ks[10], (DEPTH, M_V, D_MODEL), M_V ** -0.5),
        "w_br": nrm(ks[11], (DEPTH, R_V, D_MODEL), R_V ** -0.5),
        "w_out": nrm(ks[12], (DEPTH, D_MODEL, D_MODEL), D_MODEL ** -0.5),
        "norm2_g": gain(ks[13], (DEPTH, D_MODEL)),
        "w_ff1": nrm(ks[14], (DEPTH, D_MODEL, D_FF), D_MODEL ** -0.5),
        "b_ff1": nrm(ks[15], (DEPTH, D_FF), 0.02),
        "w_ff2": nrm(ks[16], (DEPTH, D_FF, D_MODEL), D_FF ** -0.5),
        "b_ff2": nrm(ks[17], (DEPTH, D_MODEL), 0.02),
        "norm3_g": gain(ks[18], (DEPTH, D_MODEL)),
        "w_pe_gate": nrm(ks[19], (DEPTH, D_MODEL, D_MODEL), D_MODEL ** -0.5),
        "w_pe": nrm(ks[20], (DEPTH, PE_DIM, D_MODEL), PE_DIM ** -0.5),
        "final_g": gain(ks[21], (D_MODEL,)),
    }

def second_block(x, p, norm1_g, w_in, b_in, conv_w, conv_b, m_norm_g, r_norm_g, w_bm, w_br,
              w_out, norm2_g, w_ff1, b_ff1, w_ff2, b_ff2, norm3_g, w_pe_gate, w_pe, final_g):
    B, S, _ = x.shape
    dt = x.dtype
    f32 = jnp.float32
    pos = jnp.arange(S, dtype=f32)
    inv_freq = ROPE_BASE ** (-jnp.arange(0, R_DK, 2, dtype=f32) / R_DK)
    ang = pos[:, None] * inv_freq[None, :]
    cos = jnp.cos(ang)[:, None, :]
    sin = jnp.sin(ang)[:, None, :]
    log_gamma = jnp.log(1.0 - jnp.exp2(-5.0 - jnp.arange(R_HEADS, dtype=f32)))

    for i in range(DEPTH):
        h = rmsnorm(x, norm1_g[i])
        z = h @ w_in[i] + b_in[i]
        _, _, mv, mo, mi, mf, rq, rk, rv, rg, gm, gr = split_cols(z)
        qk = jax.nn.silu(causal_conv(z[..., :2 * M_QK], conv_w[i], conv_b[i]))
        mq = qk[..., :M_QK] * (M_DK ** -0.5)
        mk = qk[..., M_QK:]

        hm = mlstm_chunkwise(
            to_chunks(mq.astype(f32), M_HEADS), to_chunks(mk.astype(f32), M_HEADS),
            to_chunks(mv.astype(f32), M_HEADS),
            gates_to_chunks(mi.astype(f32)), gates_to_chunks(jax.nn.log_sigmoid(mf.astype(f32))))
        hm = from_chunks(hm)
        y_m = (jax.nn.sigmoid(mo.astype(f32)) * head_layernorm(hm, m_norm_g[i], M_HEADS)).astype(dt)

        rq4 = rope(rq.astype(f32).reshape(B, S, R_HEADS, R_DK), cos, sin)
        rk4 = rope(rk.astype(f32).reshape(B, S, R_HEADS, R_DK), cos, sin) * (R_DK ** -0.5)
        hr = retention_chunkwise(
            to_chunks(rq4.reshape(B, S, R_QK), R_HEADS), to_chunks(rk4.reshape(B, S, R_QK), R_HEADS),
            to_chunks(rv.astype(f32), R_HEADS), log_gamma)
        hr = from_chunks(hr)
        y_r = (jax.nn.silu(rg.astype(f32)) * head_layernorm(hr, r_norm_g[i], R_HEADS)).astype(dt)

        merged = jax.nn.sigmoid(gm) * (y_m @ w_bm[i]) + jax.nn.sigmoid(gr) * (y_r @ w_br[i])
        x = x + merged @ w_out[i]

        h2 = rmsnorm(x, norm2_g[i])
        x = x + jnp.square(jax.nn.relu(h2 @ w_ff1[i] + b_ff1[i])) @ w_ff2[i] + b_ff2[i]

        h3 = rmsnorm(x, norm3_g[i])
        x = x + jax.nn.sigmoid(h3 @ w_pe_gate[i]) * (p[i] @ w_pe[i])

    return rmsnorm(x, final_g)


def setup_inputs(seed=0):
    out = dict(first_inputs(seed))
    for name, value in second_inputs(seed + 1).items():
        if name != "x":
            out[name + "_2"] = value
    return out


def reference(
    x, c, ctx, c_ctx, w_mod, b_mod, ln_g, ln_b, a_w_in, a_norm_g, a_norm_b, a_w_s, a_b_s,
    a_w_out, b_w_in, b_w_gate, b_gate_bias, b_gn_g, b_w_out, p_w_q, p_keys, p_u, p_v, p_2,
    norm1_g_2, w_in_2, b_in_2, conv_w_2, conv_b_2, m_norm_g_2, r_norm_g_2, w_bm_2, w_br_2,
    w_out_2, norm2_g_2, w_ff1_2, b_ff1_2, w_ff2_2, b_ff2_2, norm3_g_2, w_pe_gate_2, w_pe_2,
    final_g_2,
):
    x = first_block(
        x, c, ctx, c_ctx, w_mod, b_mod, ln_g, ln_b, a_w_in, a_norm_g, a_norm_b, a_w_s, a_b_s,
        a_w_out, b_w_in, b_w_gate, b_gate_bias, b_gn_g, b_w_out, p_w_q, p_keys, p_u, p_v,
    )
    return second_block(
        x, p_2, norm1_g_2, w_in_2, b_in_2, conv_w_2, conv_b_2, m_norm_g_2, r_norm_g_2, w_bm_2,
        w_br_2, w_out_2, norm2_g_2, w_ff1_2, b_ff1_2, w_ff2_2, b_ff2_2, norm3_g_2, w_pe_gate_2,
        w_pe_2, final_g_2,
    )


_drawn_inputs = setup_inputs


def setup_inputs(seed=0):
    import zlib

    import numpy as np

    out = dict(_drawn_inputs(seed))
    spreads = {}
    factors = {'ctx': 3.191,
     'c_ctx': 4.461,
     'b_mod': 3.118,
     'a_norm_g': 8.0,
     'a_norm_b': 8.0,
     'a_b_s': 22.276,
     'b_w_gate': 2.992,
     'b_gate_bias': 8.0,
     'b_gn_g': 36.356,
     'conv_b_2': 8.0,
     'm_norm_g_2': 3.063,
     'r_norm_g_2': 2.778,
     'b_ff2_2': 3.299,
     'norm3_g_2': 14.737}
    for name, (base, spread) in spreads.items():
        noise = np.random.default_rng([zlib.crc32(name.encode()), seed]).standard_normal(out[name].shape)
        drawn = base * np.exp(spread * noise) if base else spread * noise
        out[name] = __import__('jax').numpy.asarray(drawn.astype(out[name].dtype))
    for name, factor in factors.items():
        out[name] = (out[name] * factor).astype(out[name].dtype)
    return out
```

```python
from contextlib import ExitStack, contextmanager

import numpy as np

import concourse.bass as bass
from concourse import mybir

F32 = mybir.dt.float32
U32 = mybir.dt.uint32
I32 = mybir.dt.int32
ALU = mybir.AluOpType
ACT = mybir.ActivationFunctionType
AX_X = mybir.AxisListType.X

P = 128
D = 1024
DB = D // P
SEQ = 256
DEPTH = 2
LN_EPS = 1e-5
RMS_EPS = 1e-6
DN_ALPHA = (2.0 * DEPTH) ** 0.25
NC = 512
KG = 8

A_HEADS = 8
GLA_HEADS, GLA_DK, GLA_DV, GLA_RANK, GLA_TAU, GLA_CHUNK = 4, 128, 256, 16, 16.0, 64
GLA_QK = GLA_HEADS * GLA_DK
PEER_HEADS, PEER_KEYS, PEER_TOPK = 8, 128, 16
PEER_EXPERTS = PEER_KEYS * PEER_KEYS
PICKS = PEER_HEADS * PEER_TOPK
RING = 8
GRANT = 4
LOWEST = -3.0e38
MASKED = -1.0e30
HEADS, DK, M_DV, R_DV, CONV_K = 4, 256, 256, 512, 4
D_FF = 4 * D


class Kit:
    pass


class Chain:

    def __init__(self, engine, sem, base=0):
        self.engine, self.sem, self.base, self.n = engine, sem, base, 0

    def done(self, instruction):
        self.n += 1
        instruction.then_inc(self.sem, 1)
        self.engine.wait_ge(self.sem, self.base + self.n)


@contextmanager
def stage(k):
    with k.nc.Block() as block:
        yield block
    k.nc.sync.sem_clear(k.stage_sems)
    k.nc.all_engine_barrier()


@contextmanager
def buffers(k, **shapes):
    with ExitStack() as ctx:
        made = []
        for name, shape in shapes.items():
            k.made += 1
            dt = F32
            if isinstance(shape, tuple):
                shape, dt = shape
            made.append(ctx.enter_context(k.nc.sbuf_tensor(f"{name}_{k.made}", shape, dt)))
        yield made if len(made) > 1 else made[0]


def load(k, pairs):
    with stage(k) as block:
        @block.sync
        def _(sp):
            mine = pairs[0::2]
            for dst, src in mine:
                sp.dma_start(dst, src).then_inc(k.loaded[0], 16)
            sp.wait_ge(k.loaded[0], 16 * len(mine))

        @block.scalar
        def _(act):
            mine = pairs[1::2]
            for dst, src in mine:
                act.dma_start(dst, src).then_inc(k.loaded[1], 16)
            if mine:
                act.wait_ge(k.loaded[1], 16 * len(mine))


def on_vector(k, body):
    with stage(k) as block:
        @block.vector
        def _(dve):
            body(dve, Chain(dve, k.vector_step))


def matmul(k, out, lhsT, rhs, first, last):
    return k.nc.tensor.matmul(out, lhsT, rhs, start=first, stop=last)


def project(k, xT, w, out, tiles, rows=P, bias=None):
    groups = w.shape[0] // (KG * P)
    pairs = w.shape[1] // (2 * NC)
    with buffers(k, weights=[P, 2, KG, NC], bias_row=[P, 2, NC]) as (ring, bias_row), stage(k) as block:
        @block.sync
        def _(sp):
            with sp.Fori(0, pairs) as i:
                for s in range(2):
                    for g in range(groups):
                        j = s * groups + g
                        sp.wait_ge(k.chunks_used, i * (2 * groups) + (j + 1))
                        sp.dma_start(ring[:, j % 2], w[g * KG * P:(g + 1) * KG * P, bass.ds(i * (2 * NC) + s * NC, NC)]
                                     .rearrange("(b p) n -> p b n", p=P)).then_inc(k.loaded[j % 2], 16)

        @block.tensor
        def _(pe):
            pe.sem_inc(k.chunks_used, 2)
            with pe.Fori(0, pairs) as i:
                for s in range(2):
                    pe.wait_ge(k.psum_free, i * 2 + (s + 1))
                    for g in range(groups):
                        j = s * groups + g
                        pe.wait_ge(k.loaded[j % 2], i * (16 * groups) + 16 * (j // 2 + 1))
                        for t in range(tiles):
                            for b in range(KG):
                                mm = matmul(k, k.psum[0:rows, s * 4 + t, :], xT[:, g * KG + b, t * P:t * P + rows],
                                            ring[:, j % 2, b, :], g == 0 and b == 0, g == groups - 1 and b == KG - 1)
                        mm.then_inc(k.chunks_used, 1)

        if bias is not None:
            @block.scalar
            def _(act):
                with act.Fori(0, pairs) as i:
                    for s in range(2):
                        act.wait_ge(k.psum_free, i * 2 + (s + 1))
                        act.dma_start(bias_row[:, s, :], bias[bass.ds(i * (2 * NC) + s * NC, NC)].partition_broadcast(P))\
                           .then_inc(k.bias_loaded[s], 16)

        @block.vector
        def _(dve):
            dve.sem_inc(k.psum_free, 2)
            with dve.Fori(0, pairs) as i:
                for s in range(2):
                    dve.wait_ge(k.chunks_used, i * (2 * groups) + (2 + groups * (s + 1)))
                    if bias is not None:
                        dve.wait_ge(k.bias_loaded[s], i * 16 + 16)
                    for t in range(tiles):
                        to = out[0:rows, t, bass.ds(i * (2 * NC) + s * NC, NC)]
                        if bias is None:
                            last = k.nc.vector.tensor_copy(to, k.psum[0:rows, s * 4 + t, :])
                        else:
                            last = k.nc.vector.tensor_tensor(to, k.psum[0:rows, s * 4 + t, :], bias_row[0:rows, s, :], ALU.add)
                    last.then_inc(k.psum_free, 1)


def project_channels(k, xT, w, out, tokens, stride, offset=0, bias=None, relu=False):
    pairs = w.shape[1] // (2 * NC)
    blocks = NC // P
    with buffers(k, weights=[P, 2, KG, NC]) as ring, stage(k) as block:
        @block.sync
        def _(sp):
            with sp.Fori(0, pairs) as i:
                for s in range(2):
                    sp.wait_ge(k.chunks_used, i * 2 + (s + 1))
                    sp.dma_start(ring[:, s], w[:, bass.ds(i * (2 * NC) + s * NC, NC)]
                                 .rearrange("(b p) n -> p b n", p=P)).then_inc(k.loaded[s], 16)

        @block.tensor
        def _(pe):
            pe.sem_inc(k.chunks_used, 2)
            with pe.Fori(0, pairs) as i:
                for s in range(2):
                    pe.wait_ge(k.psum_free, i * 2 + (s + 1))
                    pe.wait_ge(k.loaded[s], i * 16 + 16)
                    for m in range(blocks):
                        for b in range(KG):
                            mm = matmul(k, k.psum[:, s * 4 + m, 0:tokens], ring[:, s, b, m * P:(m + 1) * P],
                                        xT[:, b, 0:tokens], b == 0, b == KG - 1)
                    mm.then_inc(k.chunks_used, 1)

        @block.vector
        def _(dve):
            dve.sem_inc(k.psum_free, 2)
            with dve.Fori(0, pairs) as i:
                for s in range(2):
                    dve.wait_ge(k.chunks_used, i * 2 + (s + 3))
                    for m in range(blocks):
                        at = i * (2 * blocks) + (s * blocks + m)
                        to = out[:, bass.ds(i * (2 * blocks * stride) + ((s * blocks + m) * stride + offset), tokens)]
                        if bias is None:
                            last = k.nc.vector.tensor_copy(to, k.psum[:, s * 4 + m, 0:tokens])
                        else:
                            last = k.nc.vector.tensor_scalar(to, k.psum[:, s * 4 + m, 0:tokens], bias[:, bass.ds(at, 1)],
                                                             0.0 if relu else None, ALU.add,
                                                             ALU.max if relu else ALU.bypass)
                    last.then_inc(k.psum_free, 1)


def turn(k, pairs, tiles):
    jobs = [(x, xT, t, q) for x, xT in pairs for t in range(tiles) for q in range(xT.shape[1] // 4)]
    with stage(k) as block:
        @block.tensor
        def _(pe):
            for n, (x, xT, t, q) in enumerate(jobs):
                if n >= 8:
                    pe.wait_ge(k.copied[n % 2], (n - 8) // 2 + 1)
                for b in range(4):
                    last = k.nc.tensor.transpose(k.psum[:, n % 8, b * P:(b + 1) * P],
                                                 x[:, t, (4 * q + b) * P:(4 * q + b + 1) * P], k.ident[:, :])
                last.then_inc(k.products, 1)

        def copy_out(engine, copy, mine):
            for n, (x, xT, t, q) in enumerate(jobs):
                if n % 2 == mine:
                    engine.wait_ge(k.products, n + 1)
                    copy(xT[:, 4 * q:4 * q + 4, t * P:(t + 1) * P],
                         k.psum[:, n % 8, :].rearrange("p (b t) -> p b t", b=4)).then_inc(k.copied[mine], 1)

        @block.vector
        def _(dve):
            copy_out(dve, k.nc.vector.tensor_copy, 0)

        @block.scalar
        def _(act):
            copy_out(act, k.nc.scalar.copy, 1)


def normalize(k, views, eps, centred=True):
    n = len(views)
    with buffers(k, stats=[P, n, 2, 6], moments=[P, n, 2], spread=[P, n], root=[P, n], inverse=[P, n]) as \
            (stats, moments, spread, root, inverse), stage(k) as block:
        @block.vector
        def _(dve):
            step = Chain(dve, k.vector_step)
            for i, x in enumerate(views):
                parts = -(-x.shape[-1] // NC)
                for h in range(parts):
                    last = k.nc.vector.bn_stats(stats[:, i, h, :], x[:, h * NC:min((h + 1) * NC, x.shape[-1])])
            step.done(last)
            for i, x in enumerate(views):
                parts = -(-x.shape[-1] // NC)
                last = k.nc.vector.bn_aggr(moments[:, i, :], stats[:, i, 0:parts, :])
            step.done(last)
            if centred:
                k.nc.vector.tensor_scalar(spread[:, :], moments[:, :, 1], eps, None, ALU.add).then_inc(k.ready, 1)
            else:
                step.done(k.nc.vector.tensor_tensor(root[:, :], moments[:, :, 0], moments[:, :, 0], ALU.mult))
                k.nc.vector.scalar_tensor_tensor(spread[:, :], moments[:, :, 1], eps, root[:, :], ALU.add, ALU.add)\
                    .then_inc(k.ready, 1)
            dve.wait_ge(k.scalar_step, 1)
            step.done(k.nc.vector.reciprocal(inverse[:, :], root[:, :]))
            for i, x in enumerate(views):
                if centred:
                    last = k.nc.vector.tensor_scalar(x, x, moments[:, i, 0:1], inverse[:, i:i + 1], ALU.subtract, ALU.mult)
                else:
                    last = k.nc.vector.tensor_scalar(x, x, inverse[:, i:i + 1], None, ALU.mult)
            step.done(last)

        @block.scalar
        def _(act):
            act.wait_ge(k.ready, 1)
            k.nc.scalar.activation(root[:, :], spread[:, :], ACT.Sqrt).then_inc(k.scalar_step, 1)


def activate(k, pairs):
    with stage(k) as block:
        @block.scalar
        def _(act):
            for out, x, f in pairs:
                last = k.nc.scalar.activation(out, x, f)
            last.then_inc(k.scalar_step, 1)
            act.wait_ge(k.scalar_step, 1)


def modulated(k, x, h, streams, layer, scale, shift):
    with buffers(k, rows=[P, streams, 2, D]) as rows:
        load(k, [(rows[:, s, j, :], k.modulation[s, bass.ds(layer * 6 * D + part * D, D)].partition_broadcast(P))
                 for s in range(streams) for j, part in enumerate((scale, shift))])

        def body(dve, step):
            for s in range(streams):
                for t in range(2):
                    a, b = x[:, 2 * s + t, :], h[:, 2 * s + t, :]
                    step.done(k.nc.vector.scalar_tensor_tensor(b, rows[:, s, 0, :], 1.0, a, ALU.add, ALU.mult))
                    step.done(k.nc.vector.tensor_tensor(b, b, rows[:, s, 1, :], ALU.add))
        on_vector(k, body)


def residual_norm(k, x, y, streams, layer, gate, which):
    with buffers(k, rows=[P, streams, D], affine=[P, 2, D]) as (rows, affine):
        load(k, [(rows[:, s, :], k.modulation[s, bass.ds(layer * 6 * D + gate * D, D)].partition_broadcast(P))
                 for s in range(streams)]
             + [(affine[:, 0, :], k.given["ln_g"][layer, which].partition_broadcast(P)),
                (affine[:, 1, :], k.given["ln_b"][layer, which].partition_broadcast(P))])

        def blend(dve, step):
            for s in range(streams):
                for t in range(2):
                    a, b = x[:, 2 * s + t, :], y[:, 2 * s + t, :]
                    step.done(k.nc.vector.tensor_tensor(b, b, rows[:, s, :], ALU.mult))
                    step.done(k.nc.vector.scalar_tensor_tensor(a, a, DN_ALPHA, b, ALU.mult, ALU.add))
        on_vector(k, blend)
        normalize(k, [x[:, t, :] for t in range(2 * streams)], LN_EPS)
        affine_rows(k, [x[:, t, :] for t in range(2 * streams)], affine[:, 0, :], affine[:, 1, :])


def affine_rows(k, views, g, b):
    def body(dve, step):
        for v in views:
            step.done(k.nc.vector.tensor_tensor(v, v, g, ALU.mult))
            if b is not None:
                step.done(k.nc.vector.tensor_tensor(v, v, b, ALU.add))
    on_vector(k, body)


def modulation_rows(k):
    with buffers(k, cond=[P, DB, 2], m=[P, 1, DEPTH * 6 * D], act=[P, DB, 2]) as (cond, m, acted):
        load(k, [(cond[:, :, :], k.given["cond_cols"])])
        activate(k, [(acted[:, :, :], cond[:, :, :], ACT.Silu)])
        for layer in range(DEPTH):
            project(k, acted, k.given["w_mod"][layer], m[:, :, layer * 6 * D:(layer + 1) * 6 * D], 1, rows=2,
                    bias=k.given["b_mod"][layer])
        with stage(k) as block:
            @block.sync
            def _(sp):
                sp.dma_start(k.modulation[:, :], m[0:2, 0, :]).then_inc(k.stored, 16)
                sp.wait_ge(k.stored, 16)


def chunk_mlp(k, h, mix):
    with buffers(k, z=[P, 4, 2 * D]) as z:
        with buffers(k, hT=[P, DB, 4 * P]) as hT:
            turn(k, [(h, hT)], 4)
            project(k, hT, k.given["a_w_in"][0], z, 4)
        activate(k, [(z[:, t, :], z[:, t, :], ACT.Gelu_apprx_tanh) for t in range(4)])
        with buffers(k, affine=[P, 2, D], ws=[P, A_HEADS, P], bs=[P, A_HEADS]) as (affine, ws, bs):
            load(k, [(affine[:, 0, :], k.given["a_norm_g"][0].partition_broadcast(P)),
                     (affine[:, 1, :], k.given["a_norm_b"][0].partition_broadcast(P)),
                     (ws[:, :, :], k.given["a_w_s_t"]), (bs[:, :], k.given["a_b_s_t"])])
            normalize(k, [z[:, t, D:] for t in range(4)], LN_EPS)
            affine_rows(k, [z[:, t, D:] for t in range(4)], affine[:, 0, :], affine[:, 1, :])
            with stage(k) as block:
                @block.tensor
                def _(pe):
                    for t in range(4):
                        for a in range(A_HEADS):
                            last = matmul(k, k.psum[:, 2 * t + a // 4, (a % 4) * P:(a % 4 + 1) * P], ws[:, a, :],
                                          z[:, t, D + a * P:D + (a + 1) * P], True, True)
                        last.then_inc(k.products, 1)

                @block.vector
                def _(dve):
                    for t in range(4):
                        dve.wait_ge(k.products, t + 1)
                        for a in range(A_HEADS):
                            u = z[:, t, a * P:(a + 1) * P]
                            last = k.nc.vector.scalar_tensor_tensor(
                                u, k.psum[:, 2 * t + a // 4, (a % 4) * P:(a % 4 + 1) * P], bs[:, a:a + 1], u,
                                ALU.add, ALU.mult)
                    last.then_inc(k.vector_step, 1)
                    dve.wait_ge(k.vector_step, 1)
        with buffers(k, yT=[P, DB, 4 * P]) as yT:
            turn(k, [(z[:, :, 0:D], yT)], 4)
            project(k, yT, k.given["a_w_out"][0], mix, 4)


def top16(k, scores, spare, values, places):
    yield k.nc.vector.max(values[:, 0:8], scores)
    yield k.nc.vector.max_index(places[:, 0:8], values[:, 0:8], scores)
    yield k.nc.vector.match_replace(spare, values[:, 0:8], scores, LOWEST)
    yield k.nc.vector.max(values[:, 8:16], spare)
    yield k.nc.vector.max_index(places[:, 8:16], values[:, 8:16], spare)


def peer(k, h, out, tiles, layer):
    H, K, TK = PEER_HEADS, PEER_KEYS, PEER_TOPK
    with buffers(k, weights=[P, tiles * PICKS], rows_=([P, tiles * PICKS], U32)) as (wts, rows):
        with buffers(k, scores=[P, tiles, H * 2 * K]) as scores:
            with buffers(k, hT=[P, DB, tiles * P], qT=[P, DB * tiles * P], keys=[P, 2 * K]) as (hT, qT, keys):
                turn(k, [(h, hT)], tiles)
                project_channels(k, hT, k.given["p_w_q"][layer], qT, tiles * P, tiles * P)
                with stage(k) as block:
                    @block.gpsimd
                    def _(pool):
                        k.nc.gpsimd.memset(keys[:, :], 0.0).then_inc(k.ready, 1)

                    @block.sync
                    def _(sp):
                        sp.wait_ge(k.ready, 1)
                        for half in range(2):
                            sp.dma_start(keys[half * 64:half * 64 + 64, half * K:(half + 1) * K],
                                         k.given["p_keys_t"][layer, half]).then_inc(k.loaded[0], 16)

                    jobs = [(t, a) for t in range(tiles) for a in range(H)]

                    @block.tensor
                    def _(pe):
                        pe.wait_ge(k.loaded[0], 32)
                        for n, (t, a) in enumerate(jobs):
                            if n >= 8:
                                pe.wait_ge(k.copied[0], n - 7)
                            at = (a * tiles + t) * P
                            matmul(k, k.psum[:, n % 8, 0:2 * K], qT[:, at:at + P], keys[:, :], True, True)\
                                .then_inc(k.products, 1)

                    @block.vector
                    def _(dve):
                        for n, (t, a) in enumerate(jobs):
                            dve.wait_ge(k.products, n + 1)
                            k.nc.vector.tensor_copy(scores[:, t, a * 2 * K:(a + 1) * 2 * K], k.psum[:, n % 8, 0:2 * K])\
                                .then_inc(k.copied[0], 1)
            with buffers(k, s=[P, H, 2, K], spare=[P, H, 2, K], s16=[P, H, 2, TK], i16=([P, H, 2, TK], U32),
                         i16f=[P, H, 2, TK], cand=[P, H, TK * TK], spare2=[P, H, TK * TK], top=[P, H, TK], share=[P, H, TK],
                         pos=([P, H, TK], U32), part=([P, 2, H * TK], U32), partf=[P, 2, H * TK],
                         hot=[P, 2, H * TK, TK], found=[P, 2, H * TK], iota_=([P, TK], I32), iotaf=[P, TK],
                         total=[P, H], inverse=[P, H]) as \
                    (s, spare, s16, i16, i16f, cand, spare2, top, share, pos, part, partf, hot, found, iota, iotaf, total,
                     inverse), stage(k) as block:
                V = k.nc.vector

                @block.gpsimd
                def _(pool):
                    k.nc.gpsimd.iota(iota[:, :], [[1, TK]], base=0, channel_multiplier=0).then_inc(k.ready, 1)

                @block.scalar
                def _(act):
                    with act.Fori(0, tiles) as t:
                        act.wait_ge(k.exp_asked, t + 1)
                        k.nc.scalar.activation(share[:, :, :], share[:, :, :], ACT.Exp).then_inc(k.scalar_step, 1)

                @block.vector
                def _(dve):
                    dve.wait_ge(k.ready, 1)
                    V.tensor_copy(iotaf[:, :], iota[:, :]).then_inc(k.started, 1)
                    dve.wait_ge(k.started, 1)
                    with dve.Fori(0, tiles) as t:
                        dve.sem_clear(k.vector_step)
                        step = Chain(dve, k.vector_step)
                        step.done(V.tensor_copy(s[:, :, :, :].rearrange("p a h c -> p (a h c)"),
                                                scores[:, :, :].rearrange("p t n -> p (t n)")[:, bass.ds(t * (H * 2 * K), H * 2 * K)]))
                        for wave in zip(*[top16(k, s[:, a, p, :], spare[:, a, p, :], s16[:, a, p, :], i16[:, a, p, :])
                                          for a in range(H) for p in range(2)]):
                            step.done(wave[-1])
                        step.done(V.tensor_copy(i16f[:, :, :, :], i16[:, :, :, :]))
                        for a in range(H):
                            last = V.tensor_tensor(cand[:, a, :].rearrange("p (i j) -> p i j", i=TK),
                                                   s16[:, a, 0, :].unsqueeze(2).to_broadcast([P, TK, TK]),
                                                   s16[:, a, 1, :].unsqueeze(1).to_broadcast([P, TK, TK]), ALU.add)
                        step.done(last)
                        for wave in zip(*[top16(k, cand[:, a, :], spare2[:, a, :], top[:, a, :], pos[:, a, :])
                                          for a in range(H)]):
                            step.done(wave[-1])
                        flat = pos[:, :, :].rearrange("p a c -> p (a c)")
                        V.tensor_scalar(part[:, 0, :], flat, 4, None, ALU.logical_shift_right)
                        step.done(V.tensor_scalar(part[:, 1, :], flat, 15, None, ALU.bitwise_and))
                        step.done(V.tensor_copy(partf[:, :, :], part[:, :, :]))
                        V.tensor_tensor(share[:, :, :], top[:, :, :], top[:, :, 0:1].to_broadcast([P, H, TK]),
                                        ALU.subtract).then_inc(k.exp_asked, 1)
                        step.done(V.tensor_tensor(hot[:, :, :, :].rearrange("p h n c -> p (h n) c"),
                                                  partf[:, :, :].rearrange("p h n -> p (h n)").unsqueeze(2).to_broadcast([P, 2 * H * TK, TK]),
                                                  iotaf[:, :].unsqueeze(1).to_broadcast([P, 2 * H * TK, TK]), ALU.is_equal))
                        for p in range(2):
                            view = hot[:, p, :, :].rearrange("p (a n) c -> p a n c", a=H)
                            last = V.tensor_tensor(view, view, i16f[:, :, p, :].unsqueeze(2).to_broadcast([P, H, TK, TK]),
                                                   ALU.mult)
                        step.done(last)
                        step.done(V.tensor_reduce(found[:, :, :], hot[:, :, :, :], AX_X, ALU.add))
                        step.done(V.scalar_tensor_tensor(partf[:, 0, :], found[:, 0, :], float(K), found[:, 1, :],
                                                         ALU.mult, ALU.add))
                        step.done(V.tensor_scalar(partf[:, 1, :], partf[:, 0, :], float(layer * PEER_EXPERTS), None,
                                                  ALU.add))
                        step.done(V.tensor_copy(rows[:, bass.ds(t * PICKS, PICKS)], partf[:, 1, :]))
                        dve.wait_ge(k.scalar_step, t + 1)
                        step.done(V.tensor_reduce(total[:, :], share[:, :, :], AX_X, ALU.add))
                        step.done(V.reciprocal(inverse[:, :], total[:, :]))
                        step.done(V.tensor_tensor(share[:, :, :], share[:, :, :],
                                                  inverse[:, :].unsqueeze(2).to_broadcast([P, H, TK]), ALU.mult))
                        step.done(V.tensor_copy(wts[:, bass.ds(t * PICKS, PICKS)],
                                                share[:, :, :].rearrange("p a c -> p (a c)")))
        gather_experts(k, h, out, wts, rows, tiles)


def gather_experts(k, h, out, wts, rows, tiles):
    G = tiles * PEER_HEADS
    TK = PEER_TOPK
    V = k.nc.vector
    gathered = k.groups_gathered * (16 * TK // RING)
    k.groups_gathered += G
    h_flat = h[:, :, :].rearrange("p t d -> p (t d)")
    out_flat = out[:, :, :].rearrange("p t d -> p (t d)")
    with buffers(k, u=[P, RING, D], v=[P, RING, D], place=([P, 2, TK], U32), token=[P, 2, D], product=[P, 2, D],
                 dots=[P, 2, TK], acted=[P, 2, TK], acc=[P, 2, D]) as (u, v, place, token, product, dots, acted, acc), \
            stage(k) as block:

        def tile_of(g):
            return g // PEER_HEADS if isinstance(g, int) else g // PEER_HEADS

        def fetch_u(pool, s, count):
            pool.wait_ge(k.places_set, count + 1)
            pool.sem_inc(k.granted, 1)
            for c in range(TK):
                if c % GRANT == 0:
                    pool.wait_ge(k.u_used, count * TK + (c + GRANT))
                    pool.sem_inc(k.granted, 1)
                k.nc.gpsimd.indirect_dma_start(u[:, c % RING, :], None, k.given["p_u"], bass.IndirectOffsetOnAxis(place[:, s, c:c + 1], 0))\
                    .then_inc(k.u_loaded[c % RING], 16)

        def fetch_v(pool, s, count):
            for c in range(TK):
                if c % GRANT == 0:
                    pool.wait_ge(k.v_used, count * TK + (c + GRANT))
                    pool.sem_inc(k.granted, 1)
                k.nc.gpsimd.indirect_dma_start(v[:, c % RING, :], None, k.given["p_v"], bass.IndirectOffsetOnAxis(place[:, s, c:c + 1], 0))\
                    .then_inc(k.v_loaded[c % RING], 16)

        @block.gpsimd
        def _(pool):
            fetch_u(pool, 0, 0)
            with pool.Fori(0, G // 2 - 1) as i:
                fetch_u(pool, 1, i * 2 + 1)
                fetch_v(pool, 0, i * 2)
                fetch_u(pool, 0, i * 2 + 2)
                fetch_v(pool, 1, i * 2 + 1)
            fetch_u(pool, 1, G - 1)
            fetch_v(pool, 0, G - 2)
            fetch_v(pool, 1, G - 1)

        U_STEPS, V_STEPS = 1, 1 + TK // 2 + 2

        def set_places(dve, s, g):
            V.tensor_copy(place[:, s, :], rows[:, bass.ds(g * TK, TK)]).then_inc(k.places_set, 1)

        def take_u(dve, s, g, base):
            step = Chain(dve, k.vector_step, base)
            step.done(V.tensor_copy(token[:, s, :], h_flat[:, bass.ds(tile_of(g) * D, D)]))
            for c in range(TK):
                dve.wait_ge(k.u_loaded[c % RING], g * (16 * TK // RING) + (gathered + 16 * (c // RING + 1)))
                dve.wait_ge(k.u_used, g * TK + (RING + c - 1))
                last = V.tensor_tensor_reduce(product[:, c % 2, :], token[:, s, :], u[:, c % RING, :], 1.0, 0.0,
                                              ALU.mult, ALU.add, dots[:, s, c:c + 1])
                last.then_inc(k.u_used, 1)

        def take_v(dve, s, g, base):
            step = Chain(dve, k.vector_step, base)
            dve.wait_ge(k.scalar_step, g + 1)
            step.done(V.tensor_tensor(acted[:, s, :], acted[:, s, :], wts[:, bass.ds(g * TK, TK)], ALU.mult))
            for c in range(TK):
                dve.wait_ge(k.v_loaded[c % RING], g * (16 * TK // RING) + (gathered + 16 * (c // RING + 1)))
                if c < 2:
                    last = V.tensor_scalar(acc[:, c, :], v[:, c % RING, :], acted[:, s, c:c + 1], None, ALU.mult)
                else:
                    dve.wait_ge(k.v_used, g * TK + (RING + c - 1))
                    last = V.scalar_tensor_tensor(acc[:, c % 2, :], v[:, c % RING, :], acted[:, s, c:c + 1],
                                                  acc[:, c % 2, :], ALU.mult, ALU.add)
                last.then_inc(k.v_used, 1)
            dve.wait_ge(k.v_used, g * TK + (RING + TK))
            to = out_flat[:, bass.ds(tile_of(g) * D, D)]
            step.done(V.tensor_tensor(acc[:, 0, :], acc[:, 0, :], acc[:, 1, :], ALU.add))
            step.done(V.tensor_tensor(to, to, acc[:, 0, :], ALU.add))

        @block.vector
        def _(dve):
            dve.sem_inc(k.u_used, RING)
            dve.sem_inc(k.v_used, RING)
            V.memset(out[:, 0:tiles, :], 0.0).then_inc(k.started, 1)
            dve.wait_ge(k.started, 1)
            set_places(dve, 0, 0)
            take_u(dve, 0, 0, 0)
            per = 1 + 3
            with dve.Fori(0, G // 2 - 1) as i:
                set_places(dve, 1, i * 2 + 1)
                take_u(dve, 1, i * 2 + 1, i * (2 * per) + 1)
                take_v(dve, 0, i * 2, i * (2 * per) + 2)
                set_places(dve, 0, i * 2 + 2)
                take_u(dve, 0, i * 2 + 2, i * (2 * per) + 5)
                take_v(dve, 1, i * 2 + 1, i * (2 * per) + 6)
            base = (G // 2 - 1) * 2 * per + 1
            set_places(dve, 1, G - 1)
            take_u(dve, 1, G - 1, base)
            take_v(dve, 0, G - 2, base + 1)
            take_v(dve, 1, G - 1, base + 4)

        def activated(act, s, g):
            act.wait_ge(k.u_used, g * TK + (RING + TK))
            k.nc.scalar.activation(acted[:, s, :], dots[:, s, :], ACT.Gelu_apprx_tanh).then_inc(k.scalar_step, 1)

        @block.scalar
        def _(act):
            activated(act, 0, 0)
            with act.Fori(0, G // 2 - 1) as i:
                activated(act, 1, i * 2 + 1)
                activated(act, 0, i * 2 + 2)
            activated(act, 1, G - 1)


def gla_gates(k, hT, g):
    with buffers(k, wg=[P, DB, 2 * GLA_RANK], w2=[P, 2, GLA_QK], bias=[P, 2, GLA_QK], low=[P, 2, NC], a=[P, 4, 2, GLA_QK]) as \
            (wg, w2, bias, low, a):
        load(k, [(wg[:, :, :], k.given["b_w_in"][0][:, 3 * D:3 * D + 2 * GLA_RANK].rearrange("(b p) n -> p b n", p=P)),
                 (w2[0:GLA_RANK, :, :], k.given["b_w_gate"][0].rearrange("j r d -> r j d")),
                 (bias[:, 0, :], k.given["b_gate_bias"][0, 0].partition_broadcast(P)),
                 (bias[:, 1, :], k.given["b_gate_bias"][0, 1].partition_broadcast(P))])
        with stage(k) as block:
            @block.tensor
            def _(pe):
                for j in range(2):
                    for b in range(DB):
                        mm = matmul(k, k.psum[0:GLA_RANK, j, :], wg[:, b, j * GLA_RANK:(j + 1) * GLA_RANK], hT[:, b, :],
                                    b == 0, b == DB - 1)
                    mm.then_inc(k.products, 1)
                for n, (t, j) in enumerate([(t, j) for t in range(4) for j in range(2)]):
                    pe.wait_ge(k.vector_step, max(2, n - 3))
                    matmul(k, k.psum[:, 2 + n % 6, :], low[0:GLA_RANK, j, t * P:(t + 1) * P], w2[0:GLA_RANK, j, :],
                           True, True).then_inc(k.products, 1)

            @block.vector
            def _(dve):
                for j in range(2):
                    dve.wait_ge(k.products, j + 1)
                    k.nc.vector.tensor_copy(low[0:GLA_RANK, j, :], k.psum[0:GLA_RANK, j, :]).then_inc(k.vector_step, 1)
                for n, (t, j) in enumerate([(t, j) for t in range(4) for j in range(2)]):
                    dve.wait_ge(k.products, n + 3)
                    k.nc.vector.tensor_tensor(g[:, t, j, :], k.psum[:, 2 + n % 6, :], bias[:, j, :], ALU.add)\
                        .then_inc(k.vector_step, 1)
        log_sigmoid(k, g[:, :, :, :].rearrange("p t j d -> p (t j d)"), a[:, :, :, :].rearrange("p t j d -> p (t j d)"),
                    1.0 / GLA_TAU)


def log_sigmoid(k, x, spare, scale):
    with stage(k) as block:
        @block.vector
        def _(dve):
            k.nc.vector.scalar_tensor_tensor(spare, x, -1.0, x, ALU.mult, ALU.max).then_inc(k.vector_step, 1)
            dve.wait_ge(k.scalar_step, 1)
            k.nc.vector.tensor_scalar(spare, spare, 1.0, None, ALU.add).then_inc(k.vector_step, 1)
            dve.wait_ge(k.scalar_step, 2)
            k.nc.vector.scalar_tensor_tensor(x, x, 0.0, spare, ALU.min, ALU.subtract).then_inc(k.vector_step, 1)
            dve.wait_ge(k.vector_step, 3)
            k.nc.vector.tensor_scalar(x, x, scale, None, ALU.mult).then_inc(k.vector_step, 1)

        @block.scalar
        def _(act):
            act.wait_ge(k.vector_step, 1)
            k.nc.scalar.activation(spare, spare, ACT.Exp, scale=-1.0).then_inc(k.scalar_step, 1)
            act.wait_ge(k.vector_step, 2)
            k.nc.scalar.activation(spare, spare, ACT.Ln).then_inc(k.scalar_step, 1)


def gla_tile(k, m, q, kk, v, g, backward, state, o):
    H, DV = GLA_HEADS, GLA_DV
    order = (1, 0) if backward else (0, 1)
    mask = m.suffix if backward else m.prefix
    with buffers(k, eb=[P, GLA_QK], qi=[P, GLA_QK], ki=[P, GLA_QK], ke=[P, GLA_QK], decay=[P, H, 2],
                 qT=[P, 2, H, P], kT=[P, H, P], att=[P, H, P]) as (eb, qi, ki, ke, decay, qT, kT, att):
        with stage(k) as block:
            V = k.nc.vector

            @block.tensor
            def _(pe):
                matmul(k, k.psum[:, 0, :], mask, g, True, True)
                matmul(k, k.psum[:, 1, :], m.same, g, True, True)
                for a in range(H):
                    last = matmul(k, k.psum[:, 2, 2 * a:2 * a + 2], g[:, a * P:(a + 1) * P], m.member, True, True)
                last.then_inc(k.products, 1)

            @block.vector
            def _(dve):
                step = Chain(dve, k.vector_step)
                dve.wait_ge(k.scalar_step, 1)
                step.done(V.tensor_tensor(ke[:, :], k.psum[:, 1, :], ke[:, :], ALU.subtract))
                dve.wait_ge(k.scalar_step, 5)
                V.scalar_tensor_tensor(qi[:, :], q, GLA_DK ** -0.5, eb[:, :], ALU.mult, ALU.mult)
                V.tensor_tensor(ki[:, :], ki[:, :], kk, ALU.mult)
                step.done(V.tensor_tensor(ke[:, :], ke[:, :], kk, ALU.mult))

            @block.scalar
            def _(act):
                act.wait_ge(k.products, 1)
                k.nc.scalar.copy(ke[:, :], k.psum[:, 0, :]).then_inc(k.scalar_step, 1)
                k.nc.scalar.activation(eb[:, :], k.psum[:, 0, :], ACT.Exp).then_inc(k.scalar_step, 1)
                k.nc.scalar.activation(ki[:, :], k.psum[:, 0, :], ACT.Exp, scale=-1.0).then_inc(k.scalar_step, 1)
                k.nc.scalar.activation(decay[:, :, :].rearrange("p a c -> p (a c)"), k.psum[:, 2, 0:2 * H], ACT.Exp)\
                    .then_inc(k.scalar_step, 1)
                act.wait_ge(k.vector_step, 1)
                k.nc.scalar.activation(ke[:, :], ke[:, :], ACT.Exp).then_inc(k.scalar_step, 1)

        with stage(k) as block:
            @block.gpsimd
            def _(pool):
                k.nc.gpsimd.memset(qT[:, :, :, :], 0.0).then_inc(k.ready, 1)
                k.nc.gpsimd.memset(att[:, :, :], 0.0).then_inc(k.ready, 1)

            @block.tensor
            def _(pe):
                for a in range(H):
                    k.nc.tensor.transpose(k.psum[:, 0, a * P:(a + 1) * P], qi[:, a * P:(a + 1) * P], k.ident[:, :])
                    last = k.nc.tensor.transpose(k.psum[:, 1, a * P:(a + 1) * P], ki[:, a * P:(a + 1) * P], k.ident[:, :])
                last.then_inc(k.products, 1)
                if o is not None:
                    pe.wait_ge(k.vector_step, 3)
                    for a in range(H):
                        for c in range(2):
                            last = matmul(k, k.psum[:, 2, a * P:(a + 1) * P], kT[:, a, :], qT[:, c, a, :], c == 0, c == 1)
                    last.then_inc(k.products, 1)
                for n, c in enumerate(order):
                    lo = c * GLA_CHUNK
                    for a in range(H):
                        last = matmul(k, k.psum[:, 6 + a // 2, (a % 2) * DV:(a % 2 + 1) * DV],
                                      ke[lo:lo + GLA_CHUNK, a * P:(a + 1) * P], v[lo:lo + GLA_CHUNK, a * DV:(a + 1) * DV], True, True)
                    last.then_inc(k.updates, 1)
                    if o is not None:
                        if n == 0:
                            pe.wait_ge(k.vector_step, 4)
                        for a in range(H):
                            to = k.psum[:, 3 + a // 2, (a % 2) * DV:(a % 2 + 1) * DV] if n == 0 else k.psum[:, (0, 1)[a // 2], (a % 2) * DV:(a % 2 + 1) * DV]
                            if n == 0:
                                matmul(k, to, att[:, a, :], v[:, a * DV:(a + 1) * DV], True, False)
                            last = matmul(k, to, qT[:, c, a, :], state[:, a, :], n == 1, True)
                        last.then_inc(k.outputs, 1)
                    else:
                        pe.drain().then_inc(k.outputs, 1)
                    if n == 0:
                        pe.wait_ge(k.states, 1)

            @block.vector
            def _(dve):
                step = Chain(dve, k.vector_step)
                dve.wait_ge(k.ready, 2)
                dve.wait_ge(k.products, 1)
                turned = k.psum[:, 0, :].rearrange("p (a t) -> p a t", a=H)
                for c in range(2):
                    lo = c * GLA_CHUNK
                    step.done(V.tensor_copy(qT[:, c, :, lo:lo + GLA_CHUNK], turned[:, :, lo:lo + GLA_CHUNK]))
                step.done(V.tensor_copy(kT[:, :, :].rearrange("p a t -> p (a t)"), k.psum[:, 1, :]))
                if o is not None:
                    dve.wait_ge(k.products, 2)
                    for a in range(H):
                        last = V.copy_predicated(att[:, a, :], mask.bitcast(U32), k.psum[:, 2, a * P:(a + 1) * P])
                    step.done(last)
                for n, c in enumerate(order):
                    dve.wait_ge(k.updates, n + 1)
                    dve.wait_ge(k.outputs, n + 1)
                    for a in range(H):
                        last = V.scalar_tensor_tensor(state[:, a, :], state[:, a, :], decay[:, a, c:c + 1],
                                                      k.psum[:, 6 + a // 2, (a % 2) * DV:(a % 2 + 1) * DV], ALU.mult, ALU.add)
                    last.then_inc(k.states, 1)
                if o is not None:
                    for part in ((3, 4), (0, 1)):
                        for half in range(2):
                            to = o[:, half * NC:(half + 1) * NC]
                            step.done(V.tensor_tensor(to, to, k.psum[:, part[half], :], ALU.add))


def gla_mixer(k, h, mix):
    with buffers(k, z=[P, 4, 3 * D], o=[P, 2, D], g=[P, 4, 2, GLA_QK]) as (z, o, g):
        with buffers(k, hT=[P, DB, 4 * P]) as hT:
            turn(k, [(h, hT)], 4)
            project(k, hT, k.given["b_w_in"][0][:, 0:3 * D], z, 4)
            gla_gates(k, hT, g)
        with buffers(k, prefix=[P, P], suffix=[P, P], same=[P, P], member=[P, 2], state=[P, 2, GLA_HEADS, GLA_DV]) as \
                (prefix, suffix, same, member, state):
            load(k, [(prefix[:, :], k.given["chunk_prefix"]), (suffix[:, :], k.given["chunk_suffix"]), (same[:, :], k.given["chunk_same"]),
                     (member[:, :], k.given["chunk_member"])])
            m = Kit()
            m.prefix, m.suffix, m.same, m.member = prefix[:, :], suffix[:, :], same[:, :], member[:, :]

            def clear(dve, step):
                k.nc.vector.memset(state[:, :, :, :], 0.0)
                step.done(k.nc.vector.memset(o[:, :, :], 0.0))
            on_vector(k, clear)
            for direction, tiles in ((0, (2, 3, 0, 1)), (1, (3, 2, 1, 0))):
                for t in tiles:
                    gla_tile(k, m, z[:, t, 0:GLA_QK], z[:, t, GLA_QK:2 * GLA_QK], z[:, t, D:2 * D],
                             g[:, t, direction, :], direction == 1, state[:, direction, :, :], o[:, t, :] if t < 2 else None)
        normalize(k, [o[:, t, a * GLA_DV:(a + 1) * GLA_DV] for t in range(2) for a in range(GLA_HEADS)], LN_EPS)
        activate(k, [(z[:, t, 2 * D:3 * D], z[:, t, 2 * D:3 * D], ACT.Silu) for t in range(2)])
        with buffers(k, gain=[P, D], yT=[P, DB, 2 * P]) as (gain, yT):
            load(k, [(gain[:, :], k.given["b_gn_g"][0].partition_broadcast(P))])

            def gate(dve, step):
                for t in range(2):
                    step.done(k.nc.vector.tensor_tensor(o[:, t, :], o[:, t, :], gain[:, :], ALU.mult))
                    step.done(k.nc.vector.tensor_tensor(o[:, t, :], o[:, t, :], z[:, t, 2 * D:3 * D], ALU.mult))
            on_vector(k, gate)
            turn(k, [(o, yT)], 2)
            project(k, yT, k.given["b_w_out"][0], mix, 2)


def rms_rows(k, x, h, g):
    def copy(dve, step):
        step.done(k.nc.vector.tensor_copy(h[:, :, :], x[:, 0:2, :]))
    on_vector(k, copy)
    normalize(k, [h[:, t, :] for t in range(2)], RMS_EPS, centred=False)
    with buffers(k, gain=[P, D]) as gain:
        load(k, [(gain[:, :], g.partition_broadcast(P))])
        affine_rows(k, [h[:, t, :] for t in range(2)], gain[:, :], None)


def mlstm_gates(k, hT, layer, li, b, c):
    at = 4 * D
    with buffers(k, w=[P, DB, 2 * HEADS], bias=[P, 2 * HEADS], f=[P, 2, HEADS], spare=[P, 2, HEADS]) as (w, bias, f, spare):
        load(k, [(w[:, :, :], k.given["w_in_2"][layer][:, at:at + 2 * HEADS].rearrange("(b p) n -> p b n", p=P)),
                 (bias[:, :], k.given["b_in_2"][layer][at:at + 2 * HEADS].partition_broadcast(P))])
        with stage(k) as block:
            @block.tensor
            def _(pe):
                for t in range(2):
                    for d in range(DB):
                        mm = matmul(k, k.psum[:, t, 0:2 * HEADS], hT[:, d, t * P:(t + 1) * P], w[:, d, :], d == 0, d == DB - 1)
                    mm.then_inc(k.products, 1)

            @block.vector
            def _(dve):
                dve.wait_ge(k.products, 2)
                for t in range(2):
                    k.nc.vector.tensor_tensor(li[:, t, :], k.psum[:, t, 0:HEADS], bias[:, 0:HEADS], ALU.add)
                    last = k.nc.vector.tensor_tensor(f[:, t, :], k.psum[:, t, HEADS:2 * HEADS], bias[:, HEADS:2 * HEADS], ALU.add)
                last.then_inc(k.vector_step, 1)
        log_sigmoid(k, f[:, :, :].rearrange("p t a -> p (t a)"), spare[:, :, :].rearrange("p t a -> p (t a)"), 1.0)
        with stage(k) as block:
            @block.tensor
            def _(pe):
                matmul(k, k.psum[:, 0, 0:HEADS], k.causal[:, :], f[:, 0, :], True, True)
                matmul(k, k.psum[:, 1, 0:HEADS], k.ones[:, :], f[:, 0, :], True, False)
                matmul(k, k.psum[:, 1, 0:HEADS], k.causal[:, :], f[:, 1, :], False, True).then_inc(k.products, 1)

            @block.vector
            def _(dve):
                step = Chain(dve, k.vector_step)
                dve.wait_ge(k.products, 1)
                for t in range(2):
                    last = k.nc.vector.tensor_copy(b[:, t, :], k.psum[:, t, 0:HEADS])
                step.done(last)
                step.done(k.nc.vector.tensor_tensor(c[:, :, :], li[:, :, :], b[:, :, :], ALU.subtract))


def mlstm(k, hT, layer, y):
    H = HEADS
    V = k.nc.vector
    with buffers(k, kT=[P, 2 * H, SEQ], qT=[P, 2 * H, SEQ], v=[P, 2, 2 * D]) as (kT, qT, v):
        stride = SEQ + CONV_K - 1
        with buffers(k, raw=[P, 16 * stride], bias=[P, 16], taps=[P, CONV_K, 16], tap_bias=[P, 16]) as \
                (raw, bias, taps, tap_bias):
            load(k, [(bias[:, :], k.given["b_qk_cols"][layer]), (taps[:, :, :], k.given["conv_w_cols"][layer]),
                     (tap_bias[:, :], k.given["conv_b_cols"][layer])])

            def pad(dve, step):
                step.done(V.memset(raw[:, :].rearrange("p (b t) -> p b t", b=16)[:, :, 0:CONV_K - 1], 0.0))
            on_vector(k, pad)
            project_channels(k, hT, k.given["w_in_2"][layer][:, 0:2 * D], raw, SEQ, stride, CONV_K - 1, bias)

            def convolve(dve, step):
                for j in range(CONV_K):
                    for n in range(16):
                        to = (qT if n < 8 else kT)[:, n % 8, :]
                        x = raw[:, n * stride + j:n * stride + j + SEQ]
                        if j == 0:
                            last = V.tensor_scalar(to, x, taps[:, j, n:n + 1], tap_bias[:, n:n + 1], ALU.mult, ALU.add)
                        else:
                            last = V.scalar_tensor_tensor(to, x, taps[:, j, n:n + 1], to, ALU.mult, ALU.add)
                    step.done(last)
            on_vector(k, convolve)
        activate(k, [(x[:, :, :], x[:, :, :], ACT.Silu) for x in (qT, kT)])
        project(k, hT, k.given["w_in_2"][layer][:, 2 * D:4 * D], v, 2, bias=k.given["b_in_2"][layer][2 * D:4 * D])
        with buffers(k, li=[P, 2, H], b=[P, 2, H], c=[P, 2, H]) as (li, b, c):
            mlstm_gates(k, hT, layer, li, b, c)

            def scale(dve, step):
                step.done(V.tensor_scalar(qT[:, :, :], qT[:, :, :], DK ** -0.5, None, ALU.mult))
            on_vector(k, scale)
            for a in range(H):
                mlstm_head(k, a, qT, kT, v, b, c, y)
        normalize(k, [y[:, t, a * M_DV:(a + 1) * M_DV] for t in range(2) for a in range(H)], RMS_EPS)
        activate(k, [(v[:, :, D:2 * D], v[:, :, D:2 * D], ACT.Sigmoid)])
        gate_rows(k, y, v[:, :, D:2 * D], k.given["m_norm_g_2"][layer], D)


def gate_rows(k, y, gate, gain_row, width):
    with buffers(k, gain=[P, width]) as gain:
        load(k, [(gain[:, :], gain_row.partition_broadcast(P))])

        def body(dve, step):
            for t in range(2):
                step.done(k.nc.vector.tensor_tensor(y[:, t, :], y[:, t, :], gain[:, :], ALU.mult))
                step.done(k.nc.vector.tensor_tensor(y[:, t, :], y[:, t, :], gate[:, t, :], ALU.mult))
        on_vector(k, body)


BLOCKS = ((0, 0), (1, 0), (1, 1))


def mlstm_head(k, a, qT, kT, v, b, c, y):
    V = k.nc.vector
    with buffers(k, diag=[P, 2, P], logs=[P, 3, P], probs=[P, 3, P], weighed=[P, 3, P], turned=[P, 3, P],
                 top=[P, 4], den=[P, 2], least=[P, 2], inverse=[P, 2]) as \
            (diag, logs, probs, weighed, turned, top, den, least, inverse), stage(k) as block:
        span = (slice(0, 1), slice(1, 3))

        @block.tensor
        def _(pe):
            for n, (t, s) in enumerate(BLOCKS):
                for d in range(2):
                    mm = matmul(k, k.psum[:, 1, n * P:(n + 1) * P], qT[:, 2 * a + d, t * P:(t + 1) * P],
                                kT[:, 2 * a + d, s * P:(s + 1) * P], d == 0, d == 1)
            mm.then_inc(k.scores, 1)
            pe.wait_ge(k.vector_step, 1)
            for s in range(2):
                mm = matmul(k, k.psum[:, 0, s * P:(s + 1) * P], k.ones[:, :], diag[:, s, :], True, True)
            mm.then_inc(k.products, 1)
            pe.wait_ge(k.weighed, 1)
            for n in range(3):
                last = k.nc.tensor.transpose(k.psum[:, 2, n * P:(n + 1) * P], weighed[:, n, :], k.ident[:, :])
            last.then_inc(k.products, 1)
            pe.wait_ge(k.weighed, 2)
            for n, (t, s) in enumerate(BLOCKS):
                mm = matmul(k, k.psum[:, 3 + t, 0:M_DV], turned[:, n, :], v[:, s, a * M_DV:(a + 1) * M_DV], s == 0, s == t)
            mm.then_inc(k.products, 1)

        @block.vector
        def _(dve):
            step = Chain(dve, k.vector_step)
            for s in range(2):
                last = V.tensor_scalar(diag[:, s, :], k.ident[:, :], c[:, s, a:a + 1], None, ALU.mult)
            step.done(last)
            dve.wait_ge(k.products, 1)
            for n, (t, s) in enumerate(BLOCKS):
                row = k.psum[:, 0, s * P:(s + 1) * P]
                if s < t:
                    last = V.tensor_scalar(logs[:, n, :], row, b[:, t, a:a + 1], None, ALU.add)
                else:
                    last = V.scalar_tensor_tensor(logs[:, n, :], row, b[:, t, a:a + 1], k.future[:, :], ALU.add, ALU.add)
            step.done(last)
            for t in range(2):
                last = V.tensor_reduce(top[:, t:t + 1], logs[:, span[t], :].rearrange("p n s -> p (n s)"), AX_X, ALU.max)
            step.done(last)
            step.done(V.tensor_tensor(top[:, 0:2], top[:, 0:2], b[:, :, a], ALU.max))
            V.tensor_scalar(top[:, 2:4], top[:, 0:2], -1.0, None, ALU.mult).then_inc(k.ready, 1)
            dve.wait_ge(k.scalar_step, 3)
            dve.wait_ge(k.scores, 1)
            for t in range(2):
                last = V.tensor_tensor_reduce(weighed[:, span[t], :].rearrange("p n s -> p (n s)"),
                                              probs[:, span[t], :].rearrange("p n s -> p (n s)"),
                                              k.psum[:, 1, span[t].start * P:span[t].stop * P], 1.0, 0.0,
                                              ALU.mult, ALU.add, den[:, t:t + 1])
            last.then_inc(k.weighed, 1)
            dve.wait_ge(k.products, 2)
            V.tensor_copy(turned[:, :, :].rearrange("p n s -> p (n s)"), k.psum[:, 2, 0:3 * P]).then_inc(k.weighed, 1)
            dve.wait_ge(k.weighed, 2)
            step.done(V.scalar_tensor_tensor(den[:, :], den[:, :], -1.0, den[:, :], ALU.mult, ALU.max))
            step.done(V.tensor_tensor(den[:, :], den[:, :], least[:, :], ALU.max))
            step.done(V.reciprocal(inverse[:, :], den[:, :]))
            dve.wait_ge(k.products, 3)
            for t in range(2):
                last = V.tensor_scalar(y[:, t, a * M_DV:(a + 1) * M_DV], k.psum[:, 3 + t, 0:M_DV], inverse[:, t:t + 1], None, ALU.mult)
            step.done(last)

        @block.scalar
        def _(act):
            act.wait_ge(k.ready, 1)
            for t in range(2):
                k.nc.scalar.activation(probs[:, span[t], :].rearrange("p n s -> p (n s)"),
                                       logs[:, span[t], :].rearrange("p n s -> p (n s)"), ACT.Exp,
                                       bias=top[:, 2 + t:3 + t]).then_inc(k.scalar_step, 1)
            k.nc.scalar.activation(least[:, :], top[:, 2:4], ACT.Exp).then_inc(k.scalar_step, 1)


def retention(k, hT, layer, y):
    H = HEADS
    V = k.nc.vector
    at = 4 * D + 2 * H
    with buffers(k, v=[P, 2, 2 * D]) as v:
        with buffers(k, raw=[P, 16 * SEQ]) as raw:
            with buffers(k, bias=[P, 16]) as bias:
                load(k, [(bias[:, :], k.given["b_r_cols"][layer])])
                project_channels(k, hT, k.given["w_in_2"][layer][:, at:at + 2 * D], raw, SEQ, SEQ, 0, bias)
            with buffers(k, cos=[P, SEQ], sin=[P, SEQ], a1=[P, 8, SEQ], a2=[P, 8, SEQ]) as (cos, sin, a1, a2):
                load(k, [(cos[:, :], k.given["rope_cos"]), (sin[:, :], k.given["rope_sin"])])

                def rope(dve, step):
                    pairs = raw[:, :].rearrange("p (n h t) -> p n h t", n=8, h=2)
                    x1, x2 = pairs[:, :, 0, :], pairs[:, :, 1, :]
                    wide_cos = cos[:, :].unsqueeze(1).to_broadcast([P, 8, SEQ])
                    wide_sin = sin[:, :].unsqueeze(1).to_broadcast([P, 8, SEQ])
                    V.tensor_tensor(a1[:, :, :], x1, wide_sin, ALU.mult)
                    step.done(V.tensor_tensor(a2[:, :, :], x2, wide_sin, ALU.mult))
                    V.tensor_tensor(x1, x1, wide_cos, ALU.mult)
                    step.done(V.tensor_tensor(x2, x2, wide_cos, ALU.mult))
                    V.tensor_tensor(x1, x1, a2[:, :, :], ALU.subtract)
                    step.done(V.tensor_tensor(x2, x2, a1[:, :, :], ALU.add))
                on_vector(k, rope)
            project(k, hT, k.given["w_in_2"][layer][:, at + 2 * D:at + 4 * D], v, 2, bias=k.given["b_in_2"][layer][at + 2 * D:at + 4 * D])
            with buffers(k, decay=[P, H, 2, SEQ], weighed=[P, H, 2, SEQ]) as (decay, weighed):
                load(k, [(decay[:, :, :, :], k.given["decay"])])
                with stage(k) as block:
                    lo = (0, P)

                    def values(pe, a):
                        pe.wait_ge(k.weighed, a + 1)
                        for t in range(2):
                            for s in range(t + 1):
                                mm = matmul(k, k.psum[:, 4 + 2 * (a % 2) + t, :], weighed[:, a, s, t * P:(t + 1) * P],
                                            v[:, s, a * R_DV:(a + 1) * R_DV], s == 0, s == t)
                        mm.then_inc(k.products, 1)

                    @block.tensor
                    def _(pe):
                        for a in range(H):
                            for s in range(2):
                                for d in range(2):
                                    q = raw[:, (2 * a + d) * SEQ + lo[s]:(2 * a + d + 1) * SEQ]
                                    kk = raw[:, (8 + 2 * a + d) * SEQ + s * P:(8 + 2 * a + d) * SEQ + (s + 1) * P]
                                    mm = matmul(k, k.psum[:, 2 * (a % 2) + s, lo[s]:SEQ], kk, q, d == 0, d == 1)
                            mm.then_inc(k.scores, 1)
                            if a >= 1:
                                values(pe, a - 1)
                        values(pe, H - 1)

                    @block.vector
                    def _(dve):
                        for a in range(H + 1):
                            if a < H:
                                dve.wait_ge(k.scores, a + 1)
                                for s in range(2):
                                    last = V.tensor_tensor(weighed[:, a, s, lo[s]:], k.psum[:, 2 * (a % 2) + s, lo[s]:SEQ],
                                                           decay[:, a, s, lo[s]:], ALU.mult)
                                last.then_inc(k.weighed, 1)
                            if a >= 1:
                                dve.wait_ge(k.products, a)
                                for t in range(2):
                                    last = V.tensor_copy(y[:, t, (a - 1) * R_DV:a * R_DV], k.psum[:, 4 + 2 * ((a - 1) % 2) + t, :])
                                last.then_inc(k.vector_step, 1)
        normalize(k, [y[:, t, a * R_DV:(a + 1) * R_DV] for t in range(2) for a in range(H)], RMS_EPS)
        project(k, hT, k.given["w_in_2"][layer][:, at + 4 * D:at + 6 * D], v, 2, bias=k.given["b_in_2"][layer][at + 4 * D:at + 6 * D])
        activate(k, [(v[:, :, :], v[:, :, :], ACT.Silu)])
        gate_rows(k, y, v, k.given["r_norm_g_2"][layer], 2 * D)


def add_to(k, x, y):
    def body(dve, step):
        step.done(k.nc.vector.tensor_tensor(x[:, 0:2, :], x[:, 0:2, :], y[:, :, :], ALU.add))
    on_vector(k, body)


def second_layer(k, x, layer):
    at = 4 * D + 2 * HEADS + 6 * D
    with buffers(k, h=[P, 2, D], hT=[P, DB, SEQ]) as (h, hT):
        rms_rows(k, x, h, k.given["norm1_g_2"][layer])
        turn(k, [(h, hT)], 2)
        with buffers(k, merged=[P, 2, D]) as merged:
            mlstm(k, hT, layer, h)
            with buffers(k, gate=[P, 2, 2 * D], yT=[P, 2 * DB, SEQ], part=[P, 2, D]) as (gate, yT, part):
                project(k, hT, k.given["w_in_2"][layer][:, at:at + 2 * D], gate, 2, bias=k.given["b_in_2"][layer][at:at + 2 * D])
                activate(k, [(gate[:, :, :], gate[:, :, :], ACT.Sigmoid)])
                turn(k, [(h, yT[:, 0:DB, :])], 2)
                project(k, yT, k.given["w_bm_2"][layer], part, 2)

                def gated(dve, step):
                    step.done(k.nc.vector.tensor_tensor(merged[:, :, :], part[:, :, :], gate[:, :, 0:D], ALU.mult))
                on_vector(k, gated)
                with buffers(k, y=[P, 2, 2 * D]) as y:
                    retention(k, hT, layer, y)
                    turn(k, [(y, yT)], 2)
                project(k, yT, k.given["w_br_2"][layer], part, 2)

                def gated_too(dve, step):
                    step.done(k.nc.vector.tensor_tensor(part[:, :, :], part[:, :, :], gate[:, :, D:2 * D], ALU.mult))
                    step.done(k.nc.vector.tensor_tensor(merged[:, :, :], merged[:, :, :], part[:, :, :], ALU.add))
                on_vector(k, gated_too)
                turn(k, [(merged, yT[:, 0:DB, :])], 2)
                project(k, yT, k.given["w_out_2"][layer], part, 2)
                add_to(k, x, part)
        rms_rows(k, x, h, k.given["norm2_g_2"][layer])
        turn(k, [(h, hT)], 2)
        with buffers(k, f=[P, D_FF // P * SEQ], bias=[P, D_FF // P]) as (f, bias):
            load(k, [(bias[:, :], k.given["b_ff1_cols"][layer])])
            project_channels(k, hT, k.given["w_ff1_2"][layer], f, SEQ, SEQ, 0, bias, relu=True)
            activate(k, [(f[:, :], f[:, :], ACT.Square)])
            project(k, f[:, :].rearrange("p (b t) -> p b t", t=SEQ), k.given["w_ff2_2"][layer], h, 2, bias=k.given["b_ff2_2"][layer])
        add_to(k, x, h)
        rms_rows(k, x, h, k.given["norm3_g_2"][layer])
        turn(k, [(h, hT)], 2)
        with buffers(k, gate=[P, 2, D], pT=[P, 2, SEQ], w=[P, 2, D]) as (gate, pT, w):
            project(k, hT, k.given["w_pe_gate_2"][layer], gate, 2)
            activate(k, [(gate[:, :, :], gate[:, :, :], ACT.Sigmoid)])
            load(k, [(pT[:, :, :], k.given["p_t"][layer].rearrange("(b p) t -> p b t", p=P)),
                     (w[:, :, :], k.given["w_pe_2"][layer].rearrange("(b p) n -> p b n", p=P))])
            with stage(k) as block:
                @block.tensor
                def _(pe):
                    for t in range(2):
                        for n in range(2):
                            for b in range(2):
                                mm = matmul(k, k.psum[:, 2 * t + n, :], pT[:, b, t * P:(t + 1) * P],
                                            w[:, b, n * NC:(n + 1) * NC], b == 0, b == 1)
                    mm.then_inc(k.products, 1)

                @block.vector
                def _(dve):
                    dve.wait_ge(k.products, 1)
                    for t in range(2):
                        for n in range(2):
                            to = gate[:, t, n * NC:(n + 1) * NC]
                            last = k.nc.vector.tensor_tensor(to, to, k.psum[:, 2 * t + n, :], ALU.mult)
                    last.then_inc(k.vector_step, 1)
            add_to(k, x, gate)


def first_layer(k, x, layer, h, mix):
    streams = 1 if layer == DEPTH - 1 else 2
    modulated(k, x, h, 2, layer, 1, 0)
    if layer == 0:
        chunk_mlp(k, h, mix)
    else:
        gla_mixer(k, h, mix)
    residual_norm(k, x, mix, streams, layer, 2, 0)
    modulated(k, x, h, streams, layer, 4, 3)
    peer(k, h, mix, 2 * streams, layer)
    residual_norm(k, x, mix, streams, layer, 5, 1)


def program(nc, given, out):
    with ExitStack() as ctx:
        k = Kit()
        k.nc, k.given, k.made = nc, given, 0

        def sem(name):
            return ctx.enter_context(nc.semaphore(name))

        k.u_loaded = [sem(f"u_loaded{n}") for n in range(RING)]
        k.v_loaded = [sem(f"v_loaded{n}") for n in range(RING)]
        k.groups_gathered = 0
        k.loaded = [sem("loaded0"), sem("loaded1")]
        k.bias_loaded = [sem("bias_loaded0"), sem("bias_loaded1")]
        k.copied = [sem("copied0"), sem("copied1")]
        k.chunks_used = sem("chunks_used")
        k.psum_free = sem("psum_free")
        k.products = sem("products")
        k.vector_step = sem("vector_step")
        k.scalar_step = sem("scalar_step")
        k.ready = sem("ready")
        k.stored = sem("stored")
        k.started = sem("started")
        k.places_set = sem("places_set")
        k.u_used = sem("u_used")
        k.v_used = sem("v_used")
        k.exp_asked = sem("exp_asked")
        k.updates = sem("updates")
        k.outputs = sem("outputs")
        k.states = sem("states")
        k.scores = sem("scores")
        k.granted = sem("granted")
        k.weighed = sem("weighed")
        first = k.loaded[0].num
        k.stage_sems = range(first, k.weighed.num + 1)
        k.psum = ctx.enter_context(nc.psum_tensor("psum", [P, 8, NC], F32))
        k.modulation = nc.dram_tensor("modulation", (2, DEPTH * 6 * D), F32).ap()
        with buffers(k, ident=[P, P], ones=[P, P], causal=[P, P], future=[P, P], x=[P, 4, D]) as \
                (k.ident, k.ones, k.causal, k.future, x):
            load(k, [(k.ident[:, :], given["ident"]), (k.ones[:, :], given["ones"]), (k.causal[:, :], given["causal"]), (k.future[:, :], given["future"]),
                     (x[:, 0:2, :], given["x"].rearrange("o (t p) d -> p (o t) d", p=P)),
                     (x[:, 2:4, :], given["ctx"].rearrange("o (t p) d -> p (o t) d", p=P))])
            modulation_rows(k)
            for layer in range(DEPTH):
                with buffers(k, h=[P, 4, D], mix=[P, 4, D]) as (h, mix):
                    first_layer(k, x, layer, h, mix)
            with nc.Fori(0, DEPTH) as layer:
                second_layer(k, x, layer)
            with buffers(k, h=[P, 2, D]) as h:
                rms_rows(k, x, h, given["final_g_2"])
                store(k, out, h)


def store(k, out, y):
    with stage(k) as block:
        @block.sync
        def _(sp):
            sp.dma_start(out.rearrange("o (t p) d -> p (o t) d", p=P), y[:, 0:2, :]).then_inc(k.stored, 16)
            sp.wait_ge(k.stored, 16)


def constants():
    f = np.float32
    r = np.arange(P)
    chunk = r // GLA_CHUNK
    same = chunk[:, None] == chunk[None, :]
    pos = np.arange(SEQ, dtype=f)
    inv_freq = (f(10000.0) ** (-np.arange(0, DK, 2, dtype=f) / f(DK))).astype(f)
    ang = (pos[:, None] * inv_freq[None, :]).astype(f)
    log_gamma = np.log(f(1.0) - np.exp2(-f(5.0) - np.arange(HEADS, dtype=f))).astype(f)
    diff = pos[None, :] - pos[:, None]
    decay = np.where(diff >= 0, np.exp(np.maximum(diff, 0)[None] * log_gamma[:, None, None]) * f(DK ** -0.5), 0.0)
    return {
        "ident": np.eye(P, dtype=f),
        "ones": np.ones((P, P), f),
        "causal": (r[:, None] <= r[None, :]).astype(f),
        "future": np.where(r[None, :] <= r[:, None], 0.0, MASKED).astype(f),
        "chunk_prefix": (same & (r[:, None] <= r[None, :])).astype(f),
        "chunk_suffix": (same & (r[:, None] >= r[None, :])).astype(f),
        "chunk_same": same.astype(f),
        "chunk_member": (chunk[:, None] == np.arange(2)[None, :]).astype(f),
        "rope_cos": np.ascontiguousarray(np.cos(ang).T.astype(f)),
        "rope_sin": np.ascontiguousarray(np.sin(ang).T.astype(f)),
        "decay": np.ascontiguousarray(decay.astype(f).reshape(HEADS, 2, P, SEQ).transpose(2, 0, 1, 3)),
    }


_AS_THEY_ARE = ("x ctx w_mod b_mod ln_g ln_b a_w_in a_norm_g a_norm_b a_w_out b_w_in b_w_gate b_gate_bias b_gn_g b_w_out "
                "p_w_q norm1_g_2 w_in_2 b_in_2 m_norm_g_2 r_norm_g_2 w_bm_2 w_br_2 w_out_2 norm2_g_2 w_ff1_2 "
                "w_ff2_2 b_ff2_2 norm3_g_2 w_pe_gate_2 w_pe_2 final_g_2").split()


def kernel(**inputs):
    import concourse.bacc as bacc
    from concourse.bass_utils import run_bass_kernel_spmd

    a = {n: np.asarray(v) for n, v in inputs.items()}
    at = 4 * D + 2 * HEADS
    given = {n: a[n] for n in _AS_THEY_ARE}
    given["cond_cols"] = np.stack([a["c"].reshape(DB, P).T, a["c_ctx"].reshape(DB, P).T], axis=2)
    given["b_qk_cols"] = a["b_in_2"][:, 0:2 * D].reshape(DEPTH, 16, P).transpose(0, 2, 1)
    given["b_r_cols"] = a["b_in_2"][:, at:at + 2 * D].reshape(DEPTH, 16, P).transpose(0, 2, 1)
    given["b_ff1_cols"] = a["b_ff1_2"].reshape(DEPTH, D_FF // P, P).transpose(0, 2, 1)
    given["conv_w_cols"] = a["conv_w_2"].reshape(DEPTH, CONV_K, 16, P).transpose(0, 3, 1, 2)
    given["conv_b_cols"] = a["conv_b_2"].reshape(DEPTH, 16, P).transpose(0, 2, 1)
    given["a_w_s_t"] = a["a_w_s"][0].transpose(2, 0, 1)
    given["a_b_s_t"] = a["a_b_s"][0].T
    given["p_keys_t"] = a["p_keys"].transpose(0, 1, 3, 2)
    given["p_t"] = a["p_2"][:, 0].transpose(0, 2, 1)
    given["p_u"] = a["p_u"].reshape(DEPTH * PEER_EXPERTS, D)
    given["p_v"] = a["p_v"].reshape(DEPTH * PEER_EXPERTS, D)
    given.update(constants())
    given = {n: np.ascontiguousarray(v) for n, v in given.items()}

    nc = bacc.Bacc("TRN2", target_bir_lowering=False, num_devices=1)
    there = {n: nc.dram_tensor(f"in_{n}", v.shape, F32, kind="ExternalInput").ap() for n, v in given.items()}
    out = nc.dram_tensor("out_x", (1, SEQ, D), F32, kind="ExternalOutput").ap()
    program(nc, there, out)
    r = run_bass_kernel_spmd(nc, [{f"in_{n}": v for n, v in given.items()}], core_ids=[0])
    return r.results[0]["out_x"]
```

```python
from contextlib import ExitStack, contextmanager

import numpy as np

import concourse.bass as bass
from concourse import mybir

F32 = mybir.dt.float32
F32R = mybir.dt.float32r
U32 = mybir.dt.uint32
I32 = mybir.dt.int32
ALU = mybir.AluOpType
ACT = mybir.ActivationFunctionType
AX_X = mybir.AxisListType.X

P = 128
D = 1024
DB = D // P
SEQ = 256
DEPTH = 2
LN_EPS = 1e-5
RMS_EPS = 1e-6
DN_ALPHA = (2.0 * DEPTH) ** 0.25
NC = 512
KG = 4
WEIGHT_SLOTS = 4

A_HEADS = 8
GLA_HEADS, GLA_DK, GLA_DV, GLA_RANK, GLA_TAU, GLA_CHUNK = 4, 128, 256, 16, 16.0, 64
GLA_QK = GLA_HEADS * GLA_DK
PEER_HEADS, PEER_KEYS, PEER_TOPK = 8, 128, 16
PEER_EXPERTS = PEER_KEYS * PEER_KEYS
PICKS = PEER_HEADS * PEER_TOPK
U_RING, V_RING = 16, 8
LOWEST = -3.0e38
MASKED = -1.0e30
HEADS, DK, M_DV, R_DV, CONV_K = 4, 256, 256, 512, 4
D_FF = 4 * D


class Kit:
    pass


class Chain:

    def __init__(self, engine, sem, base=0):
        self.engine, self.sem, self.base, self.n = engine, sem, base, 0

    def done(self, instruction):
        self.n += 1
        instruction.then_inc(self.sem, 1)
        self.engine.wait_ge(self.sem, self.base + self.n)


@contextmanager
def stage(k):
    with k.nc.Block() as block:
        yield block
    k.nc.sync.sem_clear(k.stage_sems)
    k.nc.all_engine_barrier()


@contextmanager
def buffers(k, **shapes):
    with ExitStack() as ctx:
        made = []
        for name, shape in shapes.items():
            k.made += 1
            dt = F32
            if isinstance(shape, tuple):
                shape, dt = shape
            made.append(ctx.enter_context(k.nc.sbuf_tensor(f"{name}_{k.made}", shape, dt)))
        yield made if len(made) > 1 else made[0]


def load(k, pairs):
    with stage(k) as block:
        @block.sync
        def _(sp):
            mine = pairs[0::2]
            for dst, src in mine:
                sp.dma_start(dst, src).then_inc(k.loaded[0], 16)
            sp.wait_ge(k.loaded[0], 16 * len(mine))

        @block.scalar
        def _(act):
            mine = pairs[1::2]
            for dst, src in mine:
                act.dma_start(dst, src).then_inc(k.loaded[1], 16)
            if mine:
                act.wait_ge(k.loaded[1], 16 * len(mine))


def on_vector(k, body):
    with stage(k) as block:
        @block.vector
        def _(dve):
            body(dve, Chain(dve, k.vector_step))


def matmul(k, out, lhsT, rhs, first, last):
    return k.nc.tensor.matmul(out, lhsT, rhs, start=first, stop=last)


class Split:

    def __init__(self, high, low):
        self.high, self.low = high, low

    def part(self, *index):
        return Split(self.high[index], self.low[index])


@contextmanager
def split_buffers(k, name, shape):
    with buffers(k, **{name + "_high": (shape, F32R), name + "_low": (shape, F32R)}) as (high, low):
        yield Split(high, low)


def split_matmul(k, out, lhsT, rhs, first, last):
    matmul(k, out, lhsT.high, rhs.high, first, False)
    matmul(k, out, lhsT.high, rhs.low, False, False)
    return matmul(k, out, lhsT.low, rhs.high, False, last)


@contextmanager
def weight_rings(k):
    with buffers(k, landing=[P, WEIGHT_SLOTS, KG, NC]) as k.landing, \
            split_buffers(k, "weights", [P, 2, KG, NC]) as k.weights:
        k.prefetched = False
        yield


def load_chunk(k, engine, w, i, j):
    groups = w.shape[0] // (KG * P)
    s, g = j // groups, j % groups
    engine.dma_start(k.landing[:, j % WEIGHT_SLOTS], w[g * KG * P:(g + 1) * KG * P, bass.ds(i * (2 * NC) + s * NC, NC)]
                     .rearrange("(b p) n -> p b n", p=P)).then_inc(k.weights_landed[j % WEIGHT_SLOTS], 16)


def prefetch(k, w):
    for j in range(WEIGHT_SLOTS):
        load_chunk(k, k.nc.sync, w, 0, j)
    k.prefetched = True


def projection(k, w, products, empty, bias=None, bias_row=None):
    groups = w.shape[0] // (KG * P)
    L = 2 * groups
    pairs = w.shape[1] // (2 * NC)
    if not k.prefetched:
        prefetch(k, w)
    k.prefetched = False

    def is_first(i):
        return isinstance(i, int) and i == 0

    def rounds(engine, run):
        run(0)
        if pairs > 1:
            with engine.Fori(1, pairs) as i:
                run(i)

    with stage(k) as block:
        @block.sync
        def _(sp):
            def run(i):
                for j in range(L):
                    if not is_first(i) or j >= WEIGHT_SLOTS:
                        sp.wait_ge(k.low_set, i * L + (j + 1 - WEIGHT_SLOTS))
                        load_chunk(k, sp, w, i, j)
            rounds(sp, run)

        @block.scalar
        def _(act):
            def run(i):
                for j in range(L):
                    if bias is not None and j % groups == 0:
                        s = j // groups
                        act.wait_ge(k.psum_free, i * 2 + (s + 1))
                        act.dma_start(bias_row[:, s, :], bias[bass.ds(i * (2 * NC) + s * NC, NC)].partition_broadcast(P))\
                           .then_inc(k.bias_loaded[s], 16)
                    act.wait_ge(k.weights_landed[j % WEIGHT_SLOTS], i * (16 * L // WEIGHT_SLOTS) + 16 * (j // WEIGHT_SLOTS + 1))
                    act.wait_ge(k.chunks_used, i * L + (j + 1))
                    k.nc.scalar.copy(k.weights.high[:, j % 2], k.landing[:, j % WEIGHT_SLOTS]).then_inc(k.high_set, 1)
            rounds(act, run)

        @block.tensor
        def _(pe):
            pe.sem_inc(k.chunks_used, 2)

            def run(i):
                for j in range(L):
                    s, g = j // groups, j % groups
                    if g == 0:
                        pe.wait_ge(k.psum_free, i * 2 + (s + 1))
                    pe.wait_ge(k.low_set, i * L + (j + 1))
                    products(s, g, k.weights.part(slice(None), j % 2), g == groups - 1).then_inc(k.chunks_used, 1)
            rounds(pe, run)

        @block.vector
        def _(dve):
            dve.sem_inc(k.psum_free, 2)

            def take(i, s):
                dve.wait_ge(k.chunks_used, i * L + (2 + groups * (s + 1)))
                if bias is not None:
                    dve.wait_ge(k.bias_loaded[s], i * 16 + 16)
                empty(i, s).then_inc(k.psum_free, 1)

            def run(i):
                for j in range(L):
                    dve.wait_ge(k.high_set, i * L + (j + 1))
                    k.nc.vector.tensor_tensor(k.weights.low[:, j % 2], k.landing[:, j % WEIGHT_SLOTS],
                                              k.weights.high[:, j % 2].bitcast(F32), ALU.subtract).then_inc(k.low_set, 1)
                    if j == groups:
                        take(i, 0)
                    elif j == 0 and not is_first(i):
                        take(i - 1, 1)
            rounds(dve, run)
            take(pairs - 1, 1)
    k.nc.sync.sem_clear(k.landed_sems)
    k.nc.all_engine_barrier()


def project(k, xT, w, out, tiles, bias=None):
    with buffers(k, bias_row=[P, 2, NC]) as bias_row:
        def products(s, g, weights, last):
            for t in range(tiles):
                for b in range(KG):
                    mm = split_matmul(k, k.psum[:, s * 4 + t, :], xT.part(slice(None), g * KG + b, slice(t * P, (t + 1) * P)),
                                      weights.part(slice(None), b), g == 0 and b == 0, last and b == KG - 1)
            return mm

        def empty(i, s):
            for t in range(tiles):
                to = out[:, t, bass.ds(i * (2 * NC) + s * NC, NC)]
                if bias is None:
                    last = k.nc.vector.tensor_copy(to, k.psum[:, s * 4 + t, :])
                else:
                    last = k.nc.vector.tensor_tensor(to, k.psum[:, s * 4 + t, :], bias_row[:, s, :], ALU.add)
            return last
        projection(k, w, products, empty, bias, bias_row)


def project_channels(k, xT, w, out, tokens, stride, offset=0, bias=None, relu=False):
    blocks = NC // P

    def products(s, g, weights, last):
        for m in range(blocks):
            for b in range(KG):
                mm = split_matmul(k, k.psum[:, s * 4 + m, 0:tokens], weights.part(slice(None), b, slice(m * P, (m + 1) * P)),
                                  xT.part(slice(None), g * KG + b, slice(0, tokens)), g == 0 and b == 0,
                                  last and b == KG - 1)
        return mm

    def empty(i, s):
        for m in range(blocks):
            at = i * (2 * blocks) + (s * blocks + m)
            to = out[:, bass.ds(i * (2 * blocks * stride) + ((s * blocks + m) * stride + offset), tokens)]
            if bias is None:
                last = k.nc.vector.tensor_copy(to, k.psum[:, s * 4 + m, 0:tokens])
            else:
                last = k.nc.vector.tensor_scalar(to, k.psum[:, s * 4 + m, 0:tokens], bias[:, bass.ds(at, 1)],
                                                 0.0 if relu else None, ALU.add, ALU.max if relu else ALU.bypass)
        return last
    projection(k, w, products, empty)


def turn(k, x, xT, tiles):
    jobs = [(t, q) for t in range(tiles) for q in range(xT.high.shape[1] // 4)]

    def target(part, t, q):
        return part[:, 4 * q:4 * q + 4, t * P:(t + 1) * P]

    with stage(k) as block:
        @block.tensor
        def _(pe):
            for n, (t, q) in enumerate(jobs):
                if n >= 8:
                    pe.wait_ge(k.low_set, n - 7)
                for b in range(4):
                    last = k.nc.tensor.transpose(k.psum[:, n % 8, b * P:(b + 1) * P],
                                                 x[:, t, (4 * q + b) * P:(4 * q + b + 1) * P], k.ident[:, :])
                last.then_inc(k.products, 1)

        @block.scalar
        def _(act):
            for n, (t, q) in enumerate(jobs):
                act.wait_ge(k.products, n + 1)
                k.nc.scalar.copy(target(xT.high, t, q), k.psum[:, n % 8, :].rearrange("p (b t) -> p b t", b=4))\
                    .then_inc(k.high_set, 1)

        @block.vector
        def _(dve):
            for n, (t, q) in enumerate(jobs):
                dve.wait_ge(k.high_set, n + 1)
                k.nc.vector.tensor_tensor(target(xT.low, t, q), k.psum[:, n % 8, :].rearrange("p (b t) -> p b t", b=4),
                                          target(xT.high, t, q).bitcast(F32), ALU.subtract).then_inc(k.low_set, 1)


def split(k, x, out):
    with stage(k) as block:
        @block.scalar
        def _(act):
            k.nc.scalar.copy(out.high, x).then_inc(k.high_set, 1)

        @block.vector
        def _(dve):
            dve.wait_ge(k.high_set, 1)
            k.nc.vector.tensor_tensor(out.low, x, out.high.bitcast(F32), ALU.subtract).then_inc(k.low_set, 1)


def normalize(k, views, eps, centred=True):
    n = len(views)
    with buffers(k, stats=[P, n, 2, 6], moments=[P, n, 2], spread=[P, n], root=[P, n], inverse=[P, n]) as \
            (stats, moments, spread, root, inverse), stage(k) as block:
        @block.vector
        def _(dve):
            step = Chain(dve, k.vector_step)
            for i, x in enumerate(views):
                parts = -(-x.shape[-1] // NC)
                for h in range(parts):
                    last = k.nc.vector.bn_stats(stats[:, i, h, :], x[:, h * NC:min((h + 1) * NC, x.shape[-1])])
            step.done(last)
            for i, x in enumerate(views):
                parts = -(-x.shape[-1] // NC)
                last = k.nc.vector.bn_aggr(moments[:, i, :], stats[:, i, 0:parts, :])
            step.done(last)
            if centred:
                k.nc.vector.tensor_scalar(spread[:, :], moments[:, :, 1], eps, None, ALU.add).then_inc(k.ready, 1)
            else:
                step.done(k.nc.vector.tensor_tensor(root[:, :], moments[:, :, 0], moments[:, :, 0], ALU.mult))
                k.nc.vector.scalar_tensor_tensor(spread[:, :], moments[:, :, 1], eps, root[:, :], ALU.add, ALU.add)\
                    .then_inc(k.ready, 1)
            dve.wait_ge(k.scalar_step, 1)
            step.done(k.nc.vector.reciprocal(inverse[:, :], root[:, :]))
            for i, x in enumerate(views):
                if centred:
                    last = k.nc.vector.tensor_scalar(x, x, moments[:, i, 0:1], inverse[:, i:i + 1], ALU.subtract, ALU.mult)
                else:
                    last = k.nc.vector.tensor_scalar(x, x, inverse[:, i:i + 1], None, ALU.mult)
            step.done(last)

        @block.scalar
        def _(act):
            act.wait_ge(k.ready, 1)
            k.nc.scalar.activation(root[:, :], spread[:, :], ACT.Sqrt).then_inc(k.scalar_step, 1)


def activate(k, pairs):
    with stage(k) as block:
        @block.scalar
        def _(act):
            for out, x, f in pairs:
                last = k.nc.scalar.activation(out, x, f)
            last.then_inc(k.scalar_step, 1)
            act.wait_ge(k.scalar_step, 1)


def modulated(k, x, h, streams, layer, scale, shift):
    with buffers(k, rows=[P, streams, 2, D]) as rows:
        load(k, [(rows[:, s, j, :], k.modulation[s, bass.ds(layer * 6 * D + part * D, D)].partition_broadcast(P))
                 for s in range(streams) for j, part in enumerate((scale, shift))])

        def body(dve, step):
            for s in range(streams):
                for t in range(2):
                    a, b = x[:, 2 * s + t, :], h[:, 2 * s + t, :]
                    step.done(k.nc.vector.scalar_tensor_tensor(b, rows[:, s, 0, :], 1.0, a, ALU.add, ALU.mult))
                    step.done(k.nc.vector.tensor_tensor(b, b, rows[:, s, 1, :], ALU.add))
        on_vector(k, body)


def residual_norm(k, x, y, streams, layer, gate, which):
    with buffers(k, rows=[P, streams, D], affine=[P, 2, D]) as (rows, affine):
        load(k, [(rows[:, s, :], k.modulation[s, bass.ds(layer * 6 * D + gate * D, D)].partition_broadcast(P))
                 for s in range(streams)]
             + [(affine[:, 0, :], k.given["ln_g"][layer, which].partition_broadcast(P)),
                (affine[:, 1, :], k.given["ln_b"][layer, which].partition_broadcast(P))])

        def blend(dve, step):
            for s in range(streams):
                for t in range(2):
                    a, b = x[:, 2 * s + t, :], y[:, 2 * s + t, :]
                    step.done(k.nc.vector.tensor_tensor(b, b, rows[:, s, :], ALU.mult))
                    step.done(k.nc.vector.scalar_tensor_tensor(a, a, DN_ALPHA, b, ALU.mult, ALU.add))
        on_vector(k, blend)
        normalize(k, [x[:, t, :] for t in range(2 * streams)], LN_EPS)
        affine_rows(k, [x[:, t, :] for t in range(2 * streams)], affine[:, 0, :], affine[:, 1, :])


def affine_rows(k, views, g, b):
    def body(dve, step):
        for v in views:
            step.done(k.nc.vector.tensor_tensor(v, v, g, ALU.mult))
            if b is not None:
                step.done(k.nc.vector.tensor_tensor(v, v, b, ALU.add))
    on_vector(k, body)


def modulation_rows(k):
    with buffers(k, cond=[P, DB, 2], wide=[P, DB, P], m=[P, 1, DEPTH * 6 * D]) as (cond, wide, m), \
            split_buffers(k, "acted", [P, DB, P]) as acted, weight_rings(k):
        prefetch(k, k.given["w_mod"][0])
        load(k, [(cond[:, :, :], k.given["cond_cols"])])

        def clear(dve, step):
            step.done(k.nc.vector.memset(wide[:, :, :], 0.0))
        on_vector(k, clear)
        activate(k, [(wide[:, :, 0:2], cond[:, :, :], ACT.Silu)])
        split(k, wide[:, :, :], acted.part(slice(None), slice(None), slice(None)))
        for layer in range(DEPTH):
            project(k, acted, k.given["w_mod"][layer], m[:, :, layer * 6 * D:(layer + 1) * 6 * D], 1,
                    bias=k.given["b_mod"][layer])
            if layer + 1 < DEPTH:
                prefetch(k, k.given["w_mod"][layer + 1])
        with stage(k) as block:
            @block.sync
            def _(sp):
                sp.dma_start(k.modulation[:, :], m[0:2, 0, :]).then_inc(k.stored, 16)
                sp.wait_ge(k.stored, 16)


def chunk_mlp(k, h):
    with weight_rings(k), buffers(k, z=[P, 4, 2 * D]) as z:
        prefetch(k, k.given["a_w_in"][0])
        with split_buffers(k, "hT", [P, DB, 4 * P]) as hT:
            turn(k, h, hT, 4)
            project(k, hT, k.given["a_w_in"][0], z, 4)
        prefetch(k, k.given["a_w_out"][0])
        activate(k, [(z[:, t, :], z[:, t, :], ACT.Gelu_apprx_tanh) for t in range(4)])
        with buffers(k, affine=[P, 2, D], ws=[P, A_HEADS, P], bs=[P, A_HEADS]) as (affine, ws, bs):
            load(k, [(affine[:, 0, :], k.given["a_norm_g"][0].partition_broadcast(P)),
                     (affine[:, 1, :], k.given["a_norm_b"][0].partition_broadcast(P)),
                     (ws[:, :, :], k.given["a_w_s_t"]), (bs[:, :], k.given["a_b_s_t"])])
            normalize(k, [z[:, t, D:] for t in range(4)], LN_EPS)
            affine_rows(k, [z[:, t, D:] for t in range(4)], affine[:, 0, :], affine[:, 1, :])
            with stage(k) as block:
                @block.tensor
                def _(pe):
                    for t in range(4):
                        for a in range(A_HEADS):
                            last = matmul(k, k.psum[:, 2 * t + a // 4, (a % 4) * P:(a % 4 + 1) * P], ws[:, a, :],
                                          z[:, t, D + a * P:D + (a + 1) * P], True, True)
                        last.then_inc(k.products, 1)

                @block.vector
                def _(dve):
                    for t in range(4):
                        dve.wait_ge(k.products, t + 1)
                        for a in range(A_HEADS):
                            u = z[:, t, a * P:(a + 1) * P]
                            last = k.nc.vector.scalar_tensor_tensor(
                                u, k.psum[:, 2 * t + a // 4, (a % 4) * P:(a % 4 + 1) * P], bs[:, a:a + 1], u,
                                ALU.add, ALU.mult)
                    last.then_inc(k.vector_step, 1)
                    dve.wait_ge(k.vector_step, 1)
        with split_buffers(k, "yT", [P, DB, 4 * P]) as yT:
            turn(k, z[:, :, 0:D], yT, 4)
            project(k, yT, k.given["a_w_out"][0], h, 4)


def top16(k, scores, spare, values, places):
    yield k.nc.vector.max(values[:, 0:8], scores)
    yield k.nc.vector.max_index(places[:, 0:8], values[:, 0:8], scores)
    yield k.nc.vector.match_replace(spare, values[:, 0:8], scores, LOWEST)
    yield k.nc.vector.max(values[:, 8:16], spare)
    yield k.nc.vector.max_index(places[:, 8:16], values[:, 8:16], spare)


def peer(k, h, out, tiles, layer):
    H, K = PEER_HEADS, PEER_KEYS
    with buffers(k, scores=[P, tiles * H * 2 * K]) as scores:
        with buffers(k, qT=[P, DB * tiles * P], keys=[P, 2 * K]) as (qT, keys), \
                split_buffers(k, "hT", [P, DB, tiles * P]) as hT, weight_rings(k):
            prefetch(k, k.given["p_w_q"][layer])
            turn(k, h, hT, tiles)
            project_channels(k, hT, k.given["p_w_q"][layer], qT, tiles * P, tiles * P)
            with stage(k) as block:
                @block.gpsimd
                def _(pool):
                    k.nc.gpsimd.memset(keys[:, :], 0.0).then_inc(k.ready, 1)

                @block.sync
                def _(sp):
                    sp.wait_ge(k.ready, 1)
                    for half in range(2):
                        sp.dma_start(keys[half * 64:half * 64 + 64, half * K:(half + 1) * K],
                                     k.given["p_keys_t"][layer, half]).then_inc(k.loaded[0], 16)

                jobs = [(t, a) for t in range(tiles) for a in range(H)]

                @block.tensor
                def _(pe):
                    pe.wait_ge(k.loaded[0], 32)
                    for n, (t, a) in enumerate(jobs):
                        if n >= 8:
                            pe.wait_ge(k.copied[n % 2], (n - 8) // 2 + 1)
                        at = (a * tiles + t) * P
                        matmul(k, k.psum[:, n % 8, 0:2 * K], qT[:, at:at + P], keys[:, :], True, True)\
                            .then_inc(k.products, 1)

                def copy_out(engine, copy, mine):
                    for n in range(mine, len(jobs), 2):
                        engine.wait_ge(k.products, n + 1)
                        copy(scores[:, n * 2 * K:(n + 1) * 2 * K], k.psum[:, n % 8, 0:2 * K]).then_inc(k.copied[mine], 1)

                @block.vector
                def _(dve):
                    copy_out(dve, k.nc.vector.tensor_copy, 0)

                @block.scalar
                def _(act):
                    copy_out(act, k.nc.scalar.copy, 1)
        mix_experts(k, h, out, scores, tiles, layer)


def mix_experts(k, h, out, scores, tiles, layer):
    TK, K = PEER_TOPK, PEER_KEYS
    G = tiles * PEER_HEADS
    V = k.nc.vector
    V_START = V_RING + TK
    u_before = k.groups_gathered * (16 * TK // U_RING)
    v_before = k.groups_gathered * (16 * TK // V_RING)
    k.groups_gathered += G
    h_flat = h[:, :, :].rearrange("p t d -> p (t d)")
    out_flat = out[:, :, :].rearrange("p t d -> p (t d)")
    token = k.psum[:, 0:2, :].rearrange("p b n -> p (b n)")
    with buffers(k, u=[P, U_RING, D], v=[P, V_RING, D], product=[P, 2, D], diag=[P, TK, P],
                 s=[P, 2, K], spare=[P, 2, K], s16=[P, 2, TK], i16=([P, 2, TK], U32), i16f=[P, 2, TK],
                 cand=[P, TK * TK], spare2=[P, TK * TK], top=[P, 4, TK], pos=([P, TK], U32),
                 part=([P, 2, TK], U32), partf=[P, 2, TK], hot=[P, 2, TK, TK], found=[P, 2, TK],
                 row=[P, 2, TK], iota_=([P, TK], I32), iotaf=[P, TK], place=([P, 4, TK], U32), less=[P, 4],
                 share=[P, 4, TK], total=[P, 4], inverse=[P, 1], dots=[P, 4, TK], acted=[P, 4, TK],
                 weight=[P, 4, TK]) as \
            (u, v, product, diag, s, spare, s16, i16, i16f, cand, spare2, top, pos, part, partf, hot, found, row, iota,
             iotaf, place, less, share, total, inverse, dots, acted, weight), stage(k) as block:

        def steps(run, loop):
            with loop(0, G // 4 - 1) as i:
                for j in range(4):
                    run(i * 4 + j, j)
            for j in range(4):
                run(G - 4 + j, j)

        def within(g, n):
            return not isinstance(g, int) or g + n < G

        def fetch(pool, table, ring, size, used, start, landed, g, slot):
            grant = size // 2
            for c in range(TK):
                if c % grant == 0:
                    pool.wait_ge(used, g * TK + (start + c + grant - size))
                    pool.sem_inc(k.granted, 1)
                k.nc.gpsimd.indirect_dma_start(ring[:, c % size, :], None, table,
                                               bass.IndirectOffsetOnAxis(place[:, slot, c:c + 1], 0))\
                    .then_inc(landed[c % size], 16)

        def fetch_u(pool, g, slot):
            pool.wait_ge(k.places_set, g + 1)
            pool.sem_inc(k.granted, 1)
            fetch(pool, k.given["p_u"], u, U_RING, k.u_used, U_RING, k.u_loaded, g, slot)

        @block.gpsimd
        def _(pool):
            k.nc.gpsimd.iota(iota[:, :], [[1, TK]], base=0, channel_multiplier=0).then_inc(k.ready, 1)
            fetch_u(pool, 0, 0)

            def run(g, j):
                if within(g, 1):
                    fetch_u(pool, g + 1, (j + 1) % 4)
                fetch(pool, k.given["p_v"], v, V_RING, k.v_used, V_START, k.v_loaded, g, j)
            steps(run, pool.Fori)

        def pick(dve, g, slot):
            dve.sem_clear(k.vector_step)
            step = Chain(dve, k.vector_step)
            step.done(V.tensor_copy(s[:, :, :].rearrange("p h c -> p (h c)"), scores[:, bass.ds(g * (2 * K), 2 * K)]))
            for wave in zip(*[top16(k, s[:, p, :], spare[:, p, :], s16[:, p, :], i16[:, p, :]) for p in range(2)]):
                step.done(wave[-1])
            V.tensor_copy(i16f[:, :, :], i16[:, :, :])
            step.done(V.tensor_tensor(cand[:, :].rearrange("p (i j) -> p i j", i=TK),
                                      s16[:, 0, :].unsqueeze(2).to_broadcast([P, TK, TK]),
                                      s16[:, 1, :].unsqueeze(1).to_broadcast([P, TK, TK]), ALU.add))
            for last in top16(k, cand[:, :], spare2[:, :], top[:, slot, :], pos[:, :]):
                step.done(last)
            V.tensor_scalar(less[:, slot:slot + 1], top[:, slot, 0:1], -1.0, None, ALU.mult).then_inc(k.exp_asked, 1)
            V.tensor_scalar(part[:, 0, :], pos[:, :], 4, None, ALU.logical_shift_right)
            step.done(V.tensor_scalar(part[:, 1, :], pos[:, :], 15, None, ALU.bitwise_and))
            step.done(V.tensor_copy(partf[:, :, :], part[:, :, :]))
            step.done(V.tensor_tensor(hot[:, :, :, :].rearrange("p h n c -> p (h n) c"),
                                      partf[:, :, :].rearrange("p h n -> p (h n)").unsqueeze(2).to_broadcast([P, 2 * TK, TK]),
                                      iotaf[:, :].unsqueeze(1).to_broadcast([P, 2 * TK, TK]), ALU.is_equal))
            step.done(V.tensor_tensor(hot[:, :, :, :], hot[:, :, :, :],
                                      i16f[:, :, :].unsqueeze(2).to_broadcast([P, 2, TK, TK]), ALU.mult))
            step.done(V.tensor_reduce(found[:, :, :], hot[:, :, :, :], AX_X, ALU.add))
            step.done(V.scalar_tensor_tensor(row[:, 0, :], found[:, 0, :], float(K), found[:, 1, :], ALU.mult, ALU.add))
            step.done(V.tensor_scalar(row[:, 1, :], row[:, 0, :], float(layer * PEER_EXPERTS), None, ALU.add))
            V.tensor_copy(place[:, slot, :], row[:, 1, :]).then_inc(k.places_set, 1)

        def take_u(dve, g, slot):
            dve.sem_clear(k.vector_step)
            step = Chain(dve, k.vector_step)
            step.done(V.tensor_copy(token, h_flat[:, bass.ds((g // PEER_HEADS) * D, D)]))
            for c in range(TK):
                dve.wait_ge(k.u_loaded[c % U_RING], g * (16 * TK // U_RING) + (u_before + 16 * (c // U_RING + 1)))
                dve.wait_ge(k.u_used, g * TK + (U_RING + c - 1))
                V.tensor_tensor_reduce(product[:, c % 2, :], u[:, c % U_RING, :], token, 1.0, 0.0,
                                       ALU.mult, ALU.add, dots[:, slot, c:c + 1]).then_inc(k.u_used, 1)

        def weigh(dve, g, slot):
            dve.sem_clear(k.vector_step)
            step = Chain(dve, k.vector_step)
            dve.wait_ge(k.exp_done, g + 1)
            step.done(V.reciprocal(inverse[:, :], total[:, slot:slot + 1]))
            dve.wait_ge(k.gelu_done, g + 1)
            V.scalar_tensor_tensor(weight[:, slot, :], acted[:, slot, :], inverse[:, 0:1], share[:, slot, :],
                                   ALU.mult, ALU.mult).then_inc(k.weighed, 1)

        def add_group(dve, g, slot):
            dve.wait_ge(k.v_used, g * TK + (V_START + TK))
            to = out_flat[:, bass.ds((g // PEER_HEADS) * D, D)]
            dve.wait_ge(k.summed, g + 2)
            V.tensor_tensor(to, to, k.psum[:, 2 + 2 * (slot % 2):4 + 2 * (slot % 2), :].rearrange("p b n -> p (b n)"),
                            ALU.add).then_inc(k.summed, 1)

        @block.vector
        def _(dve):
            dve.sem_inc(k.u_used, U_RING)
            dve.sem_inc(k.summed, 1)
            V.memset(out[:, 0:tiles, :], 0.0).then_inc(k.summed, 1)
            dve.wait_ge(k.ready, 1)
            V.tensor_copy(iotaf[:, :], iota[:, :]).then_inc(k.started, 1)
            dve.wait_ge(k.started, 1)
            pick(dve, 0, 0)
            pick(dve, 1, 1)
            take_u(dve, 0, 0)

            def run(g, j):
                weigh(dve, g, j)
                if within(g, 2):
                    pick(dve, g + 2, (j + 2) % 4)
                if within(g, 1):
                    take_u(dve, g + 1, (j + 1) % 4)
                add_group(dve, g, j)
            steps(run, dve.Fori)

        def asked(act, g, slot):
            act.wait_ge(k.exp_asked, g + 1)
            k.nc.scalar.activation(share[:, slot, :], top[:, slot, :], ACT.Exp, bias=less[:, slot:slot + 1],
                                   accum_out=total[:, slot:slot + 1]).then_inc(k.exp_done, 1)

        def gelu(act, g, slot):
            act.wait_ge(k.u_used, g * TK + (U_RING + TK))
            k.nc.scalar.activation(acted[:, slot, :], dots[:, slot, :], ACT.Gelu_apprx_tanh).then_inc(k.gelu_done, 1)

        @block.scalar
        def _(act):
            asked(act, 0, 0)
            asked(act, 1, 1)
            gelu(act, 0, 0)

            def run(g, j):
                act.wait_ge(k.weighed, g + 1)
                for c in range(TK):
                    act.wait_ge(k.v_used, g * TK + (V_START + c + 1 - TK))
                    k.nc.scalar.activation(diag[:, c, :], k.ident[:, :], ACT.Copy, scale=weight[:, j, c:c + 1])\
                        .then_inc(k.diag_set, 1)
                if within(g, 2):
                    asked(act, g + 2, (j + 2) % 4)
                if within(g, 1):
                    gelu(act, g + 1, (j + 1) % 4)
            steps(run, act.Fori)

        @block.tensor
        def _(pe):
            pe.sem_inc(k.v_used, V_START)

            def run(g, j):
                pe.wait_ge(k.summed, g + 1)
                for c in range(TK):
                    pe.wait_ge(k.diag_set, g * TK + (c + 1))
                    pe.wait_ge(k.v_loaded[c % V_RING], g * (16 * TK // V_RING) + (v_before + 16 * (c // V_RING + 1)))
                    for half in range(2):
                        mm = matmul(k, k.psum[:, 2 + 2 * (j % 2) + half, :], diag[:, c, :],
                                    v[:, c % V_RING, half * NC:(half + 1) * NC], c == 0, c == TK - 1)
                    mm.then_inc(k.v_used, 1)
            steps(run, pe.Fori)


def gla_gates(k, hT, g, spare):
    with buffers(k, wg=[P, DB, 2 * GLA_RANK], w2=[P, 2, GLA_QK], bias=[P, 2, GLA_QK], low=[P, 2, NC]) as \
            (wg, w2, bias, low):
        load(k, [(wg[:, :, :], k.given["b_w_in"][0][:, 3 * D:3 * D + 2 * GLA_RANK].rearrange("(b p) n -> p b n", p=P)),
                 (w2[0:GLA_RANK, :, :], k.given["b_w_gate"][0].rearrange("j r d -> r j d")),
                 (bias[:, 0, :], k.given["b_gate_bias"][0, 0].partition_broadcast(P)),
                 (bias[:, 1, :], k.given["b_gate_bias"][0, 1].partition_broadcast(P))])
        with stage(k) as block:
            @block.tensor
            def _(pe):
                for j in range(2):
                    for b in range(DB):
                        for part in (hT.high, hT.low):
                            mm = matmul(k, k.psum[0:GLA_RANK, j, :], wg[:, b, j * GLA_RANK:(j + 1) * GLA_RANK],
                                        part[:, b, :].bitcast(F32), b == 0 and part is hT.high,
                                        b == DB - 1 and part is hT.low)
                    mm.then_inc(k.products, 1)
                for n, (t, j) in enumerate([(t, j) for t in range(4) for j in range(2)]):
                    pe.wait_ge(k.vector_step, max(2, n - 3))
                    matmul(k, k.psum[:, 2 + n % 6, :], low[0:GLA_RANK, j, t * P:(t + 1) * P], w2[0:GLA_RANK, j, :],
                           True, True).then_inc(k.products, 1)

            @block.vector
            def _(dve):
                for j in range(2):
                    dve.wait_ge(k.products, j + 1)
                    k.nc.vector.tensor_copy(low[0:GLA_RANK, j, :], k.psum[0:GLA_RANK, j, :]).then_inc(k.vector_step, 1)
                for n, (t, j) in enumerate([(t, j) for t in range(4) for j in range(2)]):
                    dve.wait_ge(k.products, n + 3)
                    k.nc.vector.tensor_tensor(g[:, t, j * GLA_QK:(j + 1) * GLA_QK], k.psum[:, 2 + n % 6, :], bias[:, j, :], ALU.add)\
                        .then_inc(k.vector_step, 1)
        log_sigmoid(k, g[:, :, :], spare, 1.0 / GLA_TAU)


def log_sigmoid(k, x, spare, scale):
    with stage(k) as block:
        @block.vector
        def _(dve):
            k.nc.vector.scalar_tensor_tensor(spare, x, -1.0, x, ALU.mult, ALU.max).then_inc(k.vector_step, 1)
            dve.wait_ge(k.scalar_step, 1)
            k.nc.vector.tensor_scalar(spare, spare, 1.0, None, ALU.add).then_inc(k.vector_step, 1)
            dve.wait_ge(k.scalar_step, 2)
            k.nc.vector.scalar_tensor_tensor(x, x, 0.0, spare, ALU.min, ALU.subtract).then_inc(k.vector_step, 1)
            dve.wait_ge(k.vector_step, 3)
            k.nc.vector.tensor_scalar(x, x, scale, None, ALU.mult).then_inc(k.vector_step, 1)

        @block.scalar
        def _(act):
            act.wait_ge(k.vector_step, 1)
            k.nc.scalar.activation(spare, spare, ACT.Exp, scale=-1.0).then_inc(k.scalar_step, 1)
            act.wait_ge(k.vector_step, 2)
            k.nc.scalar.activation(spare, spare, ACT.Ln).then_inc(k.scalar_step, 1)


def gla_tile(k, m, q, kk, v, g, backward, state, o):
    H, DV = GLA_HEADS, GLA_DV
    order = (1, 0) if backward else (0, 1)
    mask = m.suffix if backward else m.prefix
    with buffers(k, eb=[P, GLA_QK], qi=[P, GLA_QK], ki=[P, GLA_QK], ke=[P, GLA_QK], decay=[P, H, 2],
                 qT=[P, 2, H, P], kT=[P, H, P], att=[P, H, P]) as (eb, qi, ki, ke, decay, qT, kT, att):
        with stage(k) as block:
            V = k.nc.vector

            @block.tensor
            def _(pe):
                matmul(k, k.psum[:, 0, :], mask, g, True, True)
                matmul(k, k.psum[:, 1, :], m.same, g, True, True)
                for a in range(H):
                    last = matmul(k, k.psum[:, 2, 2 * a:2 * a + 2], g[:, a * P:(a + 1) * P], m.member, True, True)
                last.then_inc(k.products, 1)

            @block.vector
            def _(dve):
                step = Chain(dve, k.vector_step)
                dve.wait_ge(k.scalar_step, 1)
                step.done(V.tensor_tensor(ke[:, :], k.psum[:, 1, :], ke[:, :], ALU.subtract))
                dve.wait_ge(k.scalar_step, 5)
                V.scalar_tensor_tensor(qi[:, :], q, GLA_DK ** -0.5, eb[:, :], ALU.mult, ALU.mult)
                V.tensor_tensor(ki[:, :], ki[:, :], kk, ALU.mult)
                step.done(V.tensor_tensor(ke[:, :], ke[:, :], kk, ALU.mult))

            @block.scalar
            def _(act):
                act.wait_ge(k.products, 1)
                k.nc.scalar.copy(ke[:, :], k.psum[:, 0, :]).then_inc(k.scalar_step, 1)
                k.nc.scalar.activation(eb[:, :], k.psum[:, 0, :], ACT.Exp).then_inc(k.scalar_step, 1)
                k.nc.scalar.activation(ki[:, :], k.psum[:, 0, :], ACT.Exp, scale=-1.0).then_inc(k.scalar_step, 1)
                k.nc.scalar.activation(decay[:, :, :].rearrange("p a c -> p (a c)"), k.psum[:, 2, 0:2 * H], ACT.Exp)\
                    .then_inc(k.scalar_step, 1)
                act.wait_ge(k.vector_step, 1)
                k.nc.scalar.activation(ke[:, :], ke[:, :], ACT.Exp).then_inc(k.scalar_step, 1)

        with stage(k) as block:
            @block.gpsimd
            def _(pool):
                k.nc.gpsimd.memset(qT[:, :, :, :], 0.0).then_inc(k.ready, 1)
                k.nc.gpsimd.memset(att[:, :, :], 0.0).then_inc(k.ready, 1)

            @block.tensor
            def _(pe):
                for a in range(H):
                    k.nc.tensor.transpose(k.psum[:, 0, a * P:(a + 1) * P], qi[:, a * P:(a + 1) * P], k.ident[:, :])
                    last = k.nc.tensor.transpose(k.psum[:, 1, a * P:(a + 1) * P], ki[:, a * P:(a + 1) * P], k.ident[:, :])
                last.then_inc(k.products, 1)
                if o is not None:
                    pe.wait_ge(k.vector_step, 3)
                    for a in range(H):
                        for c in range(2):
                            last = matmul(k, k.psum[:, 2, a * P:(a + 1) * P], kT[:, a, :], qT[:, c, a, :], c == 0, c == 1)
                    last.then_inc(k.products, 1)
                for n, c in enumerate(order):
                    lo = c * GLA_CHUNK
                    for a in range(H):
                        last = matmul(k, k.psum[:, 6 + a // 2, (a % 2) * DV:(a % 2 + 1) * DV],
                                      ke[lo:lo + GLA_CHUNK, a * P:(a + 1) * P], v[lo:lo + GLA_CHUNK, a * DV:(a + 1) * DV], True, True)
                    last.then_inc(k.updates, 1)
                    if o is not None:
                        if n == 0:
                            pe.wait_ge(k.vector_step, 4)
                        for a in range(H):
                            to = k.psum[:, 3 + a // 2, (a % 2) * DV:(a % 2 + 1) * DV] if n == 0 else k.psum[:, (0, 1)[a // 2], (a % 2) * DV:(a % 2 + 1) * DV]
                            if n == 0:
                                matmul(k, to, att[:, a, :], v[:, a * DV:(a + 1) * DV], True, False)
                            last = matmul(k, to, qT[:, c, a, :], state[:, a, :], n == 1, True)
                        last.then_inc(k.outputs, 1)
                    else:
                        pe.drain().then_inc(k.outputs, 1)
                    if n == 0:
                        pe.wait_ge(k.states, 1)

            @block.vector
            def _(dve):
                step = Chain(dve, k.vector_step)
                dve.wait_ge(k.ready, 2)
                dve.wait_ge(k.products, 1)
                turned = k.psum[:, 0, :].rearrange("p (a t) -> p a t", a=H)
                for c in range(2):
                    lo = c * GLA_CHUNK
                    step.done(V.tensor_copy(qT[:, c, :, lo:lo + GLA_CHUNK], turned[:, :, lo:lo + GLA_CHUNK]))
                step.done(V.tensor_copy(kT[:, :, :].rearrange("p a t -> p (a t)"), k.psum[:, 1, :]))
                if o is not None:
                    dve.wait_ge(k.products, 2)
                    for a in range(H):
                        last = V.copy_predicated(att[:, a, :], mask.bitcast(U32), k.psum[:, 2, a * P:(a + 1) * P])
                    step.done(last)
                for n, c in enumerate(order):
                    dve.wait_ge(k.updates, n + 1)
                    dve.wait_ge(k.outputs, n + 1)
                    for a in range(H):
                        last = V.scalar_tensor_tensor(state[:, a, :], state[:, a, :], decay[:, a, c:c + 1],
                                                      k.psum[:, 6 + a // 2, (a % 2) * DV:(a % 2 + 1) * DV], ALU.mult, ALU.add)
                    last.then_inc(k.states, 1)
                if o is not None:
                    for part in ((3, 4), (0, 1)):
                        for half in range(2):
                            to = o[:, half * NC:(half + 1) * NC]
                            step.done(V.tensor_tensor(to, to, k.psum[:, part[half], :], ALU.add))


def gla_mixer(k, h):
    with buffers(k, z=[P, 4, 3 * D], o=[P, 2, D], g=[P, 4, 2 * GLA_QK]) as (z, o, g):
        with split_buffers(k, "hT", [P, DB, 4 * P]) as hT:
            turn(k, h, hT, 4)
            gla_gates(k, hT, g, z[:, :, 0:2 * GLA_QK])
            with weight_rings(k):
                project(k, hT, k.given["b_w_in"][0][:, 0:3 * D], z, 4)
        with buffers(k, prefix=[P, P], suffix=[P, P], same=[P, P], member=[P, 2], state=[P, 2, GLA_HEADS, GLA_DV]) as \
                (prefix, suffix, same, member, state):
            load(k, [(prefix[:, :], k.given["chunk_prefix"]), (suffix[:, :], k.given["chunk_suffix"]), (same[:, :], k.given["chunk_same"]),
                     (member[:, :], k.given["chunk_member"])])
            m = Kit()
            m.prefix, m.suffix, m.same, m.member = prefix[:, :], suffix[:, :], same[:, :], member[:, :]

            def clear(dve, step):
                k.nc.vector.memset(state[:, :, :, :], 0.0)
                step.done(k.nc.vector.memset(o[:, :, :], 0.0))
            on_vector(k, clear)
            for direction, tiles in ((0, (2, 3, 0, 1)), (1, (3, 2, 1, 0))):
                for t in tiles:
                    gla_tile(k, m, z[:, t, 0:GLA_QK], z[:, t, GLA_QK:2 * GLA_QK], z[:, t, D:2 * D],
                             g[:, t, direction * GLA_QK:(direction + 1) * GLA_QK], direction == 1, state[:, direction, :, :], o[:, t, :] if t < 2 else None)
        normalize(k, [o[:, t, a * GLA_DV:(a + 1) * GLA_DV] for t in range(2) for a in range(GLA_HEADS)], LN_EPS)
        activate(k, [(z[:, t, 2 * D:3 * D], z[:, t, 2 * D:3 * D], ACT.Silu) for t in range(2)])
        with buffers(k, gain=[P, D]) as gain, split_buffers(k, "yT", [P, DB, 2 * P]) as yT, weight_rings(k):
            prefetch(k, k.given["b_w_out"][0])
            load(k, [(gain[:, :], k.given["b_gn_g"][0].partition_broadcast(P))])

            def gate(dve, step):
                for t in range(2):
                    step.done(k.nc.vector.tensor_tensor(o[:, t, :], o[:, t, :], gain[:, :], ALU.mult))
                    step.done(k.nc.vector.tensor_tensor(o[:, t, :], o[:, t, :], z[:, t, 2 * D:3 * D], ALU.mult))
            on_vector(k, gate)
            turn(k, o, yT, 2)
            project(k, yT, k.given["b_w_out"][0], h, 2)


def rms_rows(k, x, h, g):
    def copy(dve, step):
        step.done(k.nc.vector.tensor_copy(h[:, :, :], x[:, 0:2, :]))
    on_vector(k, copy)
    normalize(k, [h[:, t, :] for t in range(2)], RMS_EPS, centred=False)
    with buffers(k, gain=[P, D]) as gain:
        load(k, [(gain[:, :], g.partition_broadcast(P))])
        affine_rows(k, [h[:, t, :] for t in range(2)], gain[:, :], None)


def mlstm_gates(k, hT, layer, li, b, c):
    at = 4 * D
    with buffers(k, w=[P, DB, 2 * HEADS], bias=[P, 2 * HEADS], f=[P, 2, HEADS], spare=[P, 2, HEADS]) as (w, bias, f, spare):
        load(k, [(w[:, :, :], k.given["w_in_2"][layer][:, at:at + 2 * HEADS].rearrange("(b p) n -> p b n", p=P)),
                 (bias[:, :], k.given["b_in_2"][layer][at:at + 2 * HEADS].partition_broadcast(P))])
        with stage(k) as block:
            @block.tensor
            def _(pe):
                for t in range(2):
                    for d in range(DB):
                        for part in (hT.high, hT.low):
                            mm = matmul(k, k.psum[:, t, 0:2 * HEADS], part[:, d, t * P:(t + 1) * P].bitcast(F32), w[:, d, :],
                                        d == 0 and part is hT.high, d == DB - 1 and part is hT.low)
                    mm.then_inc(k.products, 1)

            @block.vector
            def _(dve):
                dve.wait_ge(k.products, 2)
                for t in range(2):
                    k.nc.vector.tensor_tensor(li[:, t, :], k.psum[:, t, 0:HEADS], bias[:, 0:HEADS], ALU.add)
                    last = k.nc.vector.tensor_tensor(f[:, t, :], k.psum[:, t, HEADS:2 * HEADS], bias[:, HEADS:2 * HEADS], ALU.add)
                last.then_inc(k.vector_step, 1)
        log_sigmoid(k, f[:, :, :].rearrange("p t a -> p (t a)"), spare[:, :, :].rearrange("p t a -> p (t a)"), 1.0)
        with stage(k) as block:
            @block.tensor
            def _(pe):
                matmul(k, k.psum[:, 0, 0:HEADS], k.causal[:, :], f[:, 0, :], True, True)
                matmul(k, k.psum[:, 1, 0:HEADS], k.ones[:, :], f[:, 0, :], True, False)
                matmul(k, k.psum[:, 1, 0:HEADS], k.causal[:, :], f[:, 1, :], False, True).then_inc(k.products, 1)

            @block.vector
            def _(dve):
                step = Chain(dve, k.vector_step)
                dve.wait_ge(k.products, 1)
                for t in range(2):
                    last = k.nc.vector.tensor_copy(b[:, t, :], k.psum[:, t, 0:HEADS])
                step.done(last)
                step.done(k.nc.vector.tensor_tensor(c[:, :, :], li[:, :, :], b[:, :, :], ALU.subtract))


def mlstm(k, hT, layer, y):
    H = HEADS
    V = k.nc.vector
    with buffers(k, kT=[P, 2 * H, SEQ], qT=[P, 2 * H, SEQ], v=[P, 2, 2 * D]) as (kT, qT, v):
        stride = SEQ + CONV_K - 1
        with buffers(k, raw=[P, 16 * stride], bias=[P, 16], taps=[P, CONV_K, 16], tap_bias=[P, 16]) as \
                (raw, bias, taps, tap_bias):
            load(k, [(bias[:, :], k.given["b_qk_cols"][layer]), (taps[:, :, :], k.given["conv_w_cols"][layer]),
                     (tap_bias[:, :], k.given["conv_b_cols"][layer])])

            def pad(dve, step):
                step.done(V.memset(raw[:, :].rearrange("p (b t) -> p b t", b=16)[:, :, 0:CONV_K - 1], 0.0))
            on_vector(k, pad)
            project_channels(k, hT, k.given["w_in_2"][layer][:, 0:2 * D], raw, SEQ, stride, CONV_K - 1, bias)
            prefetch(k, k.given["w_in_2"][layer][:, 2 * D:4 * D])

            def convolve(dve, step):
                for j in range(CONV_K):
                    for n in range(16):
                        to = (qT if n < 8 else kT)[:, n % 8, :]
                        x = raw[:, n * stride + j:n * stride + j + SEQ]
                        if j == 0:
                            last = V.tensor_scalar(to, x, taps[:, j, n:n + 1], tap_bias[:, n:n + 1], ALU.mult, ALU.add)
                        else:
                            last = V.scalar_tensor_tensor(to, x, taps[:, j, n:n + 1], to, ALU.mult, ALU.add)
                    step.done(last)
            on_vector(k, convolve)
        activate(k, [(x[:, :, :], x[:, :, :], ACT.Silu) for x in (qT, kT)])
        project(k, hT, k.given["w_in_2"][layer][:, 2 * D:4 * D], v, 2, bias=k.given["b_in_2"][layer][2 * D:4 * D])
        prefetch(k, k.given["w_bm_2"][layer])
        with buffers(k, li=[P, 2, H], b=[P, 2, H], c=[P, 2, H]) as (li, b, c):
            mlstm_gates(k, hT, layer, li, b, c)

            def scale(dve, step):
                step.done(V.tensor_scalar(qT[:, :, :], qT[:, :, :], DK ** -0.5, None, ALU.mult))
            on_vector(k, scale)
            for a in range(H):
                mlstm_head(k, a, qT, kT, v, b, c, y)
        normalize(k, [y[:, t, a * M_DV:(a + 1) * M_DV] for t in range(2) for a in range(H)], RMS_EPS)
        activate(k, [(v[:, :, D:2 * D], v[:, :, D:2 * D], ACT.Sigmoid)])
        gate_rows(k, y, v[:, :, D:2 * D], k.given["m_norm_g_2"][layer], D)


def gate_rows(k, y, gate, gain_row, width):
    with buffers(k, gain=[P, width]) as gain:
        load(k, [(gain[:, :], gain_row.partition_broadcast(P))])

        def body(dve, step):
            for t in range(2):
                step.done(k.nc.vector.tensor_tensor(y[:, t, :], y[:, t, :], gain[:, :], ALU.mult))
                step.done(k.nc.vector.tensor_tensor(y[:, t, :], y[:, t, :], gate[:, t, :], ALU.mult))
        on_vector(k, body)


BLOCKS = ((0, 0), (1, 0), (1, 1))


def mlstm_head(k, a, qT, kT, v, b, c, y):
    V = k.nc.vector
    with buffers(k, diag=[P, 2, P], logs=[P, 3, P], probs=[P, 3, P], weighed=[P, 3, P], turned=[P, 3, P],
                 top=[P, 4], den=[P, 2], least=[P, 2], inverse=[P, 2]) as \
            (diag, logs, probs, weighed, turned, top, den, least, inverse), stage(k) as block:
        span = (slice(0, 1), slice(1, 3))

        @block.tensor
        def _(pe):
            for n, (t, s) in enumerate(BLOCKS):
                for d in range(2):
                    mm = matmul(k, k.psum[:, 1, n * P:(n + 1) * P], qT[:, 2 * a + d, t * P:(t + 1) * P],
                                kT[:, 2 * a + d, s * P:(s + 1) * P], d == 0, d == 1)
            mm.then_inc(k.scores, 1)
            pe.wait_ge(k.vector_step, 1)
            for s in range(2):
                mm = matmul(k, k.psum[:, 0, s * P:(s + 1) * P], k.ones[:, :], diag[:, s, :], True, True)
            mm.then_inc(k.products, 1)
            pe.wait_ge(k.weighed, 1)
            for n in range(3):
                last = k.nc.tensor.transpose(k.psum[:, 2, n * P:(n + 1) * P], weighed[:, n, :], k.ident[:, :])
            last.then_inc(k.products, 1)
            pe.wait_ge(k.weighed, 2)
            for n, (t, s) in enumerate(BLOCKS):
                mm = matmul(k, k.psum[:, 3 + t, 0:M_DV], turned[:, n, :], v[:, s, a * M_DV:(a + 1) * M_DV], s == 0, s == t)
            mm.then_inc(k.products, 1)

        @block.vector
        def _(dve):
            step = Chain(dve, k.vector_step)
            for s in range(2):
                last = V.tensor_scalar(diag[:, s, :], k.ident[:, :], c[:, s, a:a + 1], None, ALU.mult)
            step.done(last)
            dve.wait_ge(k.products, 1)
            for n, (t, s) in enumerate(BLOCKS):
                row = k.psum[:, 0, s * P:(s + 1) * P]
                if s < t:
                    last = V.tensor_scalar(logs[:, n, :], row, b[:, t, a:a + 1], None, ALU.add)
                else:
                    last = V.scalar_tensor_tensor(logs[:, n, :], row, b[:, t, a:a + 1], k.future[:, :], ALU.add, ALU.add)
            step.done(last)
            for t in range(2):
                last = V.tensor_reduce(top[:, t:t + 1], logs[:, span[t], :].rearrange("p n s -> p (n s)"), AX_X, ALU.max)
            step.done(last)
            step.done(V.tensor_tensor(top[:, 0:2], top[:, 0:2], b[:, :, a], ALU.max))
            V.tensor_scalar(top[:, 2:4], top[:, 0:2], -1.0, None, ALU.mult).then_inc(k.ready, 1)
            dve.wait_ge(k.scalar_step, 3)
            dve.wait_ge(k.scores, 1)
            for t in range(2):
                last = V.tensor_tensor_reduce(weighed[:, span[t], :].rearrange("p n s -> p (n s)"),
                                              probs[:, span[t], :].rearrange("p n s -> p (n s)"),
                                              k.psum[:, 1, span[t].start * P:span[t].stop * P], 1.0, 0.0,
                                              ALU.mult, ALU.add, den[:, t:t + 1])
            last.then_inc(k.weighed, 1)
            dve.wait_ge(k.products, 2)
            V.tensor_copy(turned[:, :, :].rearrange("p n s -> p (n s)"), k.psum[:, 2, 0:3 * P]).then_inc(k.weighed, 1)
            dve.wait_ge(k.weighed, 2)
            step.done(V.scalar_tensor_tensor(den[:, :], den[:, :], -1.0, den[:, :], ALU.mult, ALU.max))
            step.done(V.tensor_tensor(den[:, :], den[:, :], least[:, :], ALU.max))
            step.done(V.reciprocal(inverse[:, :], den[:, :]))
            dve.wait_ge(k.products, 3)
            for t in range(2):
                last = V.tensor_scalar(y[:, t, a * M_DV:(a + 1) * M_DV], k.psum[:, 3 + t, 0:M_DV], inverse[:, t:t + 1], None, ALU.mult)
            step.done(last)

        @block.scalar
        def _(act):
            act.wait_ge(k.ready, 1)
            for t in range(2):
                k.nc.scalar.activation(probs[:, span[t], :].rearrange("p n s -> p (n s)"),
                                       logs[:, span[t], :].rearrange("p n s -> p (n s)"), ACT.Exp,
                                       bias=top[:, 2 + t:3 + t]).then_inc(k.scalar_step, 1)
            k.nc.scalar.activation(least[:, :], top[:, 2:4], ACT.Exp).then_inc(k.scalar_step, 1)


def retention(k, hT, layer, y):
    H = HEADS
    V = k.nc.vector
    at = 4 * D + 2 * H
    with buffers(k, v=[P, 2, 2 * D]) as v:
        with buffers(k, raw=[P, 16 * SEQ]) as raw:
            with buffers(k, bias=[P, 16]) as bias:
                load(k, [(bias[:, :], k.given["b_r_cols"][layer])])
                project_channels(k, hT, k.given["w_in_2"][layer][:, at:at + 2 * D], raw, SEQ, SEQ, 0, bias)
            prefetch(k, k.given["w_in_2"][layer][:, at + 2 * D:at + 4 * D])
            with buffers(k, cos=[P, SEQ], sin=[P, SEQ], a1=[P, 8, SEQ], a2=[P, 8, SEQ]) as (cos, sin, a1, a2):
                load(k, [(cos[:, :], k.given["rope_cos"]), (sin[:, :], k.given["rope_sin"])])

                def rope(dve, step):
                    pairs = raw[:, :].rearrange("p (n h t) -> p n h t", n=8, h=2)
                    x1, x2 = pairs[:, :, 0, :], pairs[:, :, 1, :]
                    wide_cos = cos[:, :].unsqueeze(1).to_broadcast([P, 8, SEQ])
                    wide_sin = sin[:, :].unsqueeze(1).to_broadcast([P, 8, SEQ])
                    V.tensor_tensor(a1[:, :, :], x1, wide_sin, ALU.mult)
                    step.done(V.tensor_tensor(a2[:, :, :], x2, wide_sin, ALU.mult))
                    V.tensor_tensor(x1, x1, wide_cos, ALU.mult)
                    step.done(V.tensor_tensor(x2, x2, wide_cos, ALU.mult))
                    V.tensor_tensor(x1, x1, a2[:, :, :], ALU.subtract)
                    step.done(V.tensor_tensor(x2, x2, a1[:, :, :], ALU.add))
                on_vector(k, rope)
            project(k, hT, k.given["w_in_2"][layer][:, at + 2 * D:at + 4 * D], v, 2, bias=k.given["b_in_2"][layer][at + 2 * D:at + 4 * D])
            prefetch(k, k.given["w_in_2"][layer][:, at + 4 * D:at + 6 * D])
            with buffers(k, decay=[P, H, 2, SEQ], weighed=[P, H, 2, SEQ]) as (decay, weighed):
                load(k, [(decay[:, :, :, :], k.given["decay"])])
                with stage(k) as block:
                    lo = (0, P)

                    def values(pe, a):
                        pe.wait_ge(k.weighed, a + 1)
                        for t in range(2):
                            for s in range(t + 1):
                                mm = matmul(k, k.psum[:, 4 + 2 * (a % 2) + t, :], weighed[:, a, s, t * P:(t + 1) * P],
                                            v[:, s, a * R_DV:(a + 1) * R_DV], s == 0, s == t)
                        mm.then_inc(k.products, 1)

                    @block.tensor
                    def _(pe):
                        for a in range(H):
                            for s in range(2):
                                for d in range(2):
                                    q = raw[:, (2 * a + d) * SEQ + lo[s]:(2 * a + d + 1) * SEQ]
                                    kk = raw[:, (8 + 2 * a + d) * SEQ + s * P:(8 + 2 * a + d) * SEQ + (s + 1) * P]
                                    mm = matmul(k, k.psum[:, 2 * (a % 2) + s, lo[s]:SEQ], kk, q, d == 0, d == 1)
                            mm.then_inc(k.scores, 1)
                            if a >= 1:
                                values(pe, a - 1)
                        values(pe, H - 1)

                    @block.vector
                    def _(dve):
                        for a in range(H + 1):
                            if a < H:
                                dve.wait_ge(k.scores, a + 1)
                                for s in range(2):
                                    last = V.tensor_tensor(weighed[:, a, s, lo[s]:], k.psum[:, 2 * (a % 2) + s, lo[s]:SEQ],
                                                           decay[:, a, s, lo[s]:], ALU.mult)
                                last.then_inc(k.weighed, 1)
                            if a >= 1:
                                dve.wait_ge(k.products, a)
                                for t in range(2):
                                    last = V.tensor_copy(y[:, t, (a - 1) * R_DV:a * R_DV], k.psum[:, 4 + 2 * ((a - 1) % 2) + t, :])
                                last.then_inc(k.vector_step, 1)
        normalize(k, [y[:, t, a * R_DV:(a + 1) * R_DV] for t in range(2) for a in range(H)], RMS_EPS)
        project(k, hT, k.given["w_in_2"][layer][:, at + 4 * D:at + 6 * D], v, 2, bias=k.given["b_in_2"][layer][at + 4 * D:at + 6 * D])
        prefetch(k, k.given["w_br_2"][layer])
        activate(k, [(v[:, :, :], v[:, :, :], ACT.Silu)])
        gate_rows(k, y, v, k.given["r_norm_g_2"][layer], 2 * D)


def add_to(k, x, y):
    def body(dve, step):
        step.done(k.nc.vector.tensor_tensor(x[:, 0:2, :], x[:, 0:2, :], y[:, :, :], ALU.add))
    on_vector(k, body)


def feed_forward_in(k, hT, layer, f):
    with buffers(k, raw=[P, D_FF // P * SEQ], bias=[P, D_FF // P]) as (raw, bias):
        load(k, [(bias[:, :], k.given["b_ff1_cols"][layer])])
        project_channels(k, hT, k.given["w_ff1_2"][layer], raw, SEQ, SEQ, 0, bias, relu=True)
        parts = 8
        wide = raw[:, :].rearrange("p (n b t) -> p n b t", n=parts, t=SEQ)
        high = f.high[:, :, :].rearrange("p (n b) t -> p n b t", n=parts)
        low = f.low[:, :, :].rearrange("p (n b) t -> p n b t", n=parts)
        with stage(k) as block:
            @block.vector
            def _(dve):
                def take_low(dve, n):
                    dve.wait_ge(k.high_set, n + 1)
                    k.nc.vector.tensor_tensor(low[:, n], wide[:, n], high[:, n].bitcast(F32), ALU.subtract).then_inc(k.low_set, 1)

                for n in range(parts):
                    k.nc.vector.tensor_tensor(wide[:, n], wide[:, n], wide[:, n], ALU.mult).then_inc(k.ready, 1)
                    if n >= 1:
                        take_low(dve, n - 1)
                take_low(dve, parts - 1)

            @block.scalar
            def _(act):
                for n in range(parts):
                    act.wait_ge(k.ready, n + 1)
                    k.nc.scalar.copy(high[:, n], wide[:, n]).then_inc(k.high_set, 1)


def second_layer(k, x, layer):
    at = 4 * D + 2 * HEADS
    w_in, b_in = k.given["w_in_2"][layer], k.given["b_in_2"][layer]
    with buffers(k, h=[P, 2, D]) as h, split_buffers(k, "hT", [P, DB, SEQ]) as hT:
        prefetch(k, w_in[:, 0:2 * D])
        rms_rows(k, x, h, k.given["norm1_g_2"][layer])
        turn(k, h, hT, 2)
        with buffers(k, merged=[P, 2, D]) as merged:
            mlstm(k, hT, layer, h)
            with split_buffers(k, "yT", [P, DB, SEQ]) as yT:
                turn(k, h, yT, 2)
                project(k, yT, k.given["w_bm_2"][layer], merged, 2)
            prefetch(k, w_in[:, at:at + 2 * D])
            with buffers(k, wide=[P, 2, 2 * D]) as wide:
                retention(k, hT, layer, wide)
                with split_buffers(k, "yT", [P, 2 * DB, SEQ]) as yT, buffers(k, part=[P, 2, D]) as part:
                    turn(k, wide, yT, 2)
                    project(k, yT, k.given["w_br_2"][layer], part, 2)
                    prefetch(k, w_in[:, at + 6 * D:at + 8 * D])
                    project(k, hT, w_in[:, at + 6 * D:at + 8 * D], wide, 2, bias=b_in[at + 6 * D:at + 8 * D])
                    prefetch(k, k.given["w_out_2"][layer])
                    activate(k, [(wide[:, :, :], wide[:, :, :], ACT.Sigmoid)])

                    def gated(dve, step):
                        k.nc.vector.tensor_tensor(merged[:, :, :], merged[:, :, :], wide[:, :, 0:D], ALU.mult)
                        step.done(k.nc.vector.tensor_tensor(part[:, :, :], part[:, :, :], wide[:, :, D:2 * D], ALU.mult))
                        step.done(k.nc.vector.tensor_tensor(merged[:, :, :], merged[:, :, :], part[:, :, :], ALU.add))
                    on_vector(k, gated)
                    turn(k, merged, yT.part(slice(None), slice(0, DB)), 2)
                    project(k, yT, k.given["w_out_2"][layer], part, 2)
                    prefetch(k, k.given["w_ff1_2"][layer])
                    add_to(k, x, part)
        rms_rows(k, x, h, k.given["norm2_g_2"][layer])
        turn(k, h, hT, 2)
        with split_buffers(k, "f", [P, D_FF // P, SEQ]) as f:
            feed_forward_in(k, hT, layer, f)
            prefetch(k, k.given["w_ff2_2"][layer])
            project(k, f, k.given["w_ff2_2"][layer], h, 2, bias=k.given["b_ff2_2"][layer])
            prefetch(k, k.given["w_pe_gate_2"][layer])
        add_to(k, x, h)
        rms_rows(k, x, h, k.given["norm3_g_2"][layer])
        turn(k, h, hT, 2)
        with buffers(k, gate=[P, 2, D], pT=[P, 2, SEQ], w=[P, 2, D]) as (gate, pT, w):
            project(k, hT, k.given["w_pe_gate_2"][layer], gate, 2)
            activate(k, [(gate[:, :, :], gate[:, :, :], ACT.Sigmoid)])
            load(k, [(pT[:, :, :], k.given["p_t"][layer].rearrange("(b p) t -> p b t", p=P)),
                     (w[:, :, :], k.given["w_pe_2"][layer].rearrange("(b p) n -> p b n", p=P))])
            with stage(k) as block:
                @block.tensor
                def _(pe):
                    for t in range(2):
                        for n in range(2):
                            for b in range(2):
                                mm = matmul(k, k.psum[:, 2 * t + n, :], pT[:, b, t * P:(t + 1) * P],
                                            w[:, b, n * NC:(n + 1) * NC], b == 0, b == 1)
                    mm.then_inc(k.products, 1)

                @block.vector
                def _(dve):
                    dve.wait_ge(k.products, 1)
                    for t in range(2):
                        for n in range(2):
                            to = gate[:, t, n * NC:(n + 1) * NC]
                            last = k.nc.vector.tensor_tensor(to, to, k.psum[:, 2 * t + n, :], ALU.mult)
                    last.then_inc(k.vector_step, 1)
            add_to(k, x, gate)


def first_layer(k, x, layer, h):
    streams = 1 if layer == DEPTH - 1 else 2
    modulated(k, x, h, 2, layer, 1, 0)
    if layer == 0:
        chunk_mlp(k, h)
    else:
        gla_mixer(k, h)
    residual_norm(k, x, h, streams, layer, 2, 0)
    modulated(k, x, h, streams, layer, 4, 3)
    with buffers(k, mix=[P, 2 * streams, D]) as mix:
        peer(k, h, mix, 2 * streams, layer)
        residual_norm(k, x, mix, streams, layer, 5, 1)


def program(nc, given, out):
    with ExitStack() as ctx:
        k = Kit()
        k.nc, k.given, k.made = nc, given, 0

        def sem(name):
            return ctx.enter_context(nc.semaphore(name))

        k.u_loaded = [sem(f"u_loaded{n}") for n in range(U_RING)]
        k.v_loaded = [sem(f"v_loaded{n}") for n in range(V_RING)]
        k.groups_gathered = 0
        k.weights_landed = [sem(f"weights_landed{n}") for n in range(WEIGHT_SLOTS)]
        k.landed_sems = range(k.weights_landed[0].num, k.weights_landed[-1].num + 1)
        k.loaded = [sem("loaded0"), sem("loaded1")]
        k.bias_loaded = [sem("bias_loaded0"), sem("bias_loaded1")]
        k.copied = [sem("copied0"), sem("copied1")]
        k.chunks_used = sem("chunks_used")
        k.high_set = sem("high_set")
        k.low_set = sem("low_set")
        k.psum_free = sem("psum_free")
        k.products = sem("products")
        k.vector_step = sem("vector_step")
        k.scalar_step = sem("scalar_step")
        k.ready = sem("ready")
        k.stored = sem("stored")
        k.started = sem("started")
        k.places_set = sem("places_set")
        k.u_used = sem("u_used")
        k.v_used = sem("v_used")
        k.exp_asked = sem("exp_asked")
        k.updates = sem("updates")
        k.outputs = sem("outputs")
        k.states = sem("states")
        k.scores = sem("scores")
        k.granted = sem("granted")
        k.exp_done = sem("exp_done")
        k.gelu_done = sem("gelu_done")
        k.diag_set = sem("diag_set")
        k.summed = sem("summed")
        k.weighed = sem("weighed")
        first = k.loaded[0].num
        k.stage_sems = range(first, k.weighed.num + 1)
        k.psum = ctx.enter_context(nc.psum_tensor("psum", [P, 8, NC], F32))
        k.modulation = nc.dram_tensor("modulation", (2, DEPTH * 6 * D), F32).ap()
        with buffers(k, ident=[P, P], ones=[P, P], causal=[P, P], future=[P, P], x=[P, 4, D]) as \
                (k.ident, k.ones, k.causal, k.future, x):
            load(k, [(k.ident[:, :], given["ident"]), (k.ones[:, :], given["ones"]), (k.causal[:, :], given["causal"]), (k.future[:, :], given["future"]),
                     (x[:, 0:2, :], given["x"].rearrange("o (t p) d -> p (o t) d", p=P)),
                     (x[:, 2:4, :], given["ctx"].rearrange("o (t p) d -> p (o t) d", p=P))])
            modulation_rows(k)
            for layer in range(DEPTH):
                with buffers(k, h=[P, 4, D]) as h:
                    first_layer(k, x, layer, h)
            with weight_rings(k), nc.Fori(0, DEPTH) as layer:
                second_layer(k, x, layer)
            with buffers(k, h=[P, 2, D]) as h:
                rms_rows(k, x, h, given["final_g_2"])
                store(k, out, h)


def store(k, out, y):
    with stage(k) as block:
        @block.sync
        def _(sp):
            sp.dma_start(out.rearrange("o (t p) d -> p (o t) d", p=P), y[:, 0:2, :]).then_inc(k.stored, 16)
            sp.wait_ge(k.stored, 16)


def constants():
    f = np.float32
    r = np.arange(P)
    chunk = r // GLA_CHUNK
    same = chunk[:, None] == chunk[None, :]
    pos = np.arange(SEQ, dtype=f)
    inv_freq = (f(10000.0) ** (-np.arange(0, DK, 2, dtype=f) / f(DK))).astype(f)
    ang = (pos[:, None] * inv_freq[None, :]).astype(f)
    log_gamma = np.log(f(1.0) - np.exp2(-f(5.0) - np.arange(HEADS, dtype=f))).astype(f)
    diff = pos[None, :] - pos[:, None]
    decay = np.where(diff >= 0, np.exp(np.maximum(diff, 0)[None] * log_gamma[:, None, None]) * f(DK ** -0.5), 0.0)
    return {
        "ident": np.eye(P, dtype=f),
        "ones": np.ones((P, P), f),
        "causal": (r[:, None] <= r[None, :]).astype(f),
        "future": np.where(r[None, :] <= r[:, None], 0.0, MASKED).astype(f),
        "chunk_prefix": (same & (r[:, None] <= r[None, :])).astype(f),
        "chunk_suffix": (same & (r[:, None] >= r[None, :])).astype(f),
        "chunk_same": same.astype(f),
        "chunk_member": (chunk[:, None] == np.arange(2)[None, :]).astype(f),
        "rope_cos": np.ascontiguousarray(np.cos(ang).T.astype(f)),
        "rope_sin": np.ascontiguousarray(np.sin(ang).T.astype(f)),
        "decay": np.ascontiguousarray(decay.astype(f).reshape(HEADS, 2, P, SEQ).transpose(2, 0, 1, 3)),
    }


_AS_THEY_ARE = ("x ctx w_mod b_mod ln_g ln_b a_w_in a_norm_g a_norm_b a_w_out b_w_in b_w_gate b_gate_bias b_gn_g b_w_out "
                "p_w_q norm1_g_2 w_in_2 b_in_2 m_norm_g_2 r_norm_g_2 w_bm_2 w_br_2 w_out_2 norm2_g_2 w_ff1_2 "
                "w_ff2_2 b_ff2_2 norm3_g_2 w_pe_gate_2 w_pe_2 final_g_2").split()


def kernel(**inputs):
    import concourse.bacc as bacc
    from concourse.bass_utils import run_bass_kernel_spmd

    a = {n: np.asarray(v) for n, v in inputs.items()}
    at = 4 * D + 2 * HEADS
    given = {n: a[n] for n in _AS_THEY_ARE}
    given["cond_cols"] = np.stack([a["c"].reshape(DB, P).T, a["c_ctx"].reshape(DB, P).T], axis=2)
    given["b_qk_cols"] = a["b_in_2"][:, 0:2 * D].reshape(DEPTH, 16, P).transpose(0, 2, 1)
    given["b_r_cols"] = a["b_in_2"][:, at:at + 2 * D].reshape(DEPTH, 16, P).transpose(0, 2, 1)
    given["b_ff1_cols"] = a["b_ff1_2"].reshape(DEPTH, D_FF // P, P).transpose(0, 2, 1)
    given["conv_w_cols"] = a["conv_w_2"].reshape(DEPTH, CONV_K, 16, P).transpose(0, 3, 1, 2)
    given["conv_b_cols"] = a["conv_b_2"].reshape(DEPTH, 16, P).transpose(0, 2, 1)
    given["a_w_s_t"] = a["a_w_s"][0].transpose(2, 0, 1)
    given["a_b_s_t"] = a["a_b_s"][0].T
    given["p_keys_t"] = a["p_keys"].transpose(0, 1, 3, 2)
    given["p_t"] = a["p_2"][:, 0].transpose(0, 2, 1)
    given["p_u"] = a["p_u"].reshape(DEPTH * PEER_EXPERTS, D)
    given["p_v"] = a["p_v"].reshape(DEPTH * PEER_EXPERTS, D)
    given.update(constants())
    given = {n: np.ascontiguousarray(v) for n, v in given.items()}

    nc = bacc.Bacc("TRN2", target_bir_lowering=False, num_devices=1)
    there = {n: nc.dram_tensor(f"in_{n}", v.shape, F32, kind="ExternalInput").ap() for n, v in given.items()}
    out = nc.dram_tensor("out_x", (1, SEQ, D), F32, kind="ExternalOutput").ap()
    program(nc, there, out)
    r = run_bass_kernel_spmd(nc, [{f"in_{n}": v for n, v in given.items()}], core_ids=[0])
    return r.results[0]["out_x"]
```

```python
from contextlib import ExitStack, contextmanager

import numpy as np

import concourse.bass as bass
from concourse import mybir

F32 = mybir.dt.float32
F32R = mybir.dt.float32r
U32 = mybir.dt.uint32
I32 = mybir.dt.int32
ALU = mybir.AluOpType
ACT = mybir.ActivationFunctionType
AX_X = mybir.AxisListType.X

P = 128
D = 1024
DB = D // P
SEQ = 256
DEPTH = 2
LN_EPS = 1e-5
RMS_EPS = 1e-6
DN_ALPHA = (2.0 * DEPTH) ** 0.25
NC = 512
KG = 4
WEIGHT_SLOTS = 4

A_HEADS = 8
GLA_HEADS, GLA_DK, GLA_DV, GLA_RANK, GLA_TAU, GLA_CHUNK = 4, 128, 256, 16, 16.0, 64
GLA_QK = GLA_HEADS * GLA_DK
PEER_HEADS, PEER_KEYS, PEER_TOPK = 8, 128, 16
PEER_EXPERTS = PEER_KEYS * PEER_KEYS
PICKS = PEER_HEADS * PEER_TOPK
U_RING, V_RING = 16, 8
LOWEST = -3.0e38
MASKED = -1.0e30
HEADS, DK, M_DV, R_DV, CONV_K = 4, 256, 256, 512, 4
D_FF = 4 * D


class Kit:
    pass


class Chain:

    def __init__(self, engine, sem, base=0):
        self.engine, self.sem, self.base, self.n = engine, sem, base, 0

    def done(self, instruction):
        self.n += 1
        instruction.then_inc(self.sem, 1)
        self.engine.wait_ge(self.sem, self.base + self.n)


@contextmanager
def stage(k):
    with k.nc.Block() as block:
        yield block
    k.nc.sync.sem_clear(k.stage_sems)
    k.nc.all_engine_barrier()


@contextmanager
def buffers(k, **shapes):
    with ExitStack() as ctx:
        made = []
        for name, shape in shapes.items():
            k.made += 1
            dt = F32
            if isinstance(shape, tuple):
                shape, dt = shape
            made.append(ctx.enter_context(k.nc.sbuf_tensor(f"{name}_{k.made}", shape, dt)))
        yield made if len(made) > 1 else made[0]


def load(k, pairs):
    with stage(k) as block:
        @block.sync
        def _(sp):
            mine = pairs[0::2]
            for dst, src in mine:
                sp.dma_start(dst, src).then_inc(k.loaded[0], 16)
            sp.wait_ge(k.loaded[0], 16 * len(mine))

        @block.scalar
        def _(act):
            mine = pairs[1::2]
            for dst, src in mine:
                act.dma_start(dst, src).then_inc(k.loaded[1], 16)
            if mine:
                act.wait_ge(k.loaded[1], 16 * len(mine))


def on_vector(k, body):
    with stage(k) as block:
        @block.vector
        def _(dve):
            body(dve, Chain(dve, k.vector_step))


def matmul(k, out, lhsT, rhs, first, last):
    return k.nc.tensor.matmul(out, lhsT, rhs, start=first, stop=last)


class Split:

    def __init__(self, high, low):
        self.high, self.low = high, low

    def part(self, *index):
        return Split(self.high[index], self.low[index])


@contextmanager
def split_buffers(k, name, shape):
    with buffers(k, **{name + "_high": (shape, F32R), name + "_low": (shape, F32R)}) as (high, low):
        yield Split(high, low)


def split_matmul(k, out, lhsT, rhs, first, last):
    matmul(k, out, lhsT.high, rhs.high, first, False)
    matmul(k, out, lhsT.high, rhs.low, False, False)
    return matmul(k, out, lhsT.low, rhs.high, False, last)


@contextmanager
def weight_rings(k):
    with buffers(k, landing=[P, WEIGHT_SLOTS, KG, NC]) as k.landing, \
            split_buffers(k, "weights", [P, 2, KG, NC]) as k.weights:
        k.prefetched = False
        yield


def load_chunk(k, engine, w, i, j):
    groups = w.shape[0] // (KG * P)
    s, g = j // groups, j % groups
    engine.dma_start(k.landing[:, j % WEIGHT_SLOTS], w[g * KG * P:(g + 1) * KG * P, bass.ds(i * (2 * NC) + s * NC, NC)]
                     .rearrange("(b p) n -> p b n", p=P)).then_inc(k.weights_landed[j % WEIGHT_SLOTS], 16)


def prefetch(k, w):
    for j in range(WEIGHT_SLOTS):
        load_chunk(k, k.nc.sync, w, 0, j)
    k.prefetched = True


def projection(k, w, products, empty, bias=None, bias_row=None):
    groups = w.shape[0] // (KG * P)
    L = 2 * groups
    pairs = w.shape[1] // (2 * NC)
    if not k.prefetched:
        prefetch(k, w)
    k.prefetched = False

    def is_first(i):
        return isinstance(i, int) and i == 0

    def rounds(engine, run):
        run(0)
        if pairs > 1:
            with engine.Fori(1, pairs) as i:
                run(i)

    with stage(k) as block:
        @block.sync
        def _(sp):
            def run(i):
                for j in range(L):
                    if not is_first(i) or j >= WEIGHT_SLOTS:
                        sp.wait_ge(k.low_set, i * L + (j + 1 - WEIGHT_SLOTS))
                        load_chunk(k, sp, w, i, j)
            rounds(sp, run)

        @block.scalar
        def _(act):
            def run(i):
                for j in range(L):
                    if bias is not None and j % groups == 0:
                        s = j // groups
                        act.wait_ge(k.psum_free, i * 2 + (s + 1))
                        act.dma_start(bias_row[:, s, :], bias[bass.ds(i * (2 * NC) + s * NC, NC)].partition_broadcast(P))\
                           .then_inc(k.bias_loaded[s], 16)
                    act.wait_ge(k.weights_landed[j % WEIGHT_SLOTS], i * (16 * L // WEIGHT_SLOTS) + 16 * (j // WEIGHT_SLOTS + 1))
                    act.wait_ge(k.chunks_used, i * L + (j + 1))
                    k.nc.scalar.copy(k.weights.high[:, j % 2], k.landing[:, j % WEIGHT_SLOTS]).then_inc(k.high_set, 1)
            rounds(act, run)

        @block.tensor
        def _(pe):
            pe.sem_inc(k.chunks_used, 2)

            def run(i):
                for j in range(L):
                    s, g = j // groups, j % groups
                    if g == 0:
                        pe.wait_ge(k.psum_free, i * 2 + (s + 1))
                    pe.wait_ge(k.low_set, i * L + (j + 1))
                    products(s, g, k.weights.part(slice(None), j % 2), g == groups - 1).then_inc(k.chunks_used, 1)
            rounds(pe, run)

        @block.vector
        def _(dve):
            dve.sem_inc(k.psum_free, 2)

            def take(i, s):
                dve.wait_ge(k.chunks_used, i * L + (2 + groups * (s + 1)))
                if bias is not None:
                    dve.wait_ge(k.bias_loaded[s], i * 16 + 16)
                empty(i, s).then_inc(k.psum_free, 1)

            def run(i):
                for j in range(L):
                    dve.wait_ge(k.high_set, i * L + (j + 1))
                    k.nc.vector.tensor_tensor(k.weights.low[:, j % 2], k.landing[:, j % WEIGHT_SLOTS],
                                              k.weights.high[:, j % 2].bitcast(F32), ALU.subtract).then_inc(k.low_set, 1)
                    if j == groups:
                        take(i, 0)
                    elif j == 0 and not is_first(i):
                        take(i - 1, 1)
            rounds(dve, run)
            take(pairs - 1, 1)
    k.nc.sync.sem_clear(k.landed_sems)
    k.nc.all_engine_barrier()


def project(k, xT, w, out, tiles, bias=None):
    with buffers(k, bias_row=[P, 2, NC]) as bias_row:
        def products(s, g, weights, last):
            for t in range(tiles):
                for b in range(KG):
                    mm = split_matmul(k, k.psum[:, s * 4 + t, :], xT.part(slice(None), g * KG + b, slice(t * P, (t + 1) * P)),
                                      weights.part(slice(None), b), g == 0 and b == 0, last and b == KG - 1)
            return mm

        def empty(i, s):
            for t in range(tiles):
                to = out[:, t, bass.ds(i * (2 * NC) + s * NC, NC)]
                if bias is None:
                    last = k.nc.vector.tensor_copy(to, k.psum[:, s * 4 + t, :])
                else:
                    last = k.nc.vector.tensor_tensor(to, k.psum[:, s * 4 + t, :], bias_row[:, s, :], ALU.add)
            return last
        projection(k, w, products, empty, bias, bias_row)


def project_channels(k, xT, w, out, tokens, stride, offset=0, bias=None, relu=False):
    blocks = NC // P

    def products(s, g, weights, last):
        for m in range(blocks):
            for b in range(KG):
                mm = split_matmul(k, k.psum[:, s * 4 + m, 0:tokens], weights.part(slice(None), b, slice(m * P, (m + 1) * P)),
                                  xT.part(slice(None), g * KG + b, slice(0, tokens)), g == 0 and b == 0,
                                  last and b == KG - 1)
        return mm

    def empty(i, s):
        for m in range(blocks):
            at = i * (2 * blocks) + (s * blocks + m)
            to = out[:, bass.ds(i * (2 * blocks * stride) + ((s * blocks + m) * stride + offset), tokens)]
            if bias is None:
                last = k.nc.vector.tensor_copy(to, k.psum[:, s * 4 + m, 0:tokens])
            else:
                last = k.nc.vector.tensor_scalar(to, k.psum[:, s * 4 + m, 0:tokens], bias[:, bass.ds(at, 1)],
                                                 0.0 if relu else None, ALU.add, ALU.max if relu else ALU.bypass)
        return last
    projection(k, w, products, empty)


def turn(k, x, xT, tiles):
    jobs = [(t, q) for t in range(tiles) for q in range(xT.high.shape[1] // 4)]

    def target(part, t, q):
        return part[:, 4 * q:4 * q + 4, t * P:(t + 1) * P]

    with stage(k) as block:
        @block.tensor
        def _(pe):
            for n, (t, q) in enumerate(jobs):
                if n >= 8:
                    pe.wait_ge(k.low_set, n - 7)
                for b in range(4):
                    last = k.nc.tensor.transpose(k.psum[:, n % 8, b * P:(b + 1) * P],
                                                 x[:, t, (4 * q + b) * P:(4 * q + b + 1) * P], k.ident[:, :])
                last.then_inc(k.products, 1)

        @block.scalar
        def _(act):
            for n, (t, q) in enumerate(jobs):
                act.wait_ge(k.products, n + 1)
                k.nc.scalar.copy(target(xT.high, t, q), k.psum[:, n % 8, :].rearrange("p (b t) -> p b t", b=4))\
                    .then_inc(k.high_set, 1)

        @block.vector
        def _(dve):
            for n, (t, q) in enumerate(jobs):
                dve.wait_ge(k.high_set, n + 1)
                k.nc.vector.tensor_tensor(target(xT.low, t, q), k.psum[:, n % 8, :].rearrange("p (b t) -> p b t", b=4),
                                          target(xT.high, t, q).bitcast(F32), ALU.subtract).then_inc(k.low_set, 1)


def split(k, x, out):
    with stage(k) as block:
        @block.scalar
        def _(act):
            k.nc.scalar.copy(out.high, x).then_inc(k.high_set, 1)

        @block.vector
        def _(dve):
            dve.wait_ge(k.high_set, 1)
            k.nc.vector.tensor_tensor(out.low, x, out.high.bitcast(F32), ALU.subtract).then_inc(k.low_set, 1)


def norm_buffers(k, n):
    return buffers(k, stats=[P, n, 2, 6], moments=[P, n, 2], spread=[P, n], root=[P, n], inverse=[P, n])


def find_spread(k, dve, step, made, views, eps, centred, roots):
    stats, moments, spread, root, inverse = made
    V = k.nc.vector
    for i, x in enumerate(views):
        parts = -(-x.shape[-1] // NC)
        for h in range(parts):
            last = V.bn_stats(stats[:, i, h, :], x[:, h * NC:min((h + 1) * NC, x.shape[-1])])
    step.done(last)
    for i, x in enumerate(views):
        last = V.bn_aggr(moments[:, i, :], stats[:, i, 0:-(-x.shape[-1] // NC), :])
    step.done(last)
    if centred:
        V.tensor_scalar(spread[:, :], moments[:, :, 1], eps, None, ALU.add).then_inc(k.ready, 1)
    else:
        step.done(V.tensor_tensor(root[:, :], moments[:, :, 0], moments[:, :, 0], ALU.mult))
        V.scalar_tensor_tensor(spread[:, :], moments[:, :, 1], eps, root[:, :], ALU.add, ALU.add).then_inc(k.ready, 1)
    dve.wait_ge(k.scalar_step, roots)
    step.done(V.reciprocal(inverse[:, :], root[:, :]))


def take_root(k, act, made):
    stats, moments, spread, root, inverse = made
    act.wait_ge(k.ready, 1)
    k.nc.scalar.activation(root[:, :], spread[:, :], ACT.Sqrt).then_inc(k.scalar_step, 1)


def norm_gain(k, step, made, views, g, b):
    stats, moments, spread, root, inverse = made
    for i, x in enumerate(views):
        last = k.nc.vector.scalar_tensor_tensor(x, x, moments[:, i, 0:1], g, ALU.subtract, ALU.mult)
    step.done(last)
    for i, x in enumerate(views):
        last = k.nc.vector.scalar_tensor_tensor(x, x, inverse[:, i:i + 1], b, ALU.mult, ALU.add)
    step.done(last)


def head_norm(k, views, eps, gates, gain, gain_row, w=None):
    with norm_buffers(k, len(views)) as made, stage(k) as block:
        @block.sync
        def _(sp):
            sp.dma_start(gain, gain_row.partition_broadcast(P)).then_inc(k.loaded[0], 16)
            if w is not None:
                prefetch(k, w)
            sp.wait_ge(k.loaded[0], 16)

        @block.vector
        def _(dve):
            step = Chain(dve, k.vector_step)
            find_spread(k, dve, step, made, views, eps, True, len(gates) + 1)
            moments, inverse = made[1], made[4]
            for i, x in enumerate(views):
                last = k.nc.vector.tensor_scalar(x, x, moments[:, i, 0:1], inverse[:, i:i + 1], ALU.subtract, ALU.mult)
            step.done(last)

        @block.scalar
        def _(act):
            for x, f in gates:
                k.nc.scalar.activation(x, x, f).then_inc(k.scalar_step, 1)
            take_root(k, act, made)


def activate(k, pairs):
    with stage(k) as block:
        @block.scalar
        def _(act):
            for out, x, f in pairs:
                last = k.nc.scalar.activation(out, x, f)
            last.then_inc(k.scalar_step, 1)
            act.wait_ge(k.scalar_step, 1)


def modulated(k, x, h, streams, layer, scale, shift):
    with buffers(k, rows=[P, streams, 2, D]) as rows, stage(k) as block:
        def row(s, part):
            return k.modulation[s, bass.ds(layer * 6 * D + part * D, D)].partition_broadcast(P)

        @block.sync
        def _(sp):
            for j, part in enumerate((scale, shift)):
                for s in range(streams):
                    sp.dma_start(rows[:, s, j, :], row(s, part)).then_inc(k.loaded[j], 16)

        @block.vector
        def _(dve):
            step = Chain(dve, k.vector_step)
            dve.wait_ge(k.loaded[0], 16 * streams)
            for t in range(2 * streams):
                last = k.nc.vector.scalar_tensor_tensor(h[:, t, :], rows[:, t // 2, 0, :], 1.0, x[:, t, :], ALU.add, ALU.mult)
            step.done(last)
            dve.wait_ge(k.loaded[1], 16 * streams)
            for t in range(2 * streams):
                last = k.nc.vector.tensor_tensor(h[:, t, :], h[:, t, :], rows[:, t // 2, 1, :], ALU.add)
            step.done(last)


def residual_norm(k, x, y, streams, layer, gate, which):
    with buffers(k, rows=[P, streams, D], affine=[P, 2, D]) as (rows, affine), \
            norm_buffers(k, 2 * streams) as made, stage(k) as block:
        @block.sync
        def _(sp):
            for s in range(streams):
                sp.dma_start(rows[:, s, :], k.modulation[s, bass.ds(layer * 6 * D + gate * D, D)].partition_broadcast(P))\
                  .then_inc(k.loaded[0], 16)
            for j, name in enumerate(("ln_g", "ln_b")):
                sp.dma_start(affine[:, j, :], k.given[name][layer, which].partition_broadcast(P)).then_inc(k.loaded[1], 16)

        @block.vector
        def _(dve):
            step = Chain(dve, k.vector_step)
            dve.wait_ge(k.loaded[0], 16 * streams)
            for t in range(2 * streams):
                last = k.nc.vector.tensor_tensor(y[:, t, :], y[:, t, :], rows[:, t // 2, :], ALU.mult)
            step.done(last)
            for t in range(2 * streams):
                last = k.nc.vector.scalar_tensor_tensor(x[:, t, :], x[:, t, :], DN_ALPHA, y[:, t, :], ALU.mult, ALU.add)
            step.done(last)
            views = [x[:, t, :] for t in range(2 * streams)]
            find_spread(k, dve, step, made, views, LN_EPS, True, 1)
            dve.wait_ge(k.loaded[1], 32)
            norm_gain(k, step, made, views, affine[:, 0, :], affine[:, 1, :])

        @block.scalar
        def _(act):
            take_root(k, act, made)


def modulation_rows(k):
    with buffers(k, cond=[P, DB, 2], wide=[P, DB, P], m=[P, 1, DEPTH * 6 * D]) as (cond, wide, m), \
            split_buffers(k, "acted", [P, DB, P]) as acted, weight_rings(k):
        prefetch(k, k.given["w_mod"][0])
        load(k, [(cond[:, :, :], k.given["cond_cols"])])

        def clear(dve, step):
            step.done(k.nc.vector.memset(wide[:, :, :], 0.0))
        on_vector(k, clear)
        activate(k, [(wide[:, :, 0:2], cond[:, :, :], ACT.Silu)])
        split(k, wide[:, :, :], acted.part(slice(None), slice(None), slice(None)))
        for layer in range(DEPTH):
            project(k, acted, k.given["w_mod"][layer], m[:, :, layer * 6 * D:(layer + 1) * 6 * D], 1,
                    bias=k.given["b_mod"][layer])
            if layer + 1 < DEPTH:
                prefetch(k, k.given["w_mod"][layer + 1])
        with stage(k) as block:
            @block.sync
            def _(sp):
                sp.dma_start(k.modulation[:, :], m[0:2, 0, :]).then_inc(k.stored, 16)
                sp.wait_ge(k.stored, 16)


def chunk_mlp(k, h):
    with weight_rings(k), buffers(k, z=[P, 4, 2 * D]) as z:
        prefetch(k, k.given["a_w_in"][0])
        with split_buffers(k, "hT", [P, DB, 4 * P]) as hT:
            turn(k, h, hT, 4)
            project(k, hT, k.given["a_w_in"][0], z, 4)
        with buffers(k, affine=[P, 2, D], ws=[P, A_HEADS, P], bs=[P, A_HEADS]) as (affine, ws, bs):
            views = [z[:, t, D:] for t in range(4)]
            with norm_buffers(k, 4) as made, stage(k) as block:
                @block.sync
                def _(sp):
                    for dst, src in ((affine[:, 0, :], k.given["a_norm_g"][0].partition_broadcast(P)),
                                     (affine[:, 1, :], k.given["a_norm_b"][0].partition_broadcast(P)),
                                     (ws[:, :, :], k.given["a_w_s_t"]), (bs[:, :], k.given["a_b_s_t"])):
                        sp.dma_start(dst, src).then_inc(k.loaded[0], 16)
                    prefetch(k, k.given["a_w_out"][0])

                @block.scalar
                def _(act):
                    for half in (1, 0):
                        for t in range(4):
                            x = z[:, t, half * D:(half + 1) * D]
                            k.nc.scalar.activation(x, x, ACT.Gelu_apprx_tanh).then_inc(k.scalar_step, 1)
                    take_root(k, act, made)

                @block.vector
                def _(dve):
                    step = Chain(dve, k.vector_step)
                    dve.wait_ge(k.scalar_step, 4)
                    find_spread(k, dve, step, made, views, LN_EPS, True, 9)
                    dve.wait_ge(k.loaded[0], 64)
                    norm_gain(k, step, made, views, affine[:, 0, :], affine[:, 1, :])
            with stage(k) as block:
                @block.tensor
                def _(pe):
                    for t in range(4):
                        for a in range(A_HEADS):
                            last = matmul(k, k.psum[:, 2 * t + a // 4, (a % 4) * P:(a % 4 + 1) * P], ws[:, a, :],
                                          z[:, t, D + a * P:D + (a + 1) * P], True, True)
                        last.then_inc(k.products, 1)

                @block.vector
                def _(dve):
                    for t in range(4):
                        dve.wait_ge(k.products, t + 1)
                        for a in range(A_HEADS):
                            u = z[:, t, a * P:(a + 1) * P]
                            last = k.nc.vector.scalar_tensor_tensor(
                                u, k.psum[:, 2 * t + a // 4, (a % 4) * P:(a % 4 + 1) * P], bs[:, a:a + 1], u,
                                ALU.add, ALU.mult)
                    last.then_inc(k.vector_step, 1)
                    dve.wait_ge(k.vector_step, 1)
        with split_buffers(k, "yT", [P, DB, 4 * P]) as yT:
            turn(k, z[:, :, 0:D], yT, 4)
            project(k, yT, k.given["a_w_out"][0], h, 4)


def top16(k, scores, spare, values, places):
    yield k.nc.vector.max(values[:, 0:8], scores)
    yield k.nc.vector.max_index(places[:, 0:8], values[:, 0:8], scores)
    yield k.nc.vector.match_replace(spare, values[:, 0:8], scores, LOWEST)
    yield k.nc.vector.max(values[:, 8:16], spare)
    yield k.nc.vector.max_index(places[:, 8:16], values[:, 8:16], spare)


def peer(k, h, out, tiles, layer):
    H, K = PEER_HEADS, PEER_KEYS
    with buffers(k, scores=[P, tiles * H * 2 * K]) as scores:
        with buffers(k, qT=[P, DB * tiles * P], keys=[P, 2 * K]) as (qT, keys), \
                split_buffers(k, "hT", [P, DB, tiles * P]) as hT, weight_rings(k):
            prefetch(k, k.given["p_w_q"][layer])
            turn(k, h, hT, tiles)
            project_channels(k, hT, k.given["p_w_q"][layer], qT, tiles * P, tiles * P)
            with stage(k) as block:
                @block.gpsimd
                def _(pool):
                    k.nc.gpsimd.memset(keys[:, :], 0.0).then_inc(k.ready, 1)

                @block.sync
                def _(sp):
                    sp.wait_ge(k.ready, 1)
                    for half in range(2):
                        sp.dma_start(keys[half * 64:half * 64 + 64, half * K:(half + 1) * K],
                                     k.given["p_keys_t"][layer, half]).then_inc(k.loaded[0], 16)

                jobs = [(t, a) for t in range(tiles) for a in range(H)]

                @block.tensor
                def _(pe):
                    pe.wait_ge(k.loaded[0], 32)
                    for n, (t, a) in enumerate(jobs):
                        if n >= 8:
                            pe.wait_ge(k.copied[n % 2], (n - 8) // 2 + 1)
                        at = (a * tiles + t) * P
                        matmul(k, k.psum[:, n % 8, 0:2 * K], qT[:, at:at + P], keys[:, :], True, True)\
                            .then_inc(k.products, 1)

                def copy_out(engine, copy, mine):
                    for n in range(mine, len(jobs), 2):
                        engine.wait_ge(k.products, n + 1)
                        copy(scores[:, n * 2 * K:(n + 1) * 2 * K], k.psum[:, n % 8, 0:2 * K]).then_inc(k.copied[mine], 1)

                @block.vector
                def _(dve):
                    copy_out(dve, k.nc.vector.tensor_copy, 0)

                @block.scalar
                def _(act):
                    copy_out(act, k.nc.scalar.copy, 1)
        mix_experts(k, h, out, scores, tiles, layer)


def mix_experts(k, h, out, scores, tiles, layer):
    TK, K = PEER_TOPK, PEER_KEYS
    G = tiles * PEER_HEADS
    V = k.nc.vector
    V_START = V_RING + TK
    u_before = k.groups_gathered * (16 * TK // U_RING)
    v_before = k.groups_gathered * (16 * TK // V_RING)
    k.groups_gathered += G
    h_flat = h[:, :, :].rearrange("p t d -> p (t d)")
    out_flat = out[:, :, :].rearrange("p t d -> p (t d)")
    token = k.psum[:, 0:2, :].rearrange("p b n -> p (b n)")
    with buffers(k, u=[P, U_RING, D], v=[P, V_RING, D], product=[P, 2, D], diag=[P, TK, P],
                 s=[P, 2, K], spare=[P, 2, K], s16=[P, 2, TK], i16=([P, 2, TK], U32), i16f=[P, 2, TK],
                 cand=[P, TK * TK], spare2=[P, TK * TK], top=[P, 4, TK], pos=([P, TK], U32),
                 part=([P, 2, TK], U32), partf=[P, 2, TK], hot=[P, 2, TK, TK], found=[P, 2, TK],
                 row=[P, 2, TK], iota_=([P, TK], I32), iotaf=[P, TK], place=([P, 4, TK], U32), less=[P, 4],
                 share=[P, 4, TK], total=[P, 4], inverse=[P, 1], dots=[P, 4, TK], acted=[P, 4, TK],
                 weight=[P, 4, TK]) as \
            (u, v, product, diag, s, spare, s16, i16, i16f, cand, spare2, top, pos, part, partf, hot, found, row, iota,
             iotaf, place, less, share, total, inverse, dots, acted, weight), stage(k) as block:

        def steps(run, loop):
            with loop(0, G // 4 - 1) as i:
                for j in range(4):
                    run(i * 4 + j, j)
            for j in range(4):
                run(G - 4 + j, j)

        def within(g, n):
            return not isinstance(g, int) or g + n < G

        def fetch(pool, table, ring, size, used, start, landed, g, slot):
            grant = size // 2
            for c in range(TK):
                if c % grant == 0:
                    pool.wait_ge(used, g * TK + (start + c + grant - size))
                    pool.sem_inc(k.granted, 1)
                k.nc.gpsimd.indirect_dma_start(ring[:, c % size, :], None, table,
                                               bass.IndirectOffsetOnAxis(place[:, slot, c:c + 1], 0))\
                    .then_inc(landed[c % size], 16)

        def fetch_u(pool, g, slot):
            pool.wait_ge(k.places_set, g + 1)
            pool.sem_inc(k.granted, 1)
            fetch(pool, k.given["p_u"], u, U_RING, k.u_used, U_RING, k.u_loaded, g, slot)

        @block.gpsimd
        def _(pool):
            k.nc.gpsimd.iota(iota[:, :], [[1, TK]], base=0, channel_multiplier=0).then_inc(k.ready, 1)
            fetch_u(pool, 0, 0)

            def run(g, j):
                if within(g, 1):
                    fetch_u(pool, g + 1, (j + 1) % 4)
                fetch(pool, k.given["p_v"], v, V_RING, k.v_used, V_START, k.v_loaded, g, j)
            steps(run, pool.Fori)

        def pick(dve, g, slot):
            dve.sem_clear(k.vector_step)
            step = Chain(dve, k.vector_step)
            step.done(V.tensor_copy(s[:, :, :].rearrange("p h c -> p (h c)"), scores[:, bass.ds(g * (2 * K), 2 * K)]))
            for wave in zip(*[top16(k, s[:, p, :], spare[:, p, :], s16[:, p, :], i16[:, p, :]) for p in range(2)]):
                step.done(wave[-1])
            V.tensor_copy(i16f[:, :, :], i16[:, :, :])
            step.done(V.tensor_tensor(cand[:, :].rearrange("p (i j) -> p i j", i=TK),
                                      s16[:, 0, :].unsqueeze(2).to_broadcast([P, TK, TK]),
                                      s16[:, 1, :].unsqueeze(1).to_broadcast([P, TK, TK]), ALU.add))
            for last in top16(k, cand[:, :], spare2[:, :], top[:, slot, :], pos[:, :]):
                step.done(last)
            V.tensor_scalar(less[:, slot:slot + 1], top[:, slot, 0:1], -1.0, None, ALU.mult).then_inc(k.exp_asked, 1)
            V.tensor_scalar(part[:, 0, :], pos[:, :], 4, None, ALU.logical_shift_right)
            step.done(V.tensor_scalar(part[:, 1, :], pos[:, :], 15, None, ALU.bitwise_and))
            step.done(V.tensor_copy(partf[:, :, :], part[:, :, :]))
            step.done(V.tensor_tensor(hot[:, :, :, :].rearrange("p h n c -> p (h n) c"),
                                      partf[:, :, :].rearrange("p h n -> p (h n)").unsqueeze(2).to_broadcast([P, 2 * TK, TK]),
                                      iotaf[:, :].unsqueeze(1).to_broadcast([P, 2 * TK, TK]), ALU.is_equal))
            step.done(V.tensor_tensor(hot[:, :, :, :], hot[:, :, :, :],
                                      i16f[:, :, :].unsqueeze(2).to_broadcast([P, 2, TK, TK]), ALU.mult))
            step.done(V.tensor_reduce(found[:, :, :], hot[:, :, :, :], AX_X, ALU.add))
            step.done(V.scalar_tensor_tensor(row[:, 0, :], found[:, 0, :], float(K), found[:, 1, :], ALU.mult, ALU.add))
            step.done(V.tensor_scalar(row[:, 1, :], row[:, 0, :], float(layer * PEER_EXPERTS), None, ALU.add))
            V.tensor_copy(place[:, slot, :], row[:, 1, :]).then_inc(k.places_set, 1)

        def take_u(dve, g, slot):
            dve.sem_clear(k.vector_step)
            step = Chain(dve, k.vector_step)
            step.done(V.tensor_copy(token, h_flat[:, bass.ds((g // PEER_HEADS) * D, D)]))
            for c in range(TK):
                dve.wait_ge(k.u_loaded[c % U_RING], g * (16 * TK // U_RING) + (u_before + 16 * (c // U_RING + 1)))
                dve.wait_ge(k.u_used, g * TK + (U_RING + c - 1))
                V.tensor_tensor_reduce(product[:, c % 2, :], u[:, c % U_RING, :], token, 1.0, 0.0,
                                       ALU.mult, ALU.add, dots[:, slot, c:c + 1]).then_inc(k.u_used, 1)

        def weigh(dve, g, slot):
            dve.sem_clear(k.vector_step)
            step = Chain(dve, k.vector_step)
            dve.wait_ge(k.exp_done, g + 1)
            step.done(V.reciprocal(inverse[:, :], total[:, slot:slot + 1]))
            dve.wait_ge(k.gelu_done, g + 1)
            V.scalar_tensor_tensor(weight[:, slot, :], acted[:, slot, :], inverse[:, 0:1], share[:, slot, :],
                                   ALU.mult, ALU.mult).then_inc(k.weighed, 1)

        def add_group(dve, g, slot):
            dve.wait_ge(k.v_used, g * TK + (V_START + TK))
            to = out_flat[:, bass.ds((g // PEER_HEADS) * D, D)]
            dve.wait_ge(k.summed, g + 2)
            V.tensor_tensor(to, to, k.psum[:, 2 + 2 * (slot % 2):4 + 2 * (slot % 2), :].rearrange("p b n -> p (b n)"),
                            ALU.add).then_inc(k.summed, 1)

        @block.vector
        def _(dve):
            dve.sem_inc(k.u_used, U_RING)
            dve.sem_inc(k.summed, 1)
            V.memset(out[:, 0:tiles, :], 0.0).then_inc(k.summed, 1)
            dve.wait_ge(k.ready, 1)
            V.tensor_copy(iotaf[:, :], iota[:, :]).then_inc(k.started, 1)
            dve.wait_ge(k.started, 1)
            pick(dve, 0, 0)
            pick(dve, 1, 1)
            take_u(dve, 0, 0)

            def run(g, j):
                weigh(dve, g, j)
                if within(g, 2):
                    pick(dve, g + 2, (j + 2) % 4)
                if within(g, 1):
                    take_u(dve, g + 1, (j + 1) % 4)
                add_group(dve, g, j)
            steps(run, dve.Fori)

        def asked(act, g, slot):
            act.wait_ge(k.exp_asked, g + 1)
            k.nc.scalar.activation(share[:, slot, :], top[:, slot, :], ACT.Exp, bias=less[:, slot:slot + 1],
                                   accum_out=total[:, slot:slot + 1]).then_inc(k.exp_done, 1)

        def gelu(act, g, slot):
            act.wait_ge(k.u_used, g * TK + (U_RING + TK))
            k.nc.scalar.activation(acted[:, slot, :], dots[:, slot, :], ACT.Gelu_apprx_tanh).then_inc(k.gelu_done, 1)

        @block.scalar
        def _(act):
            asked(act, 0, 0)
            asked(act, 1, 1)
            gelu(act, 0, 0)

            def run(g, j):
                act.wait_ge(k.weighed, g + 1)
                for c in range(TK):
                    act.wait_ge(k.v_used, g * TK + (V_START + c + 1 - TK))
                    k.nc.scalar.activation(diag[:, c, :], k.ident[:, :], ACT.Copy, scale=weight[:, j, c:c + 1])\
                        .then_inc(k.diag_set, 1)
                if within(g, 2):
                    asked(act, g + 2, (j + 2) % 4)
                if within(g, 1):
                    gelu(act, g + 1, (j + 1) % 4)
            steps(run, act.Fori)

        @block.tensor
        def _(pe):
            pe.sem_inc(k.v_used, V_START)

            def run(g, j):
                pe.wait_ge(k.summed, g + 1)
                for c in range(TK):
                    pe.wait_ge(k.diag_set, g * TK + (c + 1))
                    pe.wait_ge(k.v_loaded[c % V_RING], g * (16 * TK // V_RING) + (v_before + 16 * (c // V_RING + 1)))
                    for half in range(2):
                        mm = matmul(k, k.psum[:, 2 + 2 * (j % 2) + half, :], diag[:, c, :],
                                    v[:, c % V_RING, half * NC:(half + 1) * NC], c == 0, c == TK - 1)
                    mm.then_inc(k.v_used, 1)
            steps(run, pe.Fori)


def gla_gates(k, hT, g, spare):
    with buffers(k, wg=[P, DB, 2 * GLA_RANK], w2=[P, 2, GLA_QK], bias=[P, 2, GLA_QK], low=[P, 2, NC]) as \
            (wg, w2, bias, low):
        load(k, [(wg[:, :, :], k.given["b_w_in"][0][:, 3 * D:3 * D + 2 * GLA_RANK].rearrange("(b p) n -> p b n", p=P)),
                 (w2[0:GLA_RANK, :, :], k.given["b_w_gate"][0].rearrange("j r d -> r j d")),
                 (bias[:, 0, :], k.given["b_gate_bias"][0, 0].partition_broadcast(P)),
                 (bias[:, 1, :], k.given["b_gate_bias"][0, 1].partition_broadcast(P))])
        with stage(k) as block:
            @block.tensor
            def _(pe):
                for j in range(2):
                    for b in range(DB):
                        for part in (hT.high, hT.low):
                            mm = matmul(k, k.psum[0:GLA_RANK, j, :], wg[:, b, j * GLA_RANK:(j + 1) * GLA_RANK],
                                        part[:, b, :].bitcast(F32), b == 0 and part is hT.high,
                                        b == DB - 1 and part is hT.low)
                    mm.then_inc(k.products, 1)
                for n, (t, j) in enumerate([(t, j) for t in range(4) for j in range(2)]):
                    pe.wait_ge(k.vector_step, max(2, n - 3))
                    matmul(k, k.psum[:, 2 + n % 6, :], low[0:GLA_RANK, j, t * P:(t + 1) * P], w2[0:GLA_RANK, j, :],
                           True, True).then_inc(k.products, 1)

            @block.vector
            def _(dve):
                for j in range(2):
                    dve.wait_ge(k.products, j + 1)
                    k.nc.vector.tensor_copy(low[0:GLA_RANK, j, :], k.psum[0:GLA_RANK, j, :]).then_inc(k.vector_step, 1)
                for n, (t, j) in enumerate([(t, j) for t in range(4) for j in range(2)]):
                    dve.wait_ge(k.products, n + 3)
                    k.nc.vector.tensor_tensor(g[:, t, j * GLA_QK:(j + 1) * GLA_QK], k.psum[:, 2 + n % 6, :], bias[:, j, :], ALU.add)\
                        .then_inc(k.vector_step, 1)
        log_sigmoid(k, g[:, :, :], spare, 1.0 / GLA_TAU)


def log_sigmoid(k, x, spare, scale):
    with stage(k) as block:
        @block.vector
        def _(dve):
            k.nc.vector.scalar_tensor_tensor(spare, x, -1.0, x, ALU.mult, ALU.max).then_inc(k.vector_step, 1)
            dve.wait_ge(k.scalar_step, 1)
            k.nc.vector.tensor_scalar(spare, spare, 1.0, None, ALU.add).then_inc(k.vector_step, 1)
            dve.wait_ge(k.scalar_step, 2)
            k.nc.vector.scalar_tensor_tensor(x, x, 0.0, spare, ALU.min, ALU.subtract).then_inc(k.vector_step, 1)
            dve.wait_ge(k.vector_step, 3)
            k.nc.vector.tensor_scalar(x, x, scale, None, ALU.mult).then_inc(k.vector_step, 1)

        @block.scalar
        def _(act):
            act.wait_ge(k.vector_step, 1)
            k.nc.scalar.activation(spare, spare, ACT.Exp, scale=-1.0).then_inc(k.scalar_step, 1)
            act.wait_ge(k.vector_step, 2)
            k.nc.scalar.activation(spare, spare, ACT.Ln).then_inc(k.scalar_step, 1)


def gla_tile(k, m, q, kk, v, g, backward, state, o):
    H, DV = GLA_HEADS, GLA_DV
    order = (1, 0) if backward else (0, 1)
    mask = m.suffix if backward else m.prefix
    with buffers(k, eb=[P, GLA_QK], qi=[P, GLA_QK], ki=[P, GLA_QK], ke=[P, GLA_QK], decay=[P, H, 2],
                 qT=[P, 2, H, P], kT=[P, H, P], att=[P, H, P]) as (eb, qi, ki, ke, decay, qT, kT, att):
        with stage(k) as block:
            V = k.nc.vector

            @block.tensor
            def _(pe):
                matmul(k, k.psum[:, 0, :], mask, g, True, True)
                matmul(k, k.psum[:, 1, :], m.same, g, True, True)
                for a in range(H):
                    last = matmul(k, k.psum[:, 2, 2 * a:2 * a + 2], g[:, a * P:(a + 1) * P], m.member, True, True)
                last.then_inc(k.products, 1)

            @block.vector
            def _(dve):
                step = Chain(dve, k.vector_step)
                dve.wait_ge(k.scalar_step, 1)
                step.done(V.tensor_tensor(ke[:, :], k.psum[:, 1, :], ke[:, :], ALU.subtract))
                dve.wait_ge(k.scalar_step, 5)
                V.scalar_tensor_tensor(qi[:, :], q, GLA_DK ** -0.5, eb[:, :], ALU.mult, ALU.mult)
                V.tensor_tensor(ki[:, :], ki[:, :], kk, ALU.mult)
                step.done(V.tensor_tensor(ke[:, :], ke[:, :], kk, ALU.mult))

            @block.scalar
            def _(act):
                act.wait_ge(k.products, 1)
                k.nc.scalar.copy(ke[:, :], k.psum[:, 0, :]).then_inc(k.scalar_step, 1)
                k.nc.scalar.activation(eb[:, :], k.psum[:, 0, :], ACT.Exp).then_inc(k.scalar_step, 1)
                k.nc.scalar.activation(ki[:, :], k.psum[:, 0, :], ACT.Exp, scale=-1.0).then_inc(k.scalar_step, 1)
                k.nc.scalar.activation(decay[:, :, :].rearrange("p a c -> p (a c)"), k.psum[:, 2, 0:2 * H], ACT.Exp)\
                    .then_inc(k.scalar_step, 1)
                act.wait_ge(k.vector_step, 1)
                k.nc.scalar.activation(ke[:, :], ke[:, :], ACT.Exp).then_inc(k.scalar_step, 1)

        with stage(k) as block:
            @block.gpsimd
            def _(pool):
                k.nc.gpsimd.memset(qT[:, :, :, :], 0.0).then_inc(k.ready, 1)
                k.nc.gpsimd.memset(att[:, :, :], 0.0).then_inc(k.ready, 1)

            @block.tensor
            def _(pe):
                for a in range(H):
                    k.nc.tensor.transpose(k.psum[:, 0, a * P:(a + 1) * P], qi[:, a * P:(a + 1) * P], k.ident[:, :])
                    last = k.nc.tensor.transpose(k.psum[:, 1, a * P:(a + 1) * P], ki[:, a * P:(a + 1) * P], k.ident[:, :])
                last.then_inc(k.products, 1)
                if o is not None:
                    pe.wait_ge(k.vector_step, 3)
                    for a in range(H):
                        for c in range(2):
                            last = matmul(k, k.psum[:, 2, a * P:(a + 1) * P], kT[:, a, :], qT[:, c, a, :], c == 0, c == 1)
                    last.then_inc(k.products, 1)
                for n, c in enumerate(order):
                    lo = c * GLA_CHUNK
                    for a in range(H):
                        last = matmul(k, k.psum[:, 6 + a // 2, (a % 2) * DV:(a % 2 + 1) * DV],
                                      ke[lo:lo + GLA_CHUNK, a * P:(a + 1) * P], v[lo:lo + GLA_CHUNK, a * DV:(a + 1) * DV], True, True)
                    last.then_inc(k.updates, 1)
                    if o is not None:
                        if n == 0:
                            pe.wait_ge(k.vector_step, 4)
                        for a in range(H):
                            to = k.psum[:, 3 + a // 2, (a % 2) * DV:(a % 2 + 1) * DV] if n == 0 else k.psum[:, (0, 1)[a // 2], (a % 2) * DV:(a % 2 + 1) * DV]
                            if n == 0:
                                matmul(k, to, att[:, a, :], v[:, a * DV:(a + 1) * DV], True, False)
                            last = matmul(k, to, qT[:, c, a, :], state[:, a, :], n == 1, True)
                        last.then_inc(k.outputs, 1)
                    else:
                        pe.drain().then_inc(k.outputs, 1)
                    if n == 0:
                        pe.wait_ge(k.states, 1)

            @block.vector
            def _(dve):
                step = Chain(dve, k.vector_step)
                dve.wait_ge(k.ready, 2)
                dve.wait_ge(k.products, 1)
                turned = k.psum[:, 0, :].rearrange("p (a t) -> p a t", a=H)
                for c in range(2):
                    lo = c * GLA_CHUNK
                    step.done(V.tensor_copy(qT[:, c, :, lo:lo + GLA_CHUNK], turned[:, :, lo:lo + GLA_CHUNK]))
                step.done(V.tensor_copy(kT[:, :, :].rearrange("p a t -> p (a t)"), k.psum[:, 1, :]))
                if o is not None:
                    dve.wait_ge(k.products, 2)
                    for a in range(H):
                        last = V.copy_predicated(att[:, a, :], mask.bitcast(U32), k.psum[:, 2, a * P:(a + 1) * P])
                    step.done(last)
                for n, c in enumerate(order):
                    dve.wait_ge(k.updates, n + 1)
                    dve.wait_ge(k.outputs, n + 1)
                    for a in range(H):
                        last = V.scalar_tensor_tensor(state[:, a, :], state[:, a, :], decay[:, a, c:c + 1],
                                                      k.psum[:, 6 + a // 2, (a % 2) * DV:(a % 2 + 1) * DV], ALU.mult, ALU.add)
                    last.then_inc(k.states, 1)
                if o is not None:
                    for part in ((3, 4), (0, 1)):
                        for half in range(2):
                            to = o[:, half * NC:(half + 1) * NC]
                            step.done(V.tensor_tensor(to, to, k.psum[:, part[half], :], ALU.add))


def gla_mixer(k, h):
    with buffers(k, z=[P, 4, 3 * D], o=[P, 2, D], g=[P, 4, 2 * GLA_QK]) as (z, o, g):
        with split_buffers(k, "hT", [P, DB, 4 * P]) as hT:
            turn(k, h, hT, 4)
            gla_gates(k, hT, g, z[:, :, 0:2 * GLA_QK])
            with weight_rings(k):
                project(k, hT, k.given["b_w_in"][0][:, 0:3 * D], z, 4)
        with buffers(k, prefix=[P, P], suffix=[P, P], same=[P, P], member=[P, 2], state=[P, 2, GLA_HEADS, GLA_DV]) as \
                (prefix, suffix, same, member, state):
            load(k, [(prefix[:, :], k.given["chunk_prefix"]), (suffix[:, :], k.given["chunk_suffix"]), (same[:, :], k.given["chunk_same"]),
                     (member[:, :], k.given["chunk_member"])])
            m = Kit()
            m.prefix, m.suffix, m.same, m.member = prefix[:, :], suffix[:, :], same[:, :], member[:, :]

            def clear(dve, step):
                k.nc.vector.memset(state[:, :, :, :], 0.0)
                step.done(k.nc.vector.memset(o[:, :, :], 0.0))
            on_vector(k, clear)
            for direction, tiles in ((0, (2, 3, 0, 1)), (1, (3, 2, 1, 0))):
                for t in tiles:
                    gla_tile(k, m, z[:, t, 0:GLA_QK], z[:, t, GLA_QK:2 * GLA_QK], z[:, t, D:2 * D],
                             g[:, t, direction * GLA_QK:(direction + 1) * GLA_QK], direction == 1, state[:, direction, :, :], o[:, t, :] if t < 2 else None)
        with buffers(k, gain=[P, D]) as gain, split_buffers(k, "yT", [P, DB, 2 * P]) as yT, weight_rings(k):
            head_norm(k, [o[:, t, a * GLA_DV:(a + 1) * GLA_DV] for t in range(2) for a in range(GLA_HEADS)], LN_EPS,
                      [(z[:, t, 2 * D:3 * D], ACT.Silu) for t in range(2)], gain[:, :], k.given["b_gn_g"][0],
                      k.given["b_w_out"][0])
            gate_rows(k, o, z[:, :, 2 * D:3 * D], gain)
            turn(k, o, yT, 2)
            project(k, yT, k.given["b_w_out"][0], h, 2)


def rms_rows(k, x, h, g, w=None):
    with buffers(k, gain=[P, D]) as gain, norm_buffers(k, 2) as made, stage(k) as block:
        @block.sync
        def _(sp):
            sp.dma_start(gain[:, :], g.partition_broadcast(P)).then_inc(k.loaded[0], 16)
            if w is not None:
                prefetch(k, w)

        @block.vector
        def _(dve):
            step = Chain(dve, k.vector_step)
            find_spread(k, dve, step, made, [x[:, t, :] for t in range(2)], RMS_EPS, False, 1)
            dve.wait_ge(k.loaded[0], 16)
            inverse = made[4]
            for t in range(2):
                last = k.nc.vector.scalar_tensor_tensor(h[:, t, :], x[:, t, :], inverse[:, t:t + 1], gain[:, :], ALU.mult, ALU.mult)
            step.done(last)

        @block.scalar
        def _(act):
            take_root(k, act, made)


def mlstm_gates(k, hT, layer, li, b, c):
    at = 4 * D
    with buffers(k, w=[P, DB, 2 * HEADS], bias=[P, 2 * HEADS], f=[P, 2, HEADS], spare=[P, 2, HEADS]) as (w, bias, f, spare):
        load(k, [(w[:, :, :], k.given["w_in_2"][layer][:, at:at + 2 * HEADS].rearrange("(b p) n -> p b n", p=P)),
                 (bias[:, :], k.given["b_in_2"][layer][at:at + 2 * HEADS].partition_broadcast(P))])
        prefetch(k, k.given["w_bm_2"][layer])
        with stage(k) as block:
            @block.tensor
            def _(pe):
                for t in range(2):
                    for d in range(DB):
                        for part in (hT.high, hT.low):
                            mm = matmul(k, k.psum[:, t, 0:2 * HEADS], part[:, d, t * P:(t + 1) * P].bitcast(F32), w[:, d, :],
                                        d == 0 and part is hT.high, d == DB - 1 and part is hT.low)
                    mm.then_inc(k.products, 1)

            @block.vector
            def _(dve):
                dve.wait_ge(k.products, 2)
                for t in range(2):
                    k.nc.vector.tensor_tensor(li[:, t, :], k.psum[:, t, 0:HEADS], bias[:, 0:HEADS], ALU.add)
                    last = k.nc.vector.tensor_tensor(f[:, t, :], k.psum[:, t, HEADS:2 * HEADS], bias[:, HEADS:2 * HEADS], ALU.add)
                last.then_inc(k.vector_step, 1)
        log_sigmoid(k, f[:, :, :].rearrange("p t a -> p (t a)"), spare[:, :, :].rearrange("p t a -> p (t a)"), 1.0)
        with stage(k) as block:
            @block.tensor
            def _(pe):
                matmul(k, k.psum[:, 0, 0:HEADS], k.causal[:, :], f[:, 0, :], True, True)
                matmul(k, k.psum[:, 1, 0:HEADS], k.ones[:, :], f[:, 0, :], True, False)
                matmul(k, k.psum[:, 1, 0:HEADS], k.causal[:, :], f[:, 1, :], False, True).then_inc(k.products, 1)

            @block.vector
            def _(dve):
                step = Chain(dve, k.vector_step)
                dve.wait_ge(k.products, 1)
                for t in range(2):
                    last = k.nc.vector.tensor_copy(b[:, t, :], k.psum[:, t, 0:HEADS])
                step.done(last)
                step.done(k.nc.vector.tensor_tensor(c[:, :, :], li[:, :, :], b[:, :, :], ALU.subtract))


def mlstm(k, hT, layer, y):
    H = HEADS
    V = k.nc.vector
    with buffers(k, kT=[P, 2 * H, SEQ], qT=[P, 2 * H, SEQ], v=[P, 2, 2 * D]) as (kT, qT, v):
        stride = SEQ + CONV_K - 1
        with buffers(k, raw=[P, 16 * stride], bias=[P, 16], taps=[P, CONV_K, 16], tap_bias=[P, 16]) as \
                (raw, bias, taps, tap_bias):
            load(k, [(bias[:, :], k.given["b_qk_cols"][layer]), (taps[:, :, :], k.given["conv_w_cols"][layer]),
                     (tap_bias[:, :], k.given["conv_b_cols"][layer])])

            def pad(dve, step):
                step.done(V.memset(raw[:, :].rearrange("p (b t) -> p b t", b=16)[:, :, 0:CONV_K - 1], 0.0))
            on_vector(k, pad)
            project_channels(k, hT, k.given["w_in_2"][layer][:, 0:2 * D], raw, SEQ, stride, CONV_K - 1, bias)
            prefetch(k, k.given["w_in_2"][layer][:, 2 * D:4 * D])

            def convolve(dve, step):
                for j in range(CONV_K):
                    for n in range(16):
                        to = (qT if n < 8 else kT)[:, n % 8, :]
                        x = raw[:, n * stride + j:n * stride + j + SEQ]
                        if j == 0:
                            last = V.tensor_scalar(to, x, taps[:, j, n:n + 1], tap_bias[:, n:n + 1], ALU.mult, ALU.add)
                        else:
                            last = V.scalar_tensor_tensor(to, x, taps[:, j, n:n + 1], to, ALU.mult, ALU.add)
                    step.done(last)
            on_vector(k, convolve)
        activate(k, [(x[:, :, :], x[:, :, :], ACT.Silu) for x in (qT, kT)])
        project(k, hT, k.given["w_in_2"][layer][:, 2 * D:4 * D], v, 2, bias=k.given["b_in_2"][layer][2 * D:4 * D])
        with buffers(k, li=[P, 2, H], b=[P, 2, H], c=[P, 2, H]) as (li, b, c):
            mlstm_gates(k, hT, layer, li, b, c)

            def scale(dve, step):
                step.done(V.tensor_scalar(qT[:, :, :], qT[:, :, :], DK ** -0.5, None, ALU.mult))
            on_vector(k, scale)
            for first in range(0, H, 2):
                mlstm_heads(k, first, qT, kT, v, b, c, y)
        with buffers(k, gain=[P, D]) as gain:
            head_norm(k, [y[:, t, a * M_DV:(a + 1) * M_DV] for t in range(2) for a in range(H)], RMS_EPS,
                      [(v[:, :, D:2 * D], ACT.Sigmoid)], gain[:, :], k.given["m_norm_g_2"][layer])
            gate_rows(k, y, v[:, :, D:2 * D], gain)


def gate_rows(k, y, gate, gain):
    def body(dve, step):
        for factor in (lambda t: gain[:, :], lambda t: gate[:, t, :]):
            for t in range(2):
                last = k.nc.vector.tensor_tensor(y[:, t, :], y[:, t, :], factor(t), ALU.mult)
            step.done(last)
    on_vector(k, body)


BLOCKS = ((0, 0), (1, 0), (1, 1))


def mlstm_heads(k, first, qT, kT, v, b, c, y):
    V = k.nc.vector
    pair = range(2)
    with buffers(k, diag=[P, 2, 2, P], logs=[P, 2, 3, P], probs=[P, 2, 3, P], weighed=[P, 2, 3, P], turned=[P, 2, 3, P],
                 top=[P, 2, 4], den=[P, 2, 2], least=[P, 2, 2], inverse=[P, 2, 2]) as \
            (diag, logs, probs, weighed, turned, top, den, least, inverse), stage(k) as block:
        span = (slice(0, 1), slice(1, 3))

        def bank(h, n):
            return k.psum[:, 4 * h + n, :]

        def flat(x, h, t):
            return x[:, h, span[t], :].rearrange("p n s -> p (n s)")

        @block.tensor
        def _(pe):
            for h in pair:
                for n, (t, s) in enumerate(BLOCKS):
                    for d in range(2):
                        mm = matmul(k, bank(h, 1)[:, n * P:(n + 1) * P], qT[:, 2 * (first + h) + d, t * P:(t + 1) * P],
                                    kT[:, 2 * (first + h) + d, s * P:(s + 1) * P], d == 0, d == 1)
                mm.then_inc(k.scores, 1)
                if h == 0:
                    pe.wait_ge(k.vector_step, 1)
                    for i in pair:
                        for s in range(2):
                            mm = matmul(k, bank(i, 0)[:, s * P:(s + 1) * P], k.ones[:, :], diag[:, i, s, :], True, True)
                        mm.then_inc(k.products, 1)
            for h in pair:
                pe.wait_ge(k.weighed, h + 1)
                for n in range(3):
                    last = k.nc.tensor.transpose(bank(h, 2)[:, n * P:(n + 1) * P], weighed[:, h, n, :], k.ident[:, :])
                last.then_inc(k.products, 1)
            for h in pair:
                pe.wait_ge(k.weighed, h + 3)
                for n, (t, s) in enumerate(BLOCKS):
                    mm = matmul(k, bank(h, 3)[:, t * M_DV:(t + 1) * M_DV], turned[:, h, n, :],
                                v[:, s, (first + h) * M_DV:(first + h + 1) * M_DV], s == 0, s == t)
                mm.then_inc(k.products, 1)

        @block.vector
        def _(dve):
            step = Chain(dve, k.vector_step)
            for h in pair:
                for s in range(2):
                    last = V.tensor_scalar(diag[:, h, s, :], k.ident[:, :], c[:, s, first + h:first + h + 1], None, ALU.mult)
            step.done(last)
            for h in pair:
                dve.wait_ge(k.products, h + 1)
                for n, (t, s) in enumerate(BLOCKS):
                    row = bank(h, 0)[:, s * P:(s + 1) * P]
                    mine = b[:, t, first + h:first + h + 1]
                    if s < t:
                        last = V.tensor_scalar(logs[:, h, n, :], row, mine, None, ALU.add)
                    else:
                        last = V.scalar_tensor_tensor(logs[:, h, n, :], row, mine, k.future[:, :], ALU.add, ALU.add)
            step.done(last)
            for h in pair:
                for t in range(2):
                    last = V.tensor_reduce(top[:, h, t:t + 1], flat(logs, h, t), AX_X, ALU.max)
            step.done(last)
            for h in pair:
                last = V.tensor_tensor(top[:, h, 0:2], top[:, h, 0:2], b[:, :, first + h], ALU.max)
            step.done(last)
            V.tensor_scalar(top[:, :, 2:4], top[:, :, 0:2], -1.0, None, ALU.mult).then_inc(k.ready, 1)
            for h in pair:
                dve.wait_ge(k.scalar_step, 2 * h + 2)
                dve.wait_ge(k.scores, h + 1)
                for t in range(2):
                    last = V.tensor_tensor_reduce(flat(weighed, h, t), flat(probs, h, t),
                                                  bank(h, 1)[:, span[t].start * P:span[t].stop * P], 1.0, 0.0,
                                                  ALU.mult, ALU.add, den[:, h, t:t + 1])
                last.then_inc(k.weighed, 1)
            for h in pair:
                dve.wait_ge(k.products, h + 3)
                V.tensor_copy(turned[:, h, :, :].rearrange("p n s -> p (n s)"), bank(h, 2)[:, 0:3 * P]).then_inc(k.weighed, 1)
            dve.wait_ge(k.weighed, 4)
            step.done(V.scalar_tensor_tensor(den[:, :, :], den[:, :, :], -1.0, den[:, :, :], ALU.mult, ALU.max))
            dve.wait_ge(k.scalar_step, 5)
            step.done(V.tensor_tensor(den[:, :, :], den[:, :, :], least[:, :, :], ALU.max))
            step.done(V.reciprocal(inverse[:, :, :], den[:, :, :]))
            for h in pair:
                dve.wait_ge(k.products, h + 5)
                for t in range(2):
                    last = V.tensor_scalar(y[:, t, (first + h) * M_DV:(first + h + 1) * M_DV],
                                           bank(h, 3)[:, t * M_DV:(t + 1) * M_DV], inverse[:, h, t:t + 1], None, ALU.mult)
            step.done(last)

        @block.scalar
        def _(act):
            act.wait_ge(k.ready, 1)
            for h in pair:
                for t in range(2):
                    k.nc.scalar.activation(flat(probs, h, t), flat(logs, h, t), ACT.Exp, bias=top[:, h, 2 + t:3 + t])\
                        .then_inc(k.scalar_step, 1)
            k.nc.scalar.activation(least[:, :, :], top[:, :, 2:4], ACT.Exp).then_inc(k.scalar_step, 1)


def rope(k, raw, cos, sin):
    V = k.nc.vector
    with buffers(k, a1=[P, 8, SEQ], a2=[P, 8, SEQ]) as (a1, a2):
        def body(dve, step):
            pairs = raw[:, :].rearrange("p (n h t) -> p n h t", n=8, h=2)
            x1, x2 = pairs[:, :, 0, :], pairs[:, :, 1, :]
            wide_cos = cos[:, :].unsqueeze(1).to_broadcast([P, 8, SEQ])
            wide_sin = sin[:, :].unsqueeze(1).to_broadcast([P, 8, SEQ])
            V.tensor_tensor(a1[:, :, :], x1, wide_sin, ALU.mult)
            step.done(V.tensor_tensor(a2[:, :, :], x2, wide_sin, ALU.mult))
            V.tensor_tensor(x1, x1, wide_cos, ALU.mult)
            step.done(V.tensor_tensor(x2, x2, wide_cos, ALU.mult))
            V.tensor_tensor(x1, x1, a2[:, :, :], ALU.subtract)
            step.done(V.tensor_tensor(x2, x2, a1[:, :, :], ALU.add))
        on_vector(k, body)


def retention(k, hT, layer, y):
    H = HEADS
    V = k.nc.vector
    at = 4 * D + 2 * H
    with buffers(k, v=[P, 2, 2 * D]) as v:
        with buffers(k, raw=[P, 16 * SEQ]) as raw:
            with buffers(k, bias=[P, 16], cos=[P, SEQ], sin=[P, SEQ]) as (bias, cos, sin):
                load(k, [(bias[:, :], k.given["b_r_cols"][layer]), (cos[:, :], k.given["rope_cos"]),
                         (sin[:, :], k.given["rope_sin"])])
                project_channels(k, hT, k.given["w_in_2"][layer][:, at:at + 2 * D], raw, SEQ, SEQ, 0, bias)
                prefetch(k, k.given["w_in_2"][layer][:, at + 2 * D:at + 4 * D])
                rope(k, raw, cos, sin)
            project(k, hT, k.given["w_in_2"][layer][:, at + 2 * D:at + 4 * D], v, 2, bias=k.given["b_in_2"][layer][at + 2 * D:at + 4 * D])
            with buffers(k, decay=[P, H, 2, SEQ], weighed=[P, H, 2, SEQ]) as (decay, weighed):
                load(k, [(decay[:, :, :, :], k.given["decay"])])
                prefetch(k, k.given["w_in_2"][layer][:, at + 4 * D:at + 6 * D])
                with stage(k) as block:
                    lo = (0, P)

                    def values(pe, a):
                        pe.wait_ge(k.weighed, a + 1)
                        for t in range(2):
                            for s in range(t + 1):
                                mm = matmul(k, k.psum[:, 4 + 2 * (a % 2) + t, :], weighed[:, a, s, t * P:(t + 1) * P],
                                            v[:, s, a * R_DV:(a + 1) * R_DV], s == 0, s == t)
                        mm.then_inc(k.products, 1)

                    @block.tensor
                    def _(pe):
                        for a in range(H):
                            for s in range(2):
                                for d in range(2):
                                    q = raw[:, (2 * a + d) * SEQ + lo[s]:(2 * a + d + 1) * SEQ]
                                    kk = raw[:, (8 + 2 * a + d) * SEQ + s * P:(8 + 2 * a + d) * SEQ + (s + 1) * P]
                                    mm = matmul(k, k.psum[:, 2 * (a % 2) + s, lo[s]:SEQ], kk, q, d == 0, d == 1)
                            mm.then_inc(k.scores, 1)
                            if a >= 1:
                                values(pe, a - 1)
                        values(pe, H - 1)

                    @block.vector
                    def _(dve):
                        for a in range(H + 1):
                            if a < H:
                                dve.wait_ge(k.scores, a + 1)
                                for s in range(2):
                                    last = V.tensor_tensor(weighed[:, a, s, lo[s]:], k.psum[:, 2 * (a % 2) + s, lo[s]:SEQ],
                                                           decay[:, a, s, lo[s]:], ALU.mult)
                                last.then_inc(k.weighed, 1)
                            if a >= 1:
                                dve.wait_ge(k.products, a)
                                for t in range(2):
                                    last = V.tensor_copy(y[:, t, (a - 1) * R_DV:a * R_DV], k.psum[:, 4 + 2 * ((a - 1) % 2) + t, :])
                                last.then_inc(k.vector_step, 1)
        project(k, hT, k.given["w_in_2"][layer][:, at + 4 * D:at + 6 * D], v, 2, bias=k.given["b_in_2"][layer][at + 4 * D:at + 6 * D])
        with buffers(k, gain=[P, 2 * D]) as gain:
            head_norm(k, [y[:, t, a * R_DV:(a + 1) * R_DV] for t in range(2) for a in range(H)], RMS_EPS,
                      [(v[:, :, :], ACT.Silu)], gain[:, :], k.given["r_norm_g_2"][layer], k.given["w_br_2"][layer])
            gate_rows(k, y, v, gain)


def add_to(k, x, y):
    def body(dve, step):
        step.done(k.nc.vector.tensor_tensor(x[:, 0:2, :], x[:, 0:2, :], y[:, :, :], ALU.add))
    on_vector(k, body)


def feed_forward_in(k, hT, layer, f):
    with buffers(k, raw=[P, D_FF // P * SEQ], bias=[P, D_FF // P]) as (raw, bias):
        load(k, [(bias[:, :], k.given["b_ff1_cols"][layer])])
        project_channels(k, hT, k.given["w_ff1_2"][layer], raw, SEQ, SEQ, 0, bias, relu=True)
        parts = 8
        wide = raw[:, :].rearrange("p (n b t) -> p n b t", n=parts, t=SEQ)
        high = f.high[:, :, :].rearrange("p (n b) t -> p n b t", n=parts)
        low = f.low[:, :, :].rearrange("p (n b) t -> p n b t", n=parts)
        with stage(k) as block:
            @block.vector
            def _(dve):
                def take_low(dve, n):
                    dve.wait_ge(k.high_set, n + 1)
                    k.nc.vector.tensor_tensor(low[:, n], wide[:, n], high[:, n].bitcast(F32), ALU.subtract).then_inc(k.low_set, 1)

                for n in range(parts):
                    k.nc.vector.tensor_tensor(wide[:, n], wide[:, n], wide[:, n], ALU.mult).then_inc(k.ready, 1)
                    if n >= 1:
                        take_low(dve, n - 1)
                take_low(dve, parts - 1)

            @block.scalar
            def _(act):
                for n in range(parts):
                    act.wait_ge(k.ready, n + 1)
                    k.nc.scalar.copy(high[:, n], wide[:, n]).then_inc(k.high_set, 1)


def second_layer(k, x, layer):
    at = 4 * D + 2 * HEADS
    w_in, b_in = k.given["w_in_2"][layer], k.given["b_in_2"][layer]
    with buffers(k, h=[P, 2, D]) as h, split_buffers(k, "hT", [P, DB, SEQ]) as hT:
        rms_rows(k, x, h, k.given["norm1_g_2"][layer], w_in[:, 0:2 * D])
        turn(k, h, hT, 2)
        with buffers(k, merged=[P, 2, D]) as merged:
            mlstm(k, hT, layer, h)
            with split_buffers(k, "yT", [P, DB, SEQ]) as yT:
                turn(k, h, yT, 2)
                project(k, yT, k.given["w_bm_2"][layer], merged, 2)
            with buffers(k, wide=[P, 2, 2 * D]) as wide:
                retention(k, hT, layer, wide)
                with split_buffers(k, "yT", [P, 2 * DB, SEQ]) as yT, buffers(k, part=[P, 2, D]) as part:
                    turn(k, wide, yT, 2)
                    project(k, yT, k.given["w_br_2"][layer], part, 2)
                    prefetch(k, w_in[:, at + 6 * D:at + 8 * D])
                    project(k, hT, w_in[:, at + 6 * D:at + 8 * D], wide, 2, bias=b_in[at + 6 * D:at + 8 * D])
                    prefetch(k, k.given["w_out_2"][layer])
                    activate(k, [(wide[:, :, :], wide[:, :, :], ACT.Sigmoid)])

                    def gated(dve, step):
                        k.nc.vector.tensor_tensor(merged[:, :, :], merged[:, :, :], wide[:, :, 0:D], ALU.mult)
                        step.done(k.nc.vector.tensor_tensor(part[:, :, :], part[:, :, :], wide[:, :, D:2 * D], ALU.mult))
                        step.done(k.nc.vector.tensor_tensor(merged[:, :, :], merged[:, :, :], part[:, :, :], ALU.add))
                    on_vector(k, gated)
                    turn(k, merged, yT.part(slice(None), slice(0, DB)), 2)
                    project(k, yT, k.given["w_out_2"][layer], part, 2)
                    add_to(k, x, part)
        rms_rows(k, x, h, k.given["norm2_g_2"][layer], k.given["w_ff1_2"][layer])
        turn(k, h, hT, 2)
        with split_buffers(k, "f", [P, D_FF // P, SEQ]) as f:
            feed_forward_in(k, hT, layer, f)
            prefetch(k, k.given["w_ff2_2"][layer])
            project(k, f, k.given["w_ff2_2"][layer], h, 2, bias=k.given["b_ff2_2"][layer])
        add_to(k, x, h)
        rms_rows(k, x, h, k.given["norm3_g_2"][layer], k.given["w_pe_gate_2"][layer])
        turn(k, h, hT, 2)
        with buffers(k, gate=[P, 2, D], pT=[P, 2, SEQ], w=[P, 2, D]) as (gate, pT, w):
            project(k, hT, k.given["w_pe_gate_2"][layer], gate, 2)
            with stage(k) as block:
                @block.sync
                def _(sp):
                    sp.dma_start(pT[:, :, :], k.given["p_t"][layer].rearrange("(b p) t -> p b t", p=P)).then_inc(k.loaded[0], 16)
                    sp.dma_start(w[:, :, :], k.given["w_pe_2"][layer].rearrange("(b p) n -> p b n", p=P)).then_inc(k.loaded[0], 16)

                @block.scalar
                def _(act):
                    k.nc.scalar.activation(gate[:, :, :], gate[:, :, :], ACT.Sigmoid).then_inc(k.scalar_step, 1)

                @block.tensor
                def _(pe):
                    pe.wait_ge(k.loaded[0], 32)
                    for t in range(2):
                        for n in range(2):
                            for b in range(2):
                                mm = matmul(k, k.psum[:, 2 * t + n, :], pT[:, b, t * P:(t + 1) * P],
                                            w[:, b, n * NC:(n + 1) * NC], b == 0, b == 1)
                    mm.then_inc(k.products, 1)

                @block.vector
                def _(dve):
                    dve.wait_ge(k.products, 1)
                    dve.wait_ge(k.scalar_step, 1)
                    for t in range(2):
                        for n in range(2):
                            to = gate[:, t, n * NC:(n + 1) * NC]
                            last = k.nc.vector.tensor_tensor(to, to, k.psum[:, 2 * t + n, :], ALU.mult)
                    last.then_inc(k.vector_step, 1)
            add_to(k, x, gate)


def first_layer(k, x, layer, h):
    streams = 1 if layer == DEPTH - 1 else 2
    modulated(k, x, h, 2, layer, 1, 0)
    if layer == 0:
        chunk_mlp(k, h)
    else:
        gla_mixer(k, h)
    residual_norm(k, x, h, streams, layer, 2, 0)
    modulated(k, x, h, streams, layer, 4, 3)
    with buffers(k, mix=[P, 2 * streams, D]) as mix:
        peer(k, h, mix, 2 * streams, layer)
        residual_norm(k, x, mix, streams, layer, 5, 1)


def program(nc, given, out):
    with ExitStack() as ctx:
        k = Kit()
        k.nc, k.given, k.made = nc, given, 0

        def sem(name):
            return ctx.enter_context(nc.semaphore(name))

        k.u_loaded = [sem(f"u_loaded{n}") for n in range(U_RING)]
        k.v_loaded = [sem(f"v_loaded{n}") for n in range(V_RING)]
        k.groups_gathered = 0
        k.weights_landed = [sem(f"weights_landed{n}") for n in range(WEIGHT_SLOTS)]
        k.landed_sems = range(k.weights_landed[0].num, k.weights_landed[-1].num + 1)
        k.loaded = [sem("loaded0"), sem("loaded1")]
        k.bias_loaded = [sem("bias_loaded0"), sem("bias_loaded1")]
        k.copied = [sem("copied0"), sem("copied1")]
        k.chunks_used = sem("chunks_used")
        k.high_set = sem("high_set")
        k.low_set = sem("low_set")
        k.psum_free = sem("psum_free")
        k.products = sem("products")
        k.vector_step = sem("vector_step")
        k.scalar_step = sem("scalar_step")
        k.ready = sem("ready")
        k.stored = sem("stored")
        k.started = sem("started")
        k.places_set = sem("places_set")
        k.u_used = sem("u_used")
        k.v_used = sem("v_used")
        k.exp_asked = sem("exp_asked")
        k.updates = sem("updates")
        k.outputs = sem("outputs")
        k.states = sem("states")
        k.scores = sem("scores")
        k.granted = sem("granted")
        k.exp_done = sem("exp_done")
        k.gelu_done = sem("gelu_done")
        k.diag_set = sem("diag_set")
        k.summed = sem("summed")
        k.weighed = sem("weighed")
        first = k.loaded[0].num
        k.stage_sems = range(first, k.weighed.num + 1)
        k.psum = ctx.enter_context(nc.psum_tensor("psum", [P, 8, NC], F32))
        k.modulation = nc.dram_tensor("modulation", (2, DEPTH * 6 * D), F32).ap()
        with buffers(k, ident=[P, P], ones=[P, P], causal=[P, P], future=[P, P], x=[P, 4, D]) as \
                (k.ident, k.ones, k.causal, k.future, x):
            load(k, [(k.ident[:, :], given["ident"]), (k.ones[:, :], given["ones"]), (k.causal[:, :], given["causal"]), (k.future[:, :], given["future"]),
                     (x[:, 0:2, :], given["x"].rearrange("o (t p) d -> p (o t) d", p=P)),
                     (x[:, 2:4, :], given["ctx"].rearrange("o (t p) d -> p (o t) d", p=P))])
            modulation_rows(k)
            for layer in range(DEPTH):
                with buffers(k, h=[P, 4, D]) as h:
                    first_layer(k, x, layer, h)
            with weight_rings(k), nc.Fori(0, DEPTH) as layer:
                second_layer(k, x, layer)
            with buffers(k, h=[P, 2, D]) as h:
                rms_rows(k, x, h, given["final_g_2"])
                store(k, out, h)


def store(k, out, y):
    with stage(k) as block:
        @block.sync
        def _(sp):
            sp.dma_start(out.rearrange("o (t p) d -> p (o t) d", p=P), y[:, 0:2, :]).then_inc(k.stored, 16)
            sp.wait_ge(k.stored, 16)


def constants():
    f = np.float32
    r = np.arange(P)
    chunk = r // GLA_CHUNK
    same = chunk[:, None] == chunk[None, :]
    pos = np.arange(SEQ, dtype=f)
    inv_freq = (f(10000.0) ** (-np.arange(0, DK, 2, dtype=f) / f(DK))).astype(f)
    ang = (pos[:, None] * inv_freq[None, :]).astype(f)
    log_gamma = np.log(f(1.0) - np.exp2(-f(5.0) - np.arange(HEADS, dtype=f))).astype(f)
    diff = pos[None, :] - pos[:, None]
    decay = np.where(diff >= 0, np.exp(np.maximum(diff, 0)[None] * log_gamma[:, None, None]) * f(DK ** -0.5), 0.0)
    return {
        "ident": np.eye(P, dtype=f),
        "ones": np.ones((P, P), f),
        "causal": (r[:, None] <= r[None, :]).astype(f),
        "future": np.where(r[None, :] <= r[:, None], 0.0, MASKED).astype(f),
        "chunk_prefix": (same & (r[:, None] <= r[None, :])).astype(f),
        "chunk_suffix": (same & (r[:, None] >= r[None, :])).astype(f),
        "chunk_same": same.astype(f),
        "chunk_member": (chunk[:, None] == np.arange(2)[None, :]).astype(f),
        "rope_cos": np.ascontiguousarray(np.cos(ang).T.astype(f)),
        "rope_sin": np.ascontiguousarray(np.sin(ang).T.astype(f)),
        "decay": np.ascontiguousarray(decay.astype(f).reshape(HEADS, 2, P, SEQ).transpose(2, 0, 1, 3)),
    }


_AS_THEY_ARE = ("x ctx w_mod b_mod ln_g ln_b a_w_in a_norm_g a_norm_b a_w_out b_w_in b_w_gate b_gate_bias b_gn_g b_w_out "
                "p_w_q norm1_g_2 w_in_2 b_in_2 m_norm_g_2 r_norm_g_2 w_bm_2 w_br_2 w_out_2 norm2_g_2 w_ff1_2 "
                "w_ff2_2 b_ff2_2 norm3_g_2 w_pe_gate_2 w_pe_2 final_g_2").split()


def kernel(**inputs):
    import concourse.bacc as bacc
    from concourse.bass_utils import run_bass_kernel_spmd

    a = {n: np.asarray(v) for n, v in inputs.items()}
    at = 4 * D + 2 * HEADS
    given = {n: a[n] for n in _AS_THEY_ARE}
    given["cond_cols"] = np.stack([a["c"].reshape(DB, P).T, a["c_ctx"].reshape(DB, P).T], axis=2)
    given["b_qk_cols"] = a["b_in_2"][:, 0:2 * D].reshape(DEPTH, 16, P).transpose(0, 2, 1)
    given["b_r_cols"] = a["b_in_2"][:, at:at + 2 * D].reshape(DEPTH, 16, P).transpose(0, 2, 1)
    given["b_ff1_cols"] = a["b_ff1_2"].reshape(DEPTH, D_FF // P, P).transpose(0, 2, 1)
    given["conv_w_cols"] = a["conv_w_2"].reshape(DEPTH, CONV_K, 16, P).transpose(0, 3, 1, 2)
    given["conv_b_cols"] = a["conv_b_2"].reshape(DEPTH, 16, P).transpose(0, 2, 1)
    given["a_w_s_t"] = a["a_w_s"][0].transpose(2, 0, 1)
    given["a_b_s_t"] = a["a_b_s"][0].T
    given["p_keys_t"] = a["p_keys"].transpose(0, 1, 3, 2)
    given["p_t"] = a["p_2"][:, 0].transpose(0, 2, 1)
    given["p_u"] = a["p_u"].reshape(DEPTH * PEER_EXPERTS, D)
    given["p_v"] = a["p_v"].reshape(DEPTH * PEER_EXPERTS, D)
    given.update(constants())
    given = {n: np.ascontiguousarray(v) for n, v in given.items()}

    nc = bacc.Bacc("TRN2", target_bir_lowering=False, num_devices=1)
    there = {n: nc.dram_tensor(f"in_{n}", v.shape, F32, kind="ExternalInput").ap() for n, v in given.items()}
    out = nc.dram_tensor("out_x", (1, SEQ, D), F32, kind="ExternalOutput").ap()
    program(nc, there, out)
    r = run_bass_kernel_spmd(nc, [{f"in_{n}": v for n, v in given.items()}], core_ids=[0])
    return r.results[0]["out_x"]
```
